# Optimizing a Trainium2 kernel written in Bass

```python
import math
import jax, jax.numpy as jnp
from jax import lax
import numpy as np

D_MODEL = 1024
BATCH = 1
SEQ = 256
DEPTH = 2

N_A_LAYERS = DEPTH // 2
N_B_LAYERS = DEPTH - N_A_LAYERS
D_FF = ((8 * D_MODEL // 3) + 127) // 128 * 128
CONV_WIDTH = 31
HEAD_DIM = 128
N_HEADS = D_MODEL // HEAD_DIM
MOBA_BLOCK = 256
MOBA_TOPK = 3
Q_CHUNK = 32
RMS_EPS = 1e-6
LN_EPS = 1e-5
MACARON_WEIGHT = 0.5
NEG_INF = -1e30


def rms_norm(x, g):
    x32 = x.astype(jnp.float32)
    y = x32 * lax.rsqrt(jnp.mean(x32 * x32, axis=-1, keepdims=True) + RMS_EPS)
    return (y * g.astype(jnp.float32)).astype(x.dtype)

def swiglu_ffn(h, w_gate_up, w_down):
    gate, up = jnp.split(h @ w_gate_up, 2, axis=-1)
    return (jax.nn.silu(gate) * up) @ w_down

def conformer_conv(h, w_in, b_in, w_dw, b_dw, ln_g, ln_b, w_out, b_out):
    a, g = jnp.split(h @ w_in + b_in, 2, axis=-1)
    u = a * jax.nn.sigmoid(g)
    u = lax.conv_general_dilated(
        u, w_dw[:, None, :].astype(u.dtype), window_strides=(1,),
        padding=[(CONV_WIDTH - 1, 0)],
        dimension_numbers=('NWC', 'WIO', 'NWC'),
        feature_group_count=D_MODEL) + b_dw
    u32 = u.astype(jnp.float32)
    mu = jnp.mean(u32, axis=-1, keepdims=True)
    var = jnp.mean(jnp.square(u32 - mu), axis=-1, keepdims=True)
    u = ((u32 - mu) * lax.rsqrt(var + LN_EPS) * ln_g.astype(jnp.float32)
         + ln_b.astype(jnp.float32)).astype(h.dtype)
    return jax.nn.silu(u) @ w_out + b_out

def alibi_slopes():
    return jnp.asarray(2.0 ** (-8.0 * (np.arange(N_HEADS) + 1) / N_HEADS), dtype=jnp.float32)

def shared_kv(x, g_kv, w_kv):
    B, T, _ = x.shape
    k, v = jnp.split(rms_norm(x, g_kv) @ w_kv, 2, axis=-1)
    nb = -(-T // MOBA_BLOCK)
    pad = nb * MOBA_BLOCK - T

    def to_blocks(z):
        z = jnp.pad(z, ((0, 0), (0, pad), (0, 0)))
        return z.reshape(B, nb, MOBA_BLOCK, N_HEADS, HEAD_DIM).transpose(0, 3, 1, 2, 4)

    kb = to_blocks(k)
    vb = to_blocks(v)
    k_means = jnp.mean(kb.astype(jnp.float32), axis=3).astype(kb.dtype)
    return kb, vb, k_means

def moba_attention(q, kb, vb, k_means, slopes):
    B, T = q.shape[0], q.shape[1]
    nb = kb.shape[2]
    ksel = min(MOBA_TOPK, nb)
    q = (q * (HEAD_DIM ** -0.5)).transpose(0, 2, 1, 3)
    qblk = jnp.arange(T) // MOBA_BLOCK
    gate = jnp.einsum('bhtd,bhnd->bhtn', q, k_means, preferred_element_type=jnp.float32)
    past = jnp.arange(nb)[None, :] < qblk[:, None]
    gate = jnp.where(past, gate, NEG_INF)
    _, sel = lax.top_k(gate, ksel)

    nc = T // Q_CHUNK
    q_c = q.reshape(B, N_HEADS, nc, Q_CHUNK, HEAD_DIM).transpose(2, 0, 1, 3, 4)
    sel_c = sel.reshape(B, N_HEADS, nc, Q_CHUNK, ksel).transpose(2, 0, 1, 3, 4)
    b_ix = jnp.arange(B)[:, None, None, None]
    h_ix = jnp.arange(N_HEADS)[None, :, None, None]
    slopes5 = slopes[:, None, None, None]
    slopes4 = slopes[:, None, None]

    def chunk(args):
        c, qq, ss = args
        t = c * Q_CHUNK + jnp.arange(Q_CHUNK)
        own = (c * Q_CHUNK) // MOBA_BLOCK
        valid = jnp.arange(ksel)[None, :] < (t // MOBA_BLOCK)[:, None]
        kg = kb[b_ix, h_ix, ss]
        vg = vb[b_ix, h_ix, ss]
        s_sel = jnp.einsum('bhqd,bhqkpd->bhqkp', qq, kg, preferred_element_type=jnp.float32)
        key_pos = ss[..., None] * MOBA_BLOCK + jnp.arange(MOBA_BLOCK)
        dist = (t[:, None, None] - key_pos).astype(jnp.float32)
        s_sel = jnp.where(valid[:, :, None], s_sel - slopes5 * dist, NEG_INF)
        s_sel = s_sel.reshape(B, N_HEADS, Q_CHUNK, ksel * MOBA_BLOCK)
        k_own = lax.dynamic_index_in_dim(kb, own, axis=2, keepdims=False)
        v_own = lax.dynamic_index_in_dim(vb, own, axis=2, keepdims=False)
        s_own = jnp.einsum('bhqd,bhpd->bhqp', qq, k_own, preferred_element_type=jnp.float32)
        d_own = t[:, None] - (own * MOBA_BLOCK + jnp.arange(MOBA_BLOCK))[None, :]
        s_own = jnp.where(d_own >= 0, s_own - slopes4 * d_own.astype(jnp.float32), NEG_INF)
        p = jax.nn.softmax(jnp.concatenate([s_sel, s_own], axis=-1), axis=-1)
        p_sel = p[..., :ksel * MOBA_BLOCK].reshape(B, N_HEADS, Q_CHUNK, ksel, MOBA_BLOCK).astype(vb.dtype)
        p_own = p[..., ksel * MOBA_BLOCK:].astype(vb.dtype)
        return (jnp.einsum('bhqkp,bhqkpd->bhqd', p_sel, vg)
                + jnp.einsum('bhqp,bhpd->bhqd', p_own, v_own))

    out = lax.map(chunk, (jnp.arange(nc), q_c, sel_c))
    return out.transpose(1, 0, 3, 2, 4).reshape(B, T, N_HEADS * HEAD_DIM)

def first_inputs(seed: int = 0) -> dict:
    key = jax.random.key(seed)
    ks = jax.random.split(key, 20)
    f32 = jnp.float32

    def nrm(k, shape, scale):
        return jax.random.normal(k, shape, f32) * scale

    def gain(k, shape):
        return 1.0 + 0.02 * jax.random.normal(k, shape, f32)

    D = D_MODEL
    return {
        "x": jax.random.normal(ks[0], (BATCH, SEQ, D), f32),
        "ffn_norm_pre": gain(ks[1], (DEPTH, 2, D)),
        "ffn_norm_post": gain(ks[2], (DEPTH, 2, D)),
        "ffn_w_gate_up": nrm(ks[3], (DEPTH, 2, D, 2 * D_FF), D ** -0.5),
        "ffn_w_down": nrm(ks[4], (DEPTH, 2, D_FF, D), D_FF ** -0.5),
        "mix_norm_pre": gain(ks[5], (DEPTH, D)),
        "mix_norm_post": gain(ks[6], (DEPTH, D)),
        "conv_w_in": nrm(ks[7], (N_A_LAYERS, D, 2 * D), D ** -0.5),
        "conv_b_in": nrm(ks[8], (N_A_LAYERS, 2 * D), 0.02),
        "conv_w_dw": nrm(ks[9], (N_A_LAYERS, CONV_WIDTH, D), CONV_WIDTH ** -0.5),
        "conv_b_dw": nrm(ks[10], (N_A_LAYERS, D), 0.02),
        "conv_ln_g": gain(ks[11], (N_A_LAYERS, D)),
        "conv_ln_b": nrm(ks[12], (N_A_LAYERS, D), 0.02),
        "conv_w_out": nrm(ks[13], (N_A_LAYERS, D, D), D ** -0.5),
        "conv_b_out": nrm(ks[14], (N_A_LAYERS, D), 0.02),
        "kv_norm": gain(ks[15], (D,)),
        "w_kv": nrm(ks[16], (D, 2 * D), D ** -0.5),
        "attn_w_q": nrm(ks[17], (N_B_LAYERS, D, D), D ** -0.5),
        "attn_w_o": nrm(ks[18], (N_B_LAYERS, D, D), D ** -0.5),
    }

def first_block(x, ffn_norm_pre, ffn_norm_post, ffn_w_gate_up, ffn_w_down, mix_norm_pre,
              mix_norm_post, conv_w_in, conv_b_in, conv_w_dw, conv_b_dw, conv_ln_g, conv_ln_b,
              conv_w_out, conv_b_out, kv_norm, w_kv, attn_w_q, attn_w_o):
    B, T, _ = x.shape
    slopes = alibi_slopes()
    kv = None
    for layer in range(DEPTH):
        f = swiglu_ffn(rms_norm(x, ffn_norm_pre[layer, 0]), ffn_w_gate_up[layer, 0], ffn_w_down[layer, 0])
        x = x + MACARON_WEIGHT * rms_norm(f, ffn_norm_post[layer, 0])
        h = rms_norm(x, mix_norm_pre[layer])
        if layer < N_A_LAYERS:
            a = layer
            y = conformer_conv(h, conv_w_in[a], conv_b_in[a], conv_w_dw[a], conv_b_dw[a],
                               conv_ln_g[a], conv_ln_b[a], conv_w_out[a], conv_b_out[a])
        else:
            if kv is None:
                kv = shared_kv(x, kv_norm, w_kv)
            j = layer - N_A_LAYERS
            q = (h @ attn_w_q[j]).reshape(B, T, N_HEADS, HEAD_DIM)
            y = moba_attention(q, kv[0], kv[1], kv[2], slopes) @ attn_w_o[j]
        x = x + rms_norm(y, mix_norm_post[layer])
        f = swiglu_ffn(rms_norm(x, ffn_norm_pre[layer, 1]), ffn_w_gate_up[layer, 1], ffn_w_down[layer, 1])
        x = x + MACARON_WEIGHT * rms_norm(f, ffn_norm_post[layer, 1])
    return x


GRID_W = 64
NORM_EPS = 1e-6

NA_HEADS = 8
NA_HEAD_DIM = 64
NA_WIDTH = NA_HEADS * NA_HEAD_DIM
NA_KH_MAX = 8
NA_KW = 16

SSD_D_INNER = D_MODEL
SSD_HEAD_DIM = 64
SSD_HEADS = SSD_D_INNER // SSD_HEAD_DIM
SSD_GROUPS = 4
SSD_STATE = 128
SSD_CONV = 4
SSD_CHUNK = 128
SSD_CONV_DIM = SSD_D_INNER + 2 * SSD_GROUPS * SSD_STATE
DT_MIN = 0.001
DT_MAX = 0.1

EVEN_SPLITS = [NA_WIDTH, 2 * NA_WIDTH, 3 * NA_WIDTH,
               3 * NA_WIDTH + SSD_D_INNER,
               3 * NA_WIDTH + SSD_D_INNER + SSD_CONV_DIM]
EVEN_IN_WIDTH = 3 * NA_WIDTH + SSD_D_INNER + SSD_CONV_DIM + 2 * SSD_HEADS
EVEN_MIX_WIDTH = NA_WIDTH + SSD_D_INNER

GQA_HEADS = 16
GQA_KV_HEADS = 4
GQA_HEAD_DIM = 64
GQA_Q_WIDTH = GQA_HEADS * GQA_HEAD_DIM
GQA_KV_WIDTH = GQA_KV_HEADS * GQA_HEAD_DIM
ODD_IN_WIDTH = GQA_Q_WIDTH + 2 * GQA_KV_WIDTH
ROPE_THETA = 10000.0
Q_BLOCK = 128

FFN_HIDDEN = -(-8 * D_MODEL // (3 * 256)) * 256

N_EVEN = (DEPTH + 1) // 2
N_ODD = DEPTH // 2


def rms_norm_2(x, g):
    xf = x.astype(jnp.float32)
    y = xf * lax.rsqrt(jnp.mean(xf * xf, axis=-1, keepdims=True) + NORM_EPS)
    return (y * g.astype(jnp.float32)).astype(x.dtype)

def neighbourhood_attention(q, k, v, rpb):
    B, S, H, Dh = q.shape
    rows = S // GRID_W
    kh = min(NA_KH_MAX, rows)
    qg = q.reshape(B, rows, GRID_W, H, Dh)
    kg = k.reshape(B, rows, GRID_W, H, Dh)
    vg = v.reshape(B, rows, GRID_W, H, Dh)
    r = jnp.arange(rows)
    row_start = jnp.clip(r - kh // 2, 0, rows - kh)
    key_rows = row_start[:, None] + jnp.arange(kh)[None, :]
    k_blk = kg[:, key_rows]
    v_blk = vg[:, key_rows]
    c = jnp.arange(GRID_W)
    col_start = jnp.clip(c - NA_KW // 2, 0, GRID_W - NA_KW)
    in_win = (c[None, :] >= col_start[:, None]) & (c[None, :] < col_start[:, None] + NA_KW)
    dy = key_rows - r[:, None] + (NA_KH_MAX - 1)
    dx = jnp.clip(c[None, :] - c[:, None], -(NA_KW - 1), NA_KW - 1) + (NA_KW - 1)
    bias = rpb.astype(jnp.float32)[:, dy[:, None, :, None], dx[None, :, None, :]]
    scale = Dh ** -0.5
    s = jnp.einsum('brchd,brjkhd->bhrcjk', qg, k_blk).astype(jnp.float32) * scale + bias[None]
    s = jnp.where(in_win[:, None, :], s, -jnp.inf)
    p = jax.nn.softmax(s.reshape(B, H, rows, GRID_W, kh * GRID_W), axis=-1)
    p = p.reshape(B, H, rows, GRID_W, kh, GRID_W).astype(v.dtype)
    o = jnp.einsum('bhrcjk,brjkhd->brchd', p, v_blk)
    return o.reshape(B, S, H * Dh)

def centred_depthwise_conv(x, w, b):
    K, C = w.shape
    left = K // 2
    xp = jnp.pad(x, ((0, 0), (left, K - 1 - left), (0, 0)))
    y = lax.conv_general_dilated(xp, w[:, None, :].astype(x.dtype), window_strides=(1,), padding='VALID',
                                 dimension_numbers=('NWC', 'WIO', 'NWC'), feature_group_count=C)
    return y + b.astype(x.dtype)

def ssd_scan(x, dt, A, Bm, Cm):
    out_dtype = x.dtype
    Bsz, S, H, P = x.shape
    G, N = Bm.shape[2], Bm.shape[3]
    R = H // G
    L = SSD_CHUNK
    nc = S // L
    f32 = jnp.float32
    x = x.astype(f32); dt = dt.astype(f32)
    xc = (x * dt[..., None]).reshape(Bsz, nc, L, G, R, P)
    Bc = Bm.astype(f32).reshape(Bsz, nc, L, G, N)
    Cc = Cm.astype(f32).reshape(Bsz, nc, L, G, N)
    a = (dt * A.astype(f32)).reshape(Bsz, nc, L, G, R)
    a_cum = jnp.moveaxis(jnp.cumsum(a, axis=2), 2, -1)
    seg = a_cum[..., :, None] - a_cum[..., None, :]
    lower = jnp.tril(jnp.ones((L, L), dtype=bool))
    decay = jnp.exp(jnp.where(lower, seg, -jnp.inf))
    cb = jnp.einsum('bclgn,bcsgn->bcgls', Cc, Bc)
    y_diag = jnp.einsum('bcgls,bcgrls,bcsgrp->bclgrp', cb, decay, xc)
    decay_to_end = jnp.exp(a_cum[..., -1:] - a_cum)
    states = jnp.einsum('bcsgn,bcgrs,bcsgrp->bcgrpn', Bc, decay_to_end, xc)
    chunk_decay = jnp.exp(a_cum[..., -1])

    def step(h, inp):
        s_c, d_c = inp
        return h * d_c[..., None, None] + s_c, h

    h0 = jnp.zeros((Bsz, G, R, P, N), f32)
    _, h_prev = lax.scan(step, h0, (jnp.moveaxis(states, 1, 0), jnp.moveaxis(chunk_decay, 1, 0)))
    h_prev = jnp.moveaxis(h_prev, 0, 1)
    y_off = jnp.einsum('bclgn,bcgrpn,bcgrl->bclgrp', Cc, h_prev, jnp.exp(a_cum))
    return (y_diag + y_off).reshape(Bsz, S, H, P).astype(out_dtype)

def gated_group_rms_norm(y, z, g):
    Bsz, S, Dn = y.shape
    h = (y * jax.nn.silu(z)).astype(jnp.float32).reshape(Bsz, S, SSD_GROUPS, Dn // SSD_GROUPS)
    h = h * lax.rsqrt(jnp.mean(h * h, axis=-1, keepdims=True) + NORM_EPS)
    return (h.reshape(Bsz, S, Dn) * g.astype(jnp.float32)).astype(y.dtype)

def even_mixer(x, mix_norm, w_in, na_q_norm, na_k_norm, na_rel_bias, conv_w, conv_b,
               dt_bias, A_log, D_skip, out_norm, w_out):
    Bsz, S, _ = x.shape
    proj = rms_norm_2(x, mix_norm) @ w_in
    q, k, v, z, xbc, dt_raw = jnp.split(proj, EVEN_SPLITS, axis=-1)
    q = rms_norm_2(q.reshape(Bsz, S, NA_HEADS, NA_HEAD_DIM), na_q_norm)
    k = rms_norm_2(k.reshape(Bsz, S, NA_HEADS, NA_HEAD_DIM), na_k_norm)
    v = v.reshape(Bsz, S, NA_HEADS, NA_HEAD_DIM)
    na_out = neighbourhood_attention(q, k, v, na_rel_bias)
    xbc = jax.nn.silu(centred_depthwise_conv(xbc, conv_w, conv_b))
    xs, bm, cm = jnp.split(xbc, [SSD_D_INNER, SSD_D_INNER + SSD_GROUPS * SSD_STATE], axis=-1)
    xs = xs.reshape(Bsz, S, SSD_HEADS, SSD_HEAD_DIM)
    bm = bm.reshape(Bsz, S, SSD_GROUPS, SSD_STATE)
    cm = cm.reshape(Bsz, S, SSD_GROUPS, SSD_STATE)
    dt = jax.nn.softplus(dt_raw.astype(jnp.float32).reshape(Bsz, S, 2, SSD_HEADS)
                         + dt_bias.astype(jnp.float32))
    A = -jnp.exp(A_log.astype(jnp.float32))
    y_fwd = ssd_scan(xs, dt[:, :, 0], A[0], bm, cm)
    y_bwd = jnp.flip(ssd_scan(jnp.flip(xs, 1), jnp.flip(dt[:, :, 1], 1), A[1],
                              jnp.flip(bm, 1), jnp.flip(cm, 1)), 1)
    y = y_fwd + y_bwd + D_skip.astype(xs.dtype)[:, None] * xs
    ssd_out = gated_group_rms_norm(y.reshape(Bsz, S, SSD_D_INNER), z, out_norm)
    return jnp.concatenate([na_out, ssd_out], axis=-1) @ w_out

def axial_rope_tables(S):
    t = jnp.arange(S)
    row = (t // GRID_W).astype(jnp.float32)
    col = (t % GRID_W).astype(jnp.float32)
    axis_dims = GQA_HEAD_DIM // 2
    freqs = ROPE_THETA ** (-jnp.arange(0, axis_dims, 2, dtype=jnp.float32) / axis_dims)
    ang = jnp.concatenate([row[:, None] * freqs, col[:, None] * freqs], axis=-1)
    return jnp.cos(ang), jnp.sin(ang)

def apply_rope(x, cos, sin):
    xf = x.astype(jnp.float32).reshape(*x.shape[:-1], x.shape[-1] // 2, 2)
    x0, x1 = xf[..., 0], xf[..., 1]
    c = cos[None, :, None, :]
    s = sin[None, :, None, :]
    out = jnp.stack([x0 * c - x1 * s, x0 * s + x1 * c], axis=-1)
    return out.reshape(x.shape).astype(x.dtype)

def gqa_block_attention(q, k, v):
    Bsz, S, H, Dh = q.shape
    KV = k.shape[2]
    rep = H // KV
    nb = S // Q_BLOCK
    qb = jnp.moveaxis(q.reshape(Bsz, nb, Q_BLOCK, KV, rep, Dh), 1, 0)
    scale = Dh ** -0.5

    def one_block(q_blk):
        s = jnp.einsum('bqgrd,bkgd->bgrqk', q_blk, k).astype(jnp.float32) * scale
        p = jax.nn.softmax(s, axis=-1).astype(v.dtype)
        return jnp.einsum('bgrqk,bkgd->bqgrd', p, v)

    o = lax.map(one_block, qb)
    return jnp.moveaxis(o, 0, 1).reshape(Bsz, S, H * Dh)

def odd_mixer(x, mix_norm, w_qkv, q_norm, k_norm, w_out):
    Bsz, S, _ = x.shape
    proj = rms_norm_2(x, mix_norm) @ w_qkv
    q, k, v = jnp.split(proj, [GQA_Q_WIDTH, GQA_Q_WIDTH + GQA_KV_WIDTH], axis=-1)
    q = rms_norm_2(q.reshape(Bsz, S, GQA_HEADS, GQA_HEAD_DIM), q_norm)
    k = rms_norm_2(k.reshape(Bsz, S, GQA_KV_HEADS, GQA_HEAD_DIM), k_norm)
    v = v.reshape(Bsz, S, GQA_KV_HEADS, GQA_HEAD_DIM)
    cos, sin = axial_rope_tables(S)
    q = apply_rope(q, cos, sin)
    k = apply_rope(k, cos, sin)
    return gqa_block_attention(q, k, v) @ w_out

def swiglu_ffn_2(x, norm_g, w13, w2):
    g, u = jnp.split(rms_norm_2(x, norm_g) @ w13, 2, axis=-1)
    return (jax.nn.silu(g) * u) @ w2

def second_inputs(seed: int = 0) -> dict:
    key = jax.random.key(seed)
    ks = jax.random.split(key, 24)
    f32 = jnp.float32

    def normal(k, shape, scale):
        return jax.random.normal(k, shape, f32) * scale

    def gain(k, shape):
        return 1.0 + 0.02 * jax.random.normal(k, shape, f32)

    dt0 = jnp.exp(jax.random.uniform(ks[10], (N_EVEN, 2, SSD_HEADS), f32)
                  * (math.log(DT_MAX) - math.log(DT_MIN)) + math.log(DT_MIN))
    dt_bias = dt0 + jnp.log(-jnp.expm1(-dt0))
    A_log = jnp.log(jax.random.uniform(ks[11], (N_EVEN, 2, SSD_HEADS), f32, 1.0, 16.0))
    return {
        "x": jax.random.normal(ks[0], (BATCH, SEQ, D_MODEL), f32),
        "even_mix_norm": gain(ks[1], (N_EVEN, D_MODEL)),
        "even_w_in": normal(ks[2], (N_EVEN, D_MODEL, EVEN_IN_WIDTH), D_MODEL ** -0.5),
        "na_q_norm": gain(ks[3], (N_EVEN, NA_HEAD_DIM)),
        "na_k_norm": gain(ks[4], (N_EVEN, NA_HEAD_DIM)),
        "na_rel_bias": normal(ks[5], (N_EVEN, NA_HEADS, 2 * NA_KH_MAX - 1, 2 * NA_KW - 1), 0.05),
        "ssd_conv_w": normal(ks[6], (N_EVEN, SSD_CONV, SSD_CONV_DIM), SSD_CONV ** -0.5),
        "ssd_conv_b": normal(ks[7], (N_EVEN, SSD_CONV_DIM), 0.01),
        "ssd_dt_bias": dt_bias,
        "ssd_A_log": A_log,
        "ssd_D": gain(ks[8], (N_EVEN, SSD_HEADS)),
        "ssd_out_norm": gain(ks[9], (N_EVEN, SSD_D_INNER)),
        "even_w_out": normal(ks[12], (N_EVEN, EVEN_MIX_WIDTH, D_MODEL), EVEN_MIX_WIDTH ** -0.5),
        "odd_mix_norm": gain(ks[13], (N_ODD, D_MODEL)),
        "odd_w_qkv": normal(ks[14], (N_ODD, D_MODEL, ODD_IN_WIDTH), D_MODEL ** -0.5),
        "gqa_q_norm": gain(ks[15], (N_ODD, GQA_HEAD_DIM)),
        "gqa_k_norm": gain(ks[16], (N_ODD, GQA_HEAD_DIM)),
        "odd_w_out": normal(ks[17], (N_ODD, GQA_Q_WIDTH, D_MODEL), GQA_Q_WIDTH ** -0.5),
        "ffn_norm": gain(ks[18], (DEPTH, D_MODEL)),
        "ffn_w13": normal(ks[19], (DEPTH, D_MODEL, 2 * FFN_HIDDEN), D_MODEL ** -0.5),
        "ffn_w2": normal(ks[20], (DEPTH, FFN_HIDDEN, D_MODEL), FFN_HIDDEN ** -0.5),
    }

def second_block(x, even_mix_norm, even_w_in, na_q_norm, na_k_norm, na_rel_bias, ssd_conv_w, ssd_conv_b,
              ssd_dt_bias, ssd_A_log, ssd_D, ssd_out_norm, even_w_out, odd_mix_norm, odd_w_qkv,
              gqa_q_norm, gqa_k_norm, odd_w_out, ffn_norm, ffn_w13, ffn_w2):
    for layer in range(DEPTH):
        i = layer // 2
        if layer % 2 == 0:
            x = x + even_mixer(x, even_mix_norm[i], even_w_in[i], na_q_norm[i], na_k_norm[i],
                               na_rel_bias[i], ssd_conv_w[i], ssd_conv_b[i], ssd_dt_bias[i],
                               ssd_A_log[i], ssd_D[i], ssd_out_norm[i], even_w_out[i])
        else:
            x = x + odd_mixer(x, odd_mix_norm[i], odd_w_qkv[i], gqa_q_norm[i], gqa_k_norm[i], odd_w_out[i])
        x = x + swiglu_ffn_2(x, ffn_norm[layer], ffn_w13[layer], ffn_w2[layer])
    return x


def setup_inputs(seed=0):
    out = dict(first_inputs(seed))
    for name, value in second_inputs(seed + 1).items():
        if name != "x":
            out[name + "_2"] = value
    return out


def reference(
    x, ffn_norm_pre, ffn_norm_post, ffn_w_gate_up, ffn_w_down, mix_norm_pre, mix_norm_post,
    conv_w_in, conv_b_in, conv_w_dw, conv_b_dw, conv_ln_g, conv_ln_b, conv_w_out, conv_b_out,
    kv_norm, w_kv, attn_w_q, attn_w_o, even_mix_norm_2, even_w_in_2, na_q_norm_2, na_k_norm_2,
    na_rel_bias_2, ssd_conv_w_2, ssd_conv_b_2, ssd_dt_bias_2, ssd_A_log_2, ssd_D_2,
    ssd_out_norm_2, even_w_out_2, odd_mix_norm_2, odd_w_qkv_2, gqa_q_norm_2, gqa_k_norm_2,
    odd_w_out_2, ffn_norm_2, ffn_w13_2, ffn_w2_2,
):
    x = first_block(
        x, ffn_norm_pre, ffn_norm_post, ffn_w_gate_up, ffn_w_down, mix_norm_pre, mix_norm_post,
        conv_w_in, conv_b_in, conv_w_dw, conv_b_dw, conv_ln_g, conv_ln_b, conv_w_out,
        conv_b_out, kv_norm, w_kv, attn_w_q, attn_w_o,
    )
    return second_block(
        x, even_mix_norm_2, even_w_in_2, na_q_norm_2, na_k_norm_2, na_rel_bias_2, ssd_conv_w_2,
        ssd_conv_b_2, ssd_dt_bias_2, ssd_A_log_2, ssd_D_2, ssd_out_norm_2, even_w_out_2,
        odd_mix_norm_2, odd_w_qkv_2, gqa_q_norm_2, gqa_k_norm_2, odd_w_out_2, ffn_norm_2,
        ffn_w13_2, ffn_w2_2,
    )


_drawn_inputs = setup_inputs


def setup_inputs(seed=0):
    import zlib

    import numpy as np

    out = dict(_drawn_inputs(seed))
    spreads = {}
    factors = {'ffn_norm_post': 3.133,
     'kv_norm': 3.862,
     'even_mix_norm_2': 4.556,
     'na_q_norm_2': 8.0,
     'na_k_norm_2': 8.0,
     'na_rel_bias_2': 8.0,
     'ssd_conv_b_2': 8.0,
     'ssd_D_2': 200.0,
     'ssd_out_norm_2': 6.736,
     'odd_mix_norm_2': 8.0,
     'gqa_q_norm_2': 8.0,
     'gqa_k_norm_2': 8.0,
     'ffn_norm_2': 5.234}
    for name, (base, spread) in spreads.items():
        noise = np.random.default_rng([zlib.crc32(name.encode()), seed]).standard_normal(out[name].shape)
        drawn = base * np.exp(spread * noise) if base else spread * noise
        out[name] = __import__('jax').numpy.asarray(drawn.astype(out[name].dtype))
    for name, factor in factors.items():
        out[name] = (out[name] * factor).astype(out[name].dtype)
    return out
```

```python
from contextlib import ExitStack

import numpy as np

import concourse.bass as bass
from concourse import mybir

F32 = mybir.dt.float32
F32R = mybir.dt.float32r
ACT = mybir.ActivationFunctionType
ALU = mybir.AluOpType
AX = mybir.AxisListType

D = 1024
FF = 2816
NJ = FF // 256
RAW = 4
RING = 4
TAPS = 31
BIG = 1.0e33
NEG = -1.0e30

GAINS = (["pre00", "post00", "mixpre0", "lng", "lnb", "mixpost0", "pre01", "post01", "pre10", "post10",
          "kv", "mixpre1", "mixpost1", "pre11", "post11", "evenmix", "ssdnorm", "ffn0", "oddmix", "ffn1"])

CST = {}
COLS = {}


def _layout(table, items):
    at = 0
    for name, n in items:
        table[name] = (at, n)
        at += n
    return at


N_CST = _layout(CST, [("ident", 128), ("tf", 128), ("tb", 128), ("ones", 128), ("mf", 128), ("mb", 128),
                      ("dm", 512), ("cap", 256), ("cos", 128), ("sin", 128)])
N_KEEP = 128
N_COLS = _layout(COLS, [("dw", 8 * TAPS), ("dwb", 8), ("cw", 64), ("cb", 16), ("wdt", 256)])


def constants():
    c = np.zeros((128, N_CST), np.float32)

    def put(name, v):
        a, n = CST[name]
        c[:, a:a + n] = v.reshape(128, n)

    i = np.arange(128)
    put("ident", np.eye(128))
    put("tf", (i[:, None] <= i[None, :]))
    put("tb", (i[:, None] >= i[None, :]))
    put("ones", np.ones((128, 128)))
    put("mf", np.where(i[:, None] <= i[None, :], 0.0, NEG))
    put("mb", np.where(i[:, None] >= i[None, :], 0.0, NEG))
    q = i[:, None, None] + 128 * np.arange(2)[None, :, None]
    k = np.arange(256)[None, None, :]
    put("dm", np.where(k <= q, q - k, BIG))
    cq = i % 64
    st = np.clip(cq - 8, 0, 48)
    kc = np.arange(256) % 64
    put("cap", np.where((kc[None] >= st[:, None]) & (kc[None] < st[:, None] + 16), 3.0e38, NEG))
    t = i[:, None] + 128 * np.arange(2)[None, :]
    freqs = (np.float32(10000.0) ** (-np.arange(0, 32, 2, dtype=np.float32) / np.float32(32))).astype(np.float32)
    ang = np.concatenate([(t // 64).astype(np.float32)[:, :, None] * freqs,
                          (t % 64).astype(np.float32)[:, :, None] * freqs], axis=-1)
    put("cos", np.repeat(np.cos(ang), 2, axis=-1))
    s = np.repeat(np.sin(ang), 2, axis=-1)
    s[:, :, 0::2] *= -1.0
    put("sin", s)
    return c


def pack_stream(i):
    out = []

    def cols(w, spans):
        w = np.concatenate([w[:, a:b] for a, b in spans], axis=1)
        v = w.reshape(2, 4, 128, 512).transpose(0, 2, 1, 3).reshape(2, 128, 2048)
        out.extend([v[0], v[1]])

    def rows(w, r0):
        out.append(w[r0:r0 + 256].reshape(2, 128, 1024).transpose(1, 0, 2).reshape(128, 2048))

    def ffn(wgu, wd):
        for j in range(NJ):
            cols(wgu, [(256 * j, 256 * j + 256), (FF + 256 * j, FF + 256 * j + 256)])
            if j:
                rows(wd, 256 * (j - 1))
        rows(wd, 256 * (NJ - 1))

    gu, dn = i["ffn_w_gate_up"], i["ffn_w_down"]
    ffn(gu[0, 0], dn[0, 0])
    for j in range(4):
        cols(i["conv_w_in"][0], [(256 * j, 256 * j + 256), (1024 + 256 * j, 1280 + 256 * j)])
    for j in range(4):
        rows(i["conv_w_out"][0], 256 * j)
    ffn(gu[0, 1], dn[0, 1])
    ffn(gu[1, 0], dn[1, 0])
    for j in range(4):
        cols(i["w_kv"], [(512 * j, 512 * j + 512)])
    for j in range(2):
        cols(i["attn_w_q"][0], [(512 * j, 512 * j + 512)])
    for j in range(4):
        rows(i["attn_w_o"][0], 256 * j)
    ffn(gu[1, 1], dn[1, 1])
    we = i["even_w_in_2"][0]
    for c in (2560, 3072, 3584, 4096, 0, 512, 1024, 1536, 2048):
        cols(we, [(c, c + 512)])
    for j in range(6):
        rows(i["even_w_out_2"][0], 256 * j)
    ffn(i["ffn_w13_2"][0], i["ffn_w2_2"][0])
    for j in range(3):
        cols(i["odd_w_qkv_2"][0], [(512 * j, 512 * j + 512)])
    for j in range(4):
        rows(i["odd_w_out_2"][0], 256 * j)
    ffn(i["ffn_w13_2"][1], i["ffn_w2_2"][1])
    return np.stack(out)


def pack_rows(i):
    a, b = i["ffn_norm_pre"], i["ffn_norm_post"]
    v = {"pre00": a[0, 0], "post00": b[0, 0], "pre01": a[0, 1], "post01": b[0, 1],
         "pre10": a[1, 0], "post10": b[1, 0], "pre11": a[1, 1], "post11": b[1, 1],
         "mixpre0": i["mix_norm_pre"][0], "mixpre1": i["mix_norm_pre"][1],
         "mixpost0": i["mix_norm_post"][0], "mixpost1": i["mix_norm_post"][1],
         "lng": i["conv_ln_g"][0], "lnb": i["conv_ln_b"][0], "kv": i["kv_norm"],
         "evenmix": i["even_mix_norm_2"][0], "ssdnorm": i["ssd_out_norm_2"][0],
         "ffn0": i["ffn_norm_2"][0], "ffn1": i["ffn_norm_2"][1], "oddmix": i["odd_mix_norm_2"][0]}
    return np.stack([v[n] for n in GAINS])


SMALL = {}
N_SMALL = _layout(SMALL, [("naq", 64), ("nak", 64), ("gq", 64), ("gk", 64), ("dtb", 32), ("alog", 32), ("dskip", 16)])


def pack_small(i):
    return np.concatenate([i["na_q_norm_2"][0], i["na_k_norm_2"][0], i["gqa_q_norm_2"][0], i["gqa_k_norm_2"][0],
                           i["ssd_dt_bias_2"][0].ravel(), i["ssd_A_log_2"][0].ravel(), i["ssd_D_2"][0]])[None]


def pack_cols(i):
    def tiles(v, n):
        return v.reshape(-1, n, 128).transpose(2, 1, 0).reshape(128, -1)

    wdt = i["even_w_in_2"][0][:, 4608:4640].reshape(8, 128, 32).transpose(1, 0, 2).reshape(128, 256)
    return np.concatenate([tiles(i["conv_w_dw"][0], 8), tiles(i["conv_b_dw"], 8), tiles(i["ssd_conv_w_2"][0], 16),
                           tiles(i["ssd_conv_b_2"], 16), wdt], axis=1)


def pack_bias(i):
    return np.concatenate([i["conv_b_in"][0].reshape(2, 4, 256).transpose(1, 0, 2).ravel(), i["conv_b_out"][0]])[None]


def build(nc, x_in, w_in, rows_in, small_in, cols_in, bias_in, rpb_in, cst_in, out, stop=None):
    ctx = ExitStack()
    with ctx:
        def sb(name, shape, dt=F32, stack=ctx):
            return stack.enter_context(nc.sbuf_tensor(name, shape, dt))

        sems = {}
        counts = {}

        def sem(key):
            sems[key] = ctx.enter_context(nc.semaphore("s_" + key))
            counts[key] = 0
            return key

        engines = {"pe": nc.tensor, "act": nc.scalar, "dve": nc.vector, "pool": nc.gpsimd, "sp": nc.sync}
        for e in ("pe", "act", "dve", "pool"):
            sem(e)
        passed = {e: {} for e in engines}

        def wait(e, *toks):
            for tok in toks:
                if tok is None:
                    continue
                key, n = tok
                if passed[e].get(key, 0) < n:
                    engines[e].wait_ge(sems[key], n)
                    passed[e][key] = n

        def signal(key, ins, n=1):
            counts[key] += n
            ins.then_inc(sems[key], n)
            return (key, counts[key])

        def A(after, out_, in_, func, **kw):
            wait("act", *after)
            return signal("act", nc.scalar.activation(out_, in_, func, **kw))

        def V(after, op, *a, **kw):
            wait("dve", *after)
            return signal("dve", op(*a, **kw))

        def G(after, op, *a, **kw):
            wait("pool", *after)
            return signal("pool", op(*a, **kw))

        TT, TS, STT = nc.vector.tensor_tensor, nc.vector.tensor_scalar, nc.vector.scalar_tensor_tensor

        def load(e, key, dst, src, after=()):
            wait(e, *after)
            return signal(key, engines[e].dma_start(dst, src), 16)

        def MM(o, l, r, start, stop, skip=False):
            return nc.tensor.matmul(o, l, r, start=start, stop=stop, skip_group_check=skip)

        def mm3(o, lh, ll, rh, rl, start, stop):
            MM(o, lh, rh, start, False)
            MM(o, lh, rl, False, False)
            return MM(o, ll, rh, False, stop)

        def done(ins):
            return signal("pe", ins)

        def spread(ap, at, n):
            dims = [list(d) for d in ap.ap]
            return bass.AP(tensor=ap.tensor, offset=ap.offset, ap=dims[:at] + [[0, n]] + dims[at:])

        ps = ctx.enter_context(nc.psum_tensor("ps", [128, 4096], F32))
        emptied = {b: [] for b in range(8)}

        def bank(b, n=1):
            return ps[:, 512 * b:512 * (b + n)]

        def after_emptied(*bs):
            for b in bs:
                wait("pe", *emptied[b])
                emptied[b] = []

        raw = sb("raw", [128, RAW, 2048])
        wh = sb("wh", [128, RING, 2048], F32R)
        wl = sb("wl", [128, RING, 2048], F32R)
        x = sb("x", [128, 2, D])
        xTh = sb("xTh", [128, 8, 2, 128], F32R)
        xTl = sb("xTl", [128, 8, 2, 128], F32R)
        gains = sb("gains", [128, 4, D])
        xn = sb("xn", [128, 2, D])
        tmp = sb("tmp", [128, D])
        ident = sb("ident", [128, 128])
        cols = sb("cols", [128, N_COLS])
        small = sb("small", [128, N_SMALL])
        st = sb("st", [128, 512])
        mhalf = sb("mhalf", [128, 8])
        ones1 = sb("ones1", [1, 128])

        for n in range(RAW):
            sem(f"raw{n}")
        for n in range(4):
            sem(f"gain{n}")
        for n in ("x", "ident", "cols", "small", "bias", "cst", "out", "nab0", "nab1"):
            sem(n)

        at = [0]

        def stat(n=1):
            a = at[0]
            at[0] += n
            assert at[0] <= 512
            return st[:, a:a + n]

        t_half = G([], nc.gpsimd.memset, mhalf[:, :], -0.5)
        t_one = G([], nc.gpsimd.memset, ones1[:, :], 1.0)
        t_x = load("act", "x", x[:, :, :], x_in.rearrange("(t p) d -> p t d", p=128))
        t_ident = load("act", "ident", ident[:, :], cst_in[:, 0:128])
        t_cols = load("act", "cols", cols[:, :], cols_in)

        n_pieces = w_in.shape[0]
        fetched, landed, split_done, multiplied = [0], {}, {}, {}

        def fetch_to(n):
            while fetched[0] < min(n, n_pieces):
                p = fetched[0]
                w = [split_done[p - RAW]] if p >= RAW else []
                landed[p] = load("sp", f"raw{p % RAW}", raw[:, p % RAW, :], w_in[p], w)
                fetched[0] += 1

        n_split = [0]

        def split_to(n):
            while n_split[0] < min(n, n_pieces):
                p = n_split[0]
                fetch_to(p + 1)
                r, s = p % RAW, p % RING
                w = [multiplied[p - RING]] if p >= RING else []
                h = A([landed[p]] + w, wh[:, s, :], raw[:, r, :], ACT.Copy)
                split_done[p] = V([h], TT, wl[:, s, :], raw[:, r, :], wh[:, s, :].bitcast(F32), ALU.subtract)
                n_split[0] += 1
                fetch_to(p + 1 + RAW)

        fetch_to(RAW)
        t_small = load("sp", "small", small[:, :], spread(small_in[0, :], 0, 128))

        g_at, g_tok, gain_applied = [0], {}, {}

        def gain_to(n):
            while g_at[0] < min(n, len(GAINS)):
                i = g_at[0]
                w = gain_applied[i - 4] if i >= 4 else []
                g_tok[i] = load("sp", f"gain{i % 4}", gains[:, i % 4, :], spread(rows_in[i, :], 0, 128), w)
                g_at[0] += 1

        def gain(name):
            i = GAINS.index(name)
            return gains[:, i % 4, :], g_tok[i], i

        def gain_next():
            while g_at[0] < len(GAINS) and g_at[0] - 4 in gain_applied:
                gain_to(g_at[0] + 1)

        gain_to(4)
        piece = [0]

        def take(n):
            p = piece[0]
            piece[0] += n
            split_to(p + n)
            while n_split[0] - RING in multiplied and n_split[0] < min(p + RING, n_pieces):
                split_to(n_split[0] + 1)
            return p

        split_to(2)

        def wcols(p):
            s = p % RING
            return (wh[:, s, :].rearrange("p (k n) -> p k n", k=4), wl[:, s, :].rearrange("p (k n) -> p k n", k=4))

        def wrows(p):
            s = p % RING
            return (wh[:, s, :].rearrange("p (k n) -> p k n", k=2), wl[:, s, :].rearrange("p (k n) -> p k n", k=2))

        def project(p, t, b, act, act_tok, bias=None):
            wait("pe", *act_tok[t])
            after_emptied(b)
            if bias is not None:
                MM(bank(b), ones1[0:1, :], bias, True, False)
            for half in range(2):
                wait("pe", split_done[p + half])
                H, L = wcols(p + half)
                for k in range(4):
                    kk = 4 * half + k
                    last = mm3(bank(b), act[0][:, kk, t, :], act[1][:, kk, t, :], H[:, k, :], L[:, k, :],
                               kk == 0 and bias is None, kk == 7)
                tok = done(last)
                if t == 1:
                    multiplied[p + half] = tok
            return tok

        def project_t(p, act, act_tok, b0):
            wait("pe", *act_tok[0], *act_tok[1], split_done[p], split_done[p + 1])
            toks = []
            for n in range(4):
                b = b0 + n // 2
                if n % 2 == 0:
                    after_emptied(b)
                o = bank(b)[:, 256 * (n % 2):256 * (n % 2) + 256]
                for kk in range(8):
                    H, L = wcols(p + kk // 4)
                    a, c = H[:, kk % 4, 128 * n:128 * n + 128], L[:, kk % 4, 128 * n:128 * n + 128]
                    MM(o, a, act[0][:, kk, :, :], kk == 0, False)
                    MM(o, c, act[0][:, kk, :, :], False, False)
                    last = MM(o, a, act[1][:, kk, :, :], False, kk == 7)
                if n % 2 == 1:
                    toks.append(done(last))
            multiplied[p] = multiplied[p + 1] = toks[1]
            return toks

        def down(p, t, lhs, first, last_, toks=()):
            wait("pe", split_done[p], *toks)
            if first:
                after_emptied(2 * t, 2 * t + 1)
            H, L = wrows(p)
            for k in range(2):
                for half in range(2):
                    r = slice(512 * half, 512 * half + 512)
                    m = mm3(bank(2 * t + half), lhs(k)[0], lhs(k)[1], H[:, k, r], L[:, k, r],
                            first and k == 0, last_ and k == 1)
            tok = done(m)
            if t == 1:
                multiplied[p] = tok
            return tok

        x_tok = [t_x, t_x]
        xn_turned = [[], []]
        tmp_added = [[]]

        def rstd(tok, ss, mul, add, n=1):
            v, r = stat(n), stat(n)
            g = G([tok], nc.gpsimd.tensor_scalar, v, ss, mul, add, ALU.mult, ALU.add)
            return G([g, t_half], nc.gpsimd.tensor_tensor, r, v, mhalf[:, 0:n], ALU.pow), r

        def post(t, tok, name, half):
            a = bank(2 * t, 2)
            if name is None:
                x_tok[t] = V([tok, x_tok[t]], TT, x[:, t, :], x[:, t, :], a, ALU.add)
                emptied[2 * t] = emptied[2 * t + 1] = [x_tok[t]]
                return
            ss = stat()
            s = A([tok, *tmp_added[0]], tmp[:, :], a, ACT.Square, accum_out=ss)
            m = 4.0 if half else 1.0
            g, r = rstd(s, ss, m / D, m * 1e-6)
            ga, gt, gi = gain(name)
            v = V([g, gt] + tmp_added[0], STT, tmp[:, :], a, r, ga, ALU.mult, ALU.mult)
            emptied[2 * t] = emptied[2 * t + 1] = [v]
            gain_applied[gi] = [v]
            x_tok[t] = V([v, x_tok[t]], TT, x[:, t, :], x[:, t, :], tmp[:, :], ALU.add)
            tmp_added[0] = [x_tok[t]]

        def transposed(src, n, b, after):
            wait("pe", t_ident, *after)
            after_emptied(b)
            for k in range(n):
                m = nc.tensor.transpose(bank(b)[:, 128 * k:128 * k + 128], src(k), ident[:, :])
            return done(m)

        def hilo(b, src, dh, dl, tok, after=()):
            h = A([tok, *after], dh, src, ACT.Copy)
            v = V([h], TT, dl, src, dh.bitcast(F32), ALU.subtract)
            emptied[b] = [v]
            return v

        def flip(t, src, tok, act, after=()):
            toks = []
            for b in range(2):
                tr = transposed(lambda k: src[:, 512 * b + 128 * k:512 * b + 128 * k + 128], 4, 6 + b, [tok])
                s = bank(6 + b).rearrange("p (k n) -> p k n", k=4)
                toks.append(hilo(6 + b, s, act[0][:, 4 * b:4 * b + 4, t, :], act[1][:, 4 * b:4 * b + 4, t, :], tr, after))
            return tr, toks

        def norm_stat(t):
            ss = stat()
            s = A([x_tok[t], *xn_turned[t]], xn[:, t, :], x[:, t, :], ACT.Square, accum_out=ss)
            return rstd(s, ss, 1.0 / D, 1e-6)

        def pre(t, name, act, stats=None, after=()):
            g, rs = stats or norm_stat(t)
            ga, gt, gi = gain(name)
            v = V([g, gt, x_tok[t]] + xn_turned[t], STT, xn[:, t, :], x[:, t, :], rs, ga, ALU.mult, ALU.mult)
            gain_applied[gi] = [v]
            tr, toks = flip(t, xn[:, t, :], v, act, after)
            xn_turned[t] = [tr]
            return toks

        xT = (xTh, xTl)
        ready = [None, None]
        xT_multiplied = [[]]

        def ffn(tag, ph_w):
            ph = ExitStack()
            with ph:
                hTh = sb(f"hTh{tag}", [128, 2, 2, 2, 128], F32R, ph)
                hTl = sb(f"hTl{tag}", [128, 2, 2, 2, 128], F32R, ph)
                sg = sb(f"sg{tag}", [128, 2, 256], F32, ph)
                hb = sb(f"hb{tag}", [128, 2, 256], F32, ph)
                hT_multiplied = {}
                hb_turned = [[], []]
                hT_tok = {}
                last = [None, None]

                def turn(j):
                    after_emptied(6)
                    wait("pe", t_ident, *hb_tok)
                    for ft in range(2):
                        for t in range(2):
                            m = nc.tensor.transpose(bank(6)[:, 256 * ft + 128 * t:256 * ft + 128 * t + 128],
                                                    hb[:, t, 128 * ft:128 * ft + 128], ident[:, :])
                    tr = done(m)
                    hb_turned[0] = hb_turned[1] = [tr]
                    src = bank(6).rearrange("p (f t n) -> p f t n", f=2, t=2)
                    hT_tok[j] = hilo(6, src, hTh[:, j % 2], hTl[:, j % 2], tr, hT_multiplied.get(j - 2, ()))

                def dn(j, p, t):
                    last[t] = down(p, t, lambda k: (hTh[:, j % 2, k, t, :], hTl[:, j % 2, k, t, :]), j == 0,
                                   j == NJ - 1, [hT_tok[j]])
                    if t == 1:
                        hT_multiplied[j] = [last[t]]

                hb_tok = []
                for j in range(NJ):
                    p = take(2)
                    gt = [project(p, t, 4 + t, xT, ready) for t in range(2)]
                    hb_tok = []
                    for t in range(2):
                        b = bank(4 + t)
                        s = A([gt[t], *hb_turned[t], *ph_w], sg[:, t, :], b[:, 0:256], ACT.Silu)
                        v = V([s], TT, hb[:, t, :], sg[:, t, :], b[:, 256:512], ALU.mult)
                        emptied[4 + t] = [v]
                        hb_tok.append(v)
                    if j:
                        q = take(1)
                        dn(j - 1, q, 0)
                        if j < NJ - 1:
                            turn(j)
                            dn(j - 1, q, 1)
                        else:
                            turn(j)
                            q2 = take(1)
                            dn(j, q2, 0)
                            dn(j - 1, q, 1)
                            dn(j, q2, 1)
                    else:
                        turn(j)
                xT_multiplied[0] = gt
                return last

        def flow(last, post_name, half, pre_name, then):
            for t in range(2):
                post(t, last[t], post_name, half)
                if pre_name:
                    ready[t] = pre(t, pre_name, xT, None, xT_multiplied[0])
            gain_next()

        def write_out():
            for t in range(2):
                tk = load("sp", "out", out.rearrange("(t p) d -> p t d", p=128)[:, t, :], x[:, t, :], [x_tok[t]])
            wait("sp", tk)
            for key in counts:
                if counts[key]:
                    wait("sp", (key, counts[key]))

        def bounds():
            return [tok for r in ready for tok in (r or [])]

        for t in range(2):
            ready[t] = pre(t, "pre00", xT)
        last = ffn("a", [])
        flow(last, "post00", True, "mixpre0", None)
        if stop == "ffn0":
            return write_out()

        ph = ExitStack()
        with ph:
            PADL = TAPS - 1
            W = PADL + 256
            uT = sb("uT", [128, 8, W], F32, ph)
            ca = sb("ca", [128, 8, 256], F32, ph)
            sg = sb("csg", [128, 2, 256], F32, ph)
            ub = sb("cub", [128, 2, 256], F32, ph)
            brow = sb("brow", [1, 3072], F32, ph)
            ya = sb("ya", [128, 2, D], F32, ph)
            e0 = bounds()
            t_b = load("act", "bias", brow[:, :], bias_in, e0)
            t_z = G(e0, nc.gpsimd.memset, uT[:, :, 0:PADL], 0.0)
            wait("pe", t_b, t_one)
            ub_turned = [[], []]
            dw0, dwb = COLS["dw"][0], COLS["dwb"][0]
            ca_tok = {}

            def conv_part(j, u_tok):
                tap = {}
                for k in range(TAPS):
                    for c in (2 * j, 2 * j + 1):
                        src = uT[:, c, k:k + 256]
                        wk = cols[:, dw0 + TAPS * c + k:dw0 + TAPS * c + k + 1]
                        if k == 0:
                            tap[c] = V([u_tok, t_z, t_cols], TS, ca[:, c, :], src, wk, cols[:, dwb + c:dwb + c + 1],
                                       ALU.mult, ALU.add)
                        else:
                            tap[c] = V([tap[c]], STT, ca[:, c, :], src, wk, ca[:, c, :], ALU.mult, ALU.add)
                for c in tap:
                    ca_tok[c] = tap[c]

            for j in range(4):
                p = take(2)
                u_tok = []
                for t in range(2):
                    gt = project(p, t, 4 + t, xT, ready, brow[:, 512 * j:512 * j + 512])
                    b = bank(4 + t)
                    s = A([gt, *ub_turned[t], *e0], sg[:, t, :], b[:, 256:512], ACT.Sigmoid)
                    v = V([s], TT, ub[:, t, :], sg[:, t, :], b[:, 0:256], ALU.mult)
                    emptied[4 + t] = [v]
                    u_tok.append(v)
                after_emptied(6)
                wait("pe", *u_tok)
                for c in range(2):
                    for t in range(2):
                        m = nc.tensor.transpose(bank(6)[:, 256 * c + 128 * t:256 * c + 128 * t + 128],
                                                ub[:, t, 128 * c:128 * c + 128], ident[:, :])
                tr = done(m)
                ub_turned = [[tr], [tr]]
                e = A([tr, *e0], uT[:, 2 * j:2 * j + 2, PADL:W], bank(6).rearrange("p (c n) -> p c n", c=2), ACT.Copy)
                emptied[6] = [e]
                conv_part(j, e)
            xT_multiplied[0] = [gt]
            lg, lgt, lgi = gain("lng")
            lb, lbt, lbi = gain("lnb")
            for t in range(2):
                after_emptied(2 * t, 2 * t + 1)
                for c in range(8):
                    wait("pe", ca_tok[c])
                    m = nc.tensor.transpose(bank(2 * t, 2)[:, 128 * c:128 * c + 128], ca[:, c, 128 * t:128 * t + 128],
                                            ident[:, :])
                tr = done(m)
                bs, mv, nm = stat(12), stat(2), stat()
                for h in range(2):
                    b = V([tr], nc.vector.bn_stats, bs[:, 6 * h:6 * h + 6], bank(2 * t + h))
                b = V([b], nc.vector.bn_aggr, mv, bs)
                g, r = rstd(b, mv[:, 1:2], 1.0, 1e-5)
                n = V([g], STT, nm, mv[:, 0:1], -1.0, r, ALU.mult, ALU.mult)
                a = A([n, *e0], ya[:, t, :], bank(2 * t, 2), ACT.Identity, bias=nm, scale=r)
                emptied[2 * t] = emptied[2 * t + 1] = [a]
                v = V([a, lgt], TT, ya[:, t, :], ya[:, t, :], lg, ALU.mult)
                v = V([v, lbt], TT, ya[:, t, :], ya[:, t, :], lb, ALU.add)
                gain_applied[lgi] = gain_applied[lbi] = [v]
                a = A([v, *xn_turned[t]], xn[:, t, :], ya[:, t, :], ACT.Silu)
                tr, ready[t] = flip(t, xn[:, t, :], a, xT, xT_multiplied[0])
                xn_turned[t] = [tr]
            gain_next()
            p = take(4)
            last = [None, None]
            for t in range(2):
                wait("pe", *ready[t])
                after_emptied(2 * t, 2 * t + 1)
                for h in range(2):
                    MM(bank(2 * t + h), ones1[0:1, :], brow[:, 2048 + 512 * h:2560 + 512 * h], True, False)
                for q in range(4):
                    wait("pe", split_done[p + q])
                    H, L = wrows(p + q)
                    for k in range(2):
                        kk = 2 * q + k
                        for h in range(2):
                            m = mm3(bank(2 * t + h), xTh[:, kk, t, :], xTl[:, kk, t, :], H[:, k, 512 * h:512 * h + 512],
                                    L[:, k, 512 * h:512 * h + 512], False, kk == 7)
                    last[t] = done(m)
                    if t == 1:
                        multiplied[p + q] = last[t]
            xT_multiplied[0] = [last[1]]
        flow(last, "mixpost0", False, "pre01", None)
        if stop == "conv":
            return write_out()
        last = ffn("b", bounds())
        flow(last, "post01", True, "pre10", None)
        last = ffn("c", bounds())
        if stop == "ffn10":
            flow(last, "post10", True, None, None)
            return write_out()

        def attention(tag, ph, n_pairs, M, W, q_of, k_of, v_of, v_tok, bias, oT, e0):
            sc = sb(f"sc{tag}", [128, 2, 2, 2, 256], F32, ph)
            PT = sb(f"PT{tag}", [128, 2, 2, 2, 256], F32, ph)
            p_turned = {}
            pt_multiplied = {}
            o_tok = None

            def scores(i):
                s = i % 2
                out_ = []
                after_emptied(2 * s, 2 * s + 1)
                for t in range(2):
                    for hh in range(2):
                        l, lt = q_of(2 * i + hh, t)
                        r, rt = k_of(2 * i + hh, W[t])
                        wait("pe", *lt, *rt)
                        m = MM(bank(2 * s + hh)[:, 256 * t:256 * t + W[t]], l, r, True, True)
                tok = done(m)
                emptied[2 * s], emptied[2 * s + 1] = [], []
                for t in range(2):
                    P = sc[:, s, t, :, 0:W[t]]
                    S = bank(2 * s, 2).rearrange("p (h t n) -> p h t n", h=2, t=2)[:, :, t, 0:W[t]]
                    v = bias(i, t, P, S, [tok, *p_turned.get(i - 2, ()), *e0])
                    emptied[2 * s].append(v)
                    emptied[2 * s + 1].append(v)
                    mx, sm, rc = stat2(t, s)
                    mt = V([v], nc.vector.tensor_reduce, mx, P, AX.X, ALU.max, negate=True)
                    for hh in range(2):
                        a = A([mt], P[:, hh, :], P[:, hh, :], ACT.Exp, bias=mx[:, hh:hh + 1],
                              accum_out=sm[:, hh:hh + 1])
                    r = V([a], nc.vector.reciprocal, rc, sm)
                    for hh in range(2):
                        v = V([r], TS, P[:, hh, :], P[:, hh, :], rc[:, hh:hh + 1], None, ALU.mult)
                    out_.append(v)
                return out_

            def values(i, toks):
                s = i % 2
                pt = []
                for kk in range(2):
                    ts = [t for t in range(2) if W[t] > 128 * kk]
                    after_emptied(4 + kk)
                    wait("pe", *toks)
                    for hh in range(2):
                        for t in ts:
                            m = nc.tensor.transpose(bank(4 + kk)[:, 256 * hh + 128 * t:256 * hh + 128 * t + 128],
                                                    sc[:, s, t, hh, 128 * kk:128 * kk + 128], ident[:, :])
                    tr = done(m)
                    lo = 128 * ts[0]
                    src = bank(4 + kk).rearrange("p (h n) -> p h n", h=2)[:, :, lo:256]
                    dst = PT[:, s, kk, :, lo:256]
                    w = [tr, *pt_multiplied.get(i - 2, ()), *e0]
                    e = A(w, dst, src, ACT.Copy) if kk == 0 else V(w, nc.vector.tensor_copy, dst, src)
                    emptied[4 + kk] = [e]
                    pt.append((e, lo))
                p_turned[i] = [tr]
                ob = 6 + i % 2
                after_emptied(ob)
                wait("pe", *v_tok)
                for hh in range(2):
                    o = bank(ob)[:, 256 * hh:256 * hh + 256] if M == 128 else bank(ob)[64 * hh:64 * hh + 64, 0:256]
                    for kk in range(2):
                        e, lo = pt[kk]
                        wait("pe", e)
                        m = MM(o[:, lo:256], v_of(2 * i + hh, kk), PT[:, s, kk, hh, lo:256], kk == 0, kk == 1)
                tok = done(m)
                pt_multiplied[i] = [tok]
                if M == 128:
                    src = bank(ob).rearrange("p (h t n) -> p h t n", h=2, t=2)
                    d = slice(2 * i, 2 * i + 2)
                    return hilo(ob, src, oT[0][:, d, :, :], oT[1][:, d, :, :], tok, [*e0, *xT_multiplied[0]])
                src = bank(ob)[:, 0:256].rearrange("p (t n) -> p t n", t=2)
                return hilo(ob, src, oT[0][:, i, :, :], oT[1][:, i, :, :], tok, [*e0, *xT_multiplied[0]])

            bufs = sb(f"sm{tag}", [128, 24], F32, ph)

            def stat2(t, s):
                a = 12 * s + 6 * t
                return bufs[:, a:a + 2], bufs[:, a + 2:a + 4], bufs[:, a + 4:a + 6]

            toks = scores(0)
            outs = []
            for i in range(n_pairs):
                nxt = scores(i + 1) if i + 1 < n_pairs else None
                outs.append(values(i, toks))
                toks = nxt
            return outs

        ph = ExitStack()
        with ph:
            kvh = sb("kvh", [128, 8, 2, 128], F32R, ph)
            kvl = sb("kvl", [128, 8, 2, 128], F32R, ph)
            kT = sb("kT", [128, 8, 256], F32, ph)
            qT = sb("qT", [128, 8, 256], F32, ph)
            vv = sb("vv", [128, 2, D], F32, ph)
            dm = sb("dm", [128, 2, 256], F32, ph)
            kready = [None, None]
            ends = [*last]
            for t in range(2):
                post(t, last[t], "post10", True)
                r = norm_stat(t)
                kready[t] = pre(t, "kv", (kvh, kvl), r, ends)
                ready[t] = pre(t, "mixpre1", xT, r, xT_multiplied[0])
            e0 = bounds()
            gain_next()
            a0 = CST["dm"][0]
            t_dm = load("sp", "cst", dm[:, :, :], cst_in[:, a0:a0 + 512].rearrange("p (t n) -> p t n", t=2), e0)

            def heads_t(dst, act, tok, scale):
                toks = []
                for j in range(2):
                    p = take(2)
                    for n, m in enumerate(project_t(p, act, tok, 4)):
                        h = 4 * j + 2 * n
                        toks.append(A([m, *e0], dst[:, h:h + 2, :], bank(4 + n).rearrange("p (h n) -> p h n", h=2),
                                      ACT.Copy, scale=scale))
                        emptied[4 + n] = [toks[-1]]
                return toks

            k_tok = heads_t(kT, (kvh, kvl), kready, 1.0)
            v_tok = []
            for j in range(2):
                p = take(2)
                for t in range(2):
                    gt = project(p, t, 4 + t, (kvh, kvl), kready)
                    v_tok.append(A([gt, *e0], vv[:, t, 512 * j:512 * j + 512], bank(4 + t), ACT.Copy))
                    emptied[4 + t] = [v_tok[-1]]
            q_tok = heads_t(qT, xT, ready, float(128 ** -0.5))
            xT_multiplied[0] = [("pe", counts["pe"])]

            def alibi(i, t, P, S, after):
                n = P.shape[2]
                for hh in range(2):
                    v = V([t_dm, *after], STT, P[:, hh, :], dm[:, t, 0:n], -float(2.0 ** -(2 * i + hh + 1)), S[:, hh, :],
                          ALU.mult, ALU.add)
                return v

            o_tok = attention("a", ph, 4, 128, [128, 256],
                              lambda h, t: (qT[:, h, 128 * t:128 * t + 128], q_tok),
                              lambda h, n: (kT[:, h, 0:n], k_tok),
                              lambda h, kk: vv[:, kk, 128 * h:128 * h + 128], v_tok, alibi, xT, e0)
            p = take(4)
            last = [None, None]
            for t in range(2):
                for q in range(4):
                    last[t] = down(p + q, t, lambda k: (xTh[:, 2 * q + k, t, :], xTl[:, 2 * q + k, t, :]), q == 0,
                                   q == 3, o_tok)
            xT_multiplied[0] = [last[1]]
        flow(last, "mixpost1", False, "pre11", None)
        if stop == "attn":
            return write_out()
        last = ffn("d", bounds())
        flow(last, "post11", True, "evenmix", None)
        if stop == "ffn11":
            return write_out()

        def head_norm(tag, src, n, gname, dst, tok, after, mul, add, sq, sq_summed):
            a0 = SMALL[gname][0]
            g64 = small[:, a0:a0 + 64]
            ss, v, r = stat(n), stat(n), stat(n)
            s = A([tok, *sq_summed], sq[:, 0:64 * n], src, ACT.Square)
            s = V([s], nc.vector.tensor_reduce, ss, sq[:, 0:64 * n].rearrange("p (h d) -> p h d", d=64), AX.X, ALU.add)
            g = G([s], nc.gpsimd.tensor_scalar, v, ss, mul, add, ALU.mult, ALU.add)
            g = G([g, t_half], nc.gpsimd.tensor_tensor, r, v, mhalf[:, 0:n], ALU.pow)
            src3 = src.rearrange("p (h d) -> p h d", d=64)
            v1 = V([g, *after], TT, dst, src3, spread(r, 2, 64), ALU.mult)
            v2 = V([v1, t_small], TT, dst, dst, spread(g64, 1, n), ALU.mult)
            return v1, v2, s

        ph = ExitStack()
        with ph:
            oTh = sb("oTh", [128, 4, 2, 128], F32R, ph)
            oTl = sb("oTl", [128, 4, 2, 128], F32R, ph)
            xc = sb("xc", [128, 16, 256], F32, ph)
            dz = sb("dz", [128, 8, 64], F32, ph)
            nac = sb("nac", [128, 64], F32, ph)
            e0 = bounds()
            xw = [*e0]
            ph2 = ExitStack()
            with ph2:
                kTn = sb("kTn", [128, 4, 256], F32, ph2)
                qTn = sb("qTn", [128, 4, 256], F32, ph2)
                vn = sb("vn", [128, 2, 512], F32, ph2)
                ph3 = ExitStack()
                ctx.enter_context(ph3)
                xp = sb("xp", [128, 4, 260], F32, ph3)
                qn = sb("qn", [128, 2, 512], F32, ph3)
                sq = sb("sqn", [128, 512], F32, ph3)
                wdh = sb("wdh", [128, 8, 32], F32R, ph3)
                wdl = sb("wdl", [128, 8, 32], F32R, ph3)
                t_z = G(e0, nc.gpsimd.memset, xp[:, :, 0:2], 0.0)
                t_z = G(e0, nc.gpsimd.memset, xp[:, :, 258:260], 0.0)
                wd = cols[:, COLS["wdt"][0]:COLS["wdt"][0] + 256].rearrange("p (k n) -> p k n", k=8)
                t_wd = A([t_cols, *e0], wdh[:, :, :], wd, ACT.Copy)
                t_wd = V([t_wd], TT, wdl[:, :, :], wd, wdh[:, :, :].bitcast(F32), ALU.subtract)
                xp_convolved = {0: [], 1: []}
                xc_tok = {}
                cw0, cb0 = COLS["cw"][0], COLS["cb"][0]
                for c in range(4):
                    p = take(2)
                    for n, m in enumerate(project_t(p, xT, ready, 4)):
                        e = A([m, t_z, *e0, *xp_convolved[n]], xp[:, 2 * n:2 * n + 2, 2:258],
                              bank(4 + n).rearrange("p (h n) -> p h n", h=2), ACT.Copy)
                        emptied[4 + n] = [e]
                        tap = {}
                        for k in range(4):
                            for u in range(2):
                                ch = 4 * c + 2 * n + u
                                wk = cols[:, cw0 + 4 * ch + k:cw0 + 4 * ch + k + 1]
                                s = xp[:, 2 * n + u, k:k + 256]
                                if k == 0:
                                    tap[u] = V([e], TS, xc[:, ch, :], s, wk, cols[:, cb0 + ch:cb0 + ch + 1], ALU.mult, ALU.add)
                                else:
                                    tap[u] = V([tap[u]], STT, xc[:, ch, :], s, wk, xc[:, ch, :], ALU.mult, ALU.add)
                        xp_convolved[n] = [tap[1]]
                        ch = 4 * c + 2 * n
                        xc_tok[ch] = xc_tok[ch + 1] = A([tap[0], tap[1]], xc[:, ch:ch + 2, :], xc[:, ch:ch + 2, :], ACT.Silu)
                sq_summed = []
                qk_tok = {}
                qn_turned = [[], []]
                for which, dst in (("naq", qTn), ("nak", kTn)):
                    p = take(2)
                    for t in range(2):
                        gt = project(p, t, 4 + t, xT, ready)
                        mul, add = (1.0, 64e-6) if which == "naq" else (1.0 / 64, 1e-6)
                        v1, v2, s = head_norm(which, bank(4 + t), 8, which,
                                              qn[:, t, :].rearrange("p (h d) -> p h d", d=64), gt, [*e0, *qn_turned[t]],
                                              mul, add, sq, [*sq_summed, *e0])
                        sq_summed = [s]
                        emptied[4 + t] = [v1]
                        tr = transposed(lambda k: qn[:, t, 128 * k:128 * k + 128], 4, 6 + t, [v2])
                        qn_turned[t] = [tr]
                        e = A([tr, *e0], dst[:, :, 128 * t:128 * t + 128], bank(6 + t).rearrange("p (k n) -> p k n", k=4), ACT.Copy)
                        emptied[6 + t] = [e]
                        qk_tok[which, t] = e
                p = take(2)
                v_tok = []
                for t in range(2):
                    gt = project(p, t, 4 + t, xT, ready)
                    v_tok.append(A([gt, *e0], vn[:, t, :], bank(4 + t), ACT.Copy))
                    emptied[4 + t] = [v_tok[-1]]
                after_emptied(6)
                wait("pe", t_wd)
                for t in range(2):
                    for k in range(8):
                        m = mm3(bank(6)[:, 32 * t:32 * t + 32], xTh[:, k, t, :], xTl[:, k, t, :], wdh[:, k, :], wdl[:, k, :],
                                k == 0, k == 7)
                dt_tok = done(m)
                db = small[:, SMALL["dtb"][0]:SMALL["dtb"][0] + 32]
                al = small[:, SMALL["alog"][0]:SMALL["alog"][0] + 32]
                d = [dz[:, i, :] for i in range(8)]
                d3 = [dz[:, i, :].rearrange("p (t n) -> p t n", t=2) for i in range(8)]
                v = V([dt_tok, t_small, *e0], TT, d3[0], bank(6)[:, 0:64].rearrange("p (t n) -> p t n", t=2), spread(db, 1, 2), ALU.add)
                emptied[6] = [v]
                v = V([v], STT, d[1], d[0], -1.0, d[0], ALU.mult, ALU.max)
                a = A([v], d[2], d[1], ACT.Exp, scale=-1.0)
                v = V([a], TS, d[3], d[2], 1.0, None, ALU.add)
                a = A([v], d[4], d[3], ACT.Ln)
                v = V([v], STT, d[5], d[3], -1.0, d[2], ALU.add, ALU.subtract)
                v = V([v], nc.vector.reciprocal, d[6], d[3])
                v = V([v], TT, d[5], d[5], d[6], ALU.mult)
                v = V([v, a], TT, d[4], d[4], d[5], ALU.subtract)
                v_dt = V([v], STT, d[0], d[0], 0.0, d[4], ALU.max, ALU.add)
                a = A([t_small, v], d[7][:, 0:32], al, ACT.Exp)
                v_a = V([a, v_dt], STT, d3[1], d3[0], -1.0, spread(d[7][:, 0:32], 1, 2), ALU.mult, ALU.mult)
                e2 = [*e0, dt_tok, v_a, *qk_tok.values(), *v_tok]
                ph3.close()
                nab = sb("nab", [128, 2, 2, 2, 256], F32, ph2)
                cap = sb("cap", [128, 256], F32, ph2)
                a0 = CST["cap"][0]
                t_cap = load("sp", "cst", cap[:, :], cst_in[:, a0:a0 + 256], e2)

                nab_added = {}

                def nabias(i, t, P, S, after):
                    s = i % 2
                    if t == 0:
                        for r in range(4):
                            for j in range(4):
                                off = 2 * i * 465 + (j - r + 7) * 31 - 48
                                src = bass.AP(tensor=rpb_in.tensor, offset=off, ap=[[1, 64], [465, 2], [1, 64]])
                                dst = nab[64 * (r % 2):64 * (r % 2) + 64, s, r // 2, :, 64 * j:64 * j + 64]
                                nab_tok[i] = load("sp", f"nab{s}", dst, src, [*e2, *nab_added.get(i - 2, ())])
                    B = nab[:, s, t, :, :]
                    rev = bass.AP(tensor=B.tensor, offset=B.offset + 63, ap=[list(B.ap[0]), [64, 8], [-1, 64]])
                    c8 = bass.AP(tensor=cap, offset=0, ap=[list(cap[:, :].ap[0]), [0, 2], [1, 256]])
                    P8 = P.rearrange("p h (j c) -> p (h j) c", c=64)
                    v = V([*after, nab_tok[i], t_cap], TT, P8, rev, bass.AP(tensor=cap, offset=0, ap=[list(cap[:, :].ap[0]), [0, 8], [1, 64]]), ALU.min)
                    v = V([v], TT, P, P, S, ALU.add)
                    nab_added[i] = [v]
                    return v

                nab_tok = {}
                o_tok = attention("n", ph2, 4, 64, [256, 256],
                                  lambda h, t: (qTn[64 * (h % 2):64 * (h % 2) + 64, h // 2, 128 * t:128 * t + 128], [qk_tok["naq", t]]),
                                  lambda h, n: (kTn[64 * (h % 2):64 * (h % 2) + 64, h // 2, 0:n], [qk_tok["nak", 0], qk_tok["nak", 1]]),
                                  lambda h, kk: vn[:, kk, 64 * h:64 * h + 64], v_tok, nabias, (oTh, oTl), e2)
            e1 = [o_tok[-1], ("act", counts["act"]), ("dve", counts["dve"]), ("pe", counts["pe"])]
            zs = sb("zs", [128, 2, D], F32, ph)
            z_tok = [[], []]
            for j in range(2):
                p = take(2)
                for t in range(2):
                    gt = project(p, t, 4 + t, xT, ready)
                    z = A([gt, *e1], zs[:, t, 512 * j:512 * j + 512], bank(4 + t), ACT.Silu)
                    emptied[4 + t] = [z]
                    z_tok[t].append(z)
            xT_multiplied[0] = [gt]
            xd = sb("xd", [128, 2, 2, D], F32, ph)
            cb = sb("cbm", [128, 2, 4, 256], F32, ph)
            m2 = sb("m2", [128, 8, 128], F32, ph)
            tri = sb("tri", [128, 5, 128], F32, ph)
            a0 = CST["tf"][0]
            t_tri = load("sp", "cst", tri[:, :, :], cst_in[:, a0:a0 + 640].rearrange("p (a n) -> p a n", a=5), e1)
            TF, TB, ON, MF, MB = (tri[:, i, :] for i in range(5))
            xs_tok = []
            for t in range(2):
                for b in range(2):
                    tr = transposed(lambda k: xc[:, 4 * b + k, 128 * t:128 * t + 128], 4, 6 + b, [xc_tok[4 * b + k] for k in range(4)])
                    e = A([tr, *xn_turned[t]], xn[:, t, 512 * b:512 * b + 512], bank(6 + b), ACT.Copy)
                    emptied[6 + b] = [e]
                xs_tok.append(e)
            xd_tok = {}
            for t in range(2):
                for r in range(2):
                    xd_tok[r, t] = V([xs_tok[t], v_dt, *e1], TT, xd[:, r, t, :].rearrange("p (h d) -> p h d", d=64),
                                     xn[:, t, :].rearrange("p (h d) -> p h d", d=64),
                                     spread(d3[0][:, t, 16 * r:16 * r + 16], 2, 64), ALU.mult)
            for s in range(2):
                after_emptied(4 + 0, 5)
                wait("pe", *[xc_tok[c] for c in range(8, 16)])
                for g in range(4):
                    m = MM(bank(4 + g // 2)[:, 256 * (g % 2):256 * (g % 2) + 256], xc[:, 8 + g, 128 * s:128 * s + 128],
                           xc[:, 12 + g, :], True, True)
                tok = done(m)
                cb_tok = A([tok, *e1], cb[:, s, :, :], bank(4, 2).rearrange("p (g n) -> p g n", g=4), ACT.Copy)
                emptied[4] = emptied[5] = [cb_tok]
            after_emptied(6)
            wait("pe", t_tri, v_a)
            av = d3[1]
            for r in range(2):
                T = (TF, TB)[r]
                for s in range(2):
                    o = bank(6)[:, 32 * r + 16 * s:32 * r + 16 * s + 16]
                    near = s != r
                    m = MM(o, T, av[:, s, 16 * r:16 * r + 16], True, not near)
                    if near:
                        m = MM(o, ON, av[:, 1 - s, 16 * r:16 * r + 16], False, True)
            tok = done(m)
            t_nac = V([tok, *e1], TS, nac[:, :], bank(6)[:, 0:64], -1.0, None, ALU.mult)
            emptied[6] = [t_nac]
            Mx = [xc[:, 0:4, :].rearrange("p c (u n) -> p (c u) n", u=2), xc[:, 4:8, :].rearrange("p c (u n) -> p (c u) n", u=2),
                  m2[:, :, :]]
            mx_multiplied = {i: [] for i in range(3)}
            sn, snt, sni = gain("ssdnorm")
            Dk = small[:, SMALL["dskip"][0]:SMALL["dskip"][0] + 16]
            for l in range(2):
                blocks = [(0, 0), (1, 0), (1, 1)] if l == 0 else [(0, 0), (0, 1), (1, 1)]
                for hh in range(2):
                    m_tok = []
                    for i, (r, s) in enumerate(blocks):
                        T, msk = (TF, TB)[r], (MF, MB)[r]
                        cross = l != r
                        for b in range(2):
                            bk = 2 * (i % 2) + b
                            after_emptied(bk)
                            if s == l:
                                MM(bank(bk), ident[:, :], spread(msk, 1, 4), True, False)
                            for h in range(4):
                                hd = 8 * hh + 4 * b + h
                                o = bank(bk)[:, 128 * h:128 * h + 128]
                                ends = s != l or h == 3
                                m = MM(o, spread(av[:, l, 16 * r + hd], 1, 128), T, s != l, not cross and ends)
                                if cross:
                                    m = MM(o, spread(av[:, 1 - l, 16 * r + hd], 1, 128), ON, False, ends)
                            tok = done(m)
                            for h in range(4):
                                hd = 8 * hh + 4 * b + h
                                e = A([tok, t_nac, *mx_multiplied[i], *xs_tok, *e1], Mx[i][:, 4 * b + h, :], bank(bk)[:, 128 * h:128 * h + 128],
                                      ACT.Exp, bias=nac[:, 32 * r + 16 * s + hd:32 * r + 16 * s + hd + 1])
                            emptied[bk] = [e]
                        m4 = Mx[i].rearrange("p (g r) n -> p g r n", g=2)
                        m_tok.append(V([e, cb_tok], TT, m4, m4, spread(cb[:, s, 2 * hh:2 * hh + 2, 128 * l:128 * l + 128], 2, 4), ALU.mult))
                    after_emptied(4 + hh)
                    wait("pe", *m_tok, *[xd_tok[k] for k in xd_tok])
                    for h in range(8):
                        hd = 8 * hh + h
                        for i, (r, s) in enumerate(blocks):
                            m = MM(bank(4 + hh)[:, 64 * h:64 * h + 64], Mx[i][:, h, :], xd[:, r, s, 64 * hd:64 * hd + 64], i == 0, i == 2)
                    y_tok = done(m)
                    mx_multiplied = {i: [y_tok] for i in range(3)}
                ya = tmp[:, :]
                y3 = ya.rearrange("p (h d) -> p h d", d=64)
                v = V([xs_tok[l], *tmp_added[0]], TT, y3, xn[:, l, :].rearrange("p (h d) -> p h d", d=64), spread(Dk, 2, 64), ALU.mult)
                v = V([v, y_tok], TT, ya, ya, bank(4, 2), ALU.add)
                emptied[4] = emptied[5] = [v]
                v = V([v, *z_tok[l]], TT, ya, ya, zs[:, l, :], ALU.mult)
                ss = stat(4)
                for g in range(4):
                    a = A([v], xn[:, l, 256 * g:256 * g + 256], ya[:, 256 * g:256 * g + 256], ACT.Square, accum_out=ss[:, g:g + 1])
                g, rr = rstd(a, ss, 1.0 / 256, 1e-6, 4)
                v = V([g], TT, ya.rearrange("p (g d) -> p g d", g=4), ya.rearrange("p (g d) -> p g d", g=4), spread(rr, 2, 256), ALU.mult)
                v = V([v, snt], TT, xn[:, l, :], ya, sn, ALU.mult)
                tmp_added[0] = [v]
                gain_applied[sni] = [v]
                tr, ready[l] = flip(l, xn[:, l, :], v, xT, xT_multiplied[0])
                xn_turned[l] = [tr]
            last = [None, None]
            p = take(2)
            for q in range(2):
                for t in range(2):
                    down(p + q, t, lambda k: (oTh[:, 2 * q + k, t, :], oTl[:, 2 * q + k, t, :]), q == 0, False, o_tok)
            p = take(4)
            for t in range(2):
                for q in range(4):
                    last[t] = down(p + q, t, lambda k: (xTh[:, 2 * q + k, t, :], xTl[:, 2 * q + k, t, :]), False,
                                   q == 3, ready[t])
            xT_multiplied[0] = [last[1]]
        flow(last, None, False, "ffn0", None)
        if stop == "even":
            return write_out()
        last = ffn("e", bounds())
        flow(last, None, False, "oddmix", None)
        if stop == "ffn20":
            return write_out()

        ph = ExitStack()
        with ph:
            e0 = bounds()
            qg = sb("qg", [128, 2, D], F32, ph)
            qTg = sb("qTg", [128, 8, 256], F32, ph)
            kd = sb("kd", [128, 2, 4, 2, 64], F32, ph)
            kTg = sb("kTg", [128, 4, 256], F32, ph)
            vg = sb("vg", [128, 2, 256], F32, ph)
            kg = sb("kg", [128, 2, 256], F32, ph)
            sq = sb("sqg", [128, 512], F32, ph)
            r1 = sb("r1", [128, 512], F32, ph)
            r2 = sb("r2", [128, 512], F32, ph)
            cs = sb("cs", [128, 2, 2, 64], F32, ph)
            a0 = CST["cos"][0]
            t_cs = load("sp", "cst", cs[:, :, :, :], cst_in[:, a0:a0 + 256].rearrange("p (a t n) -> p a t n", a=2, t=2), e0)
            sq_summed = []
            rf = [[]]

            def rope(src, n, t, dst, tok):
                a, b = r1[:, 0:64 * n].rearrange("p (h d) -> p h d", d=64), r2[:, 0:64 * n].rearrange("p (h d) -> p h d", d=64)
                v1 = V([tok, t_cs, *rf[0], *e0], TT, a, src, spread(cs[:, 0, t, :], 1, n), ALU.mult)
                sw = bass.AP(tensor=src.tensor, offset=src.offset + 1, ap=[list(src.ap[0]), [2, 32 * n], [-1, 2]])
                sn_ = cs[:, 1, t, :]
                b4 = r2[:, 0:64 * n].rearrange("p (m u) -> p m u", u=2)
                v2 = V([], nc.vector.tensor_copy, b4, sw)
                v2 = V([v2], TT, b, b, spread(sn_, 1, n), ALU.mult)
                for dd in dst:
                    v = V([v1, v2], TT, dd, a, b, ALU.add)
                rf[0] = [v]
                return v

            qg_tok = {}
            for j in range(2):
                p = take(2)
                for t in range(2):
                    gt = project(p, t, 4 + t, xT, ready)
                    dst = qg[:, t, 512 * j:512 * j + 512].rearrange("p (h d) -> p h d", d=64)
                    v1, v2, s = head_norm("gq", bank(4 + t), 8, "gq", dst, gt, e0, 1.0, 64e-6, sq, [*sq_summed, *e0])
                    sq_summed = [s]
                    emptied[4 + t] = [v1]
                    v = rope(dst, 8, t, [dst], v2)
                    tr = transposed(lambda k: qg[:, t, 512 * j + 128 * k:512 * j + 128 * k + 128], 4, 6 + t, [v])
                    e = A([tr, *e0], qTg[:, 4 * j:4 * j + 4, 128 * t:128 * t + 128], bank(6 + t).rearrange("p (k n) -> p k n", k=4), ACT.Copy)
                    emptied[6 + t] = [e]
                    qg_tok[j, t] = e
            p = take(2)
            kg_tok, v_tok = [], []
            for t in range(2):
                gt = project(p, t, 4 + t, xT, ready)
                b = bank(4 + t)
                dst = kg[:, t, :].rearrange("p (h d) -> p h d", d=64)
                v1, v2, s = head_norm("gk", b[:, 0:256], 4, "gk", dst, gt, e0, 1.0 / 64, 1e-6, sq, [*sq_summed, *e0])
                sq_summed = [s]
                a = A([v1, *e0], vg[:, t, :], b[:, 256:512], ACT.Copy)
                v_tok.append(a)
                emptied[4 + t] = [a]
                v = rope(dst, 4, t, [kd[:, t, :, 0, :], kd[:, t, :, 1, :]], v2)
                tr = transposed(lambda k: kd[:, t, k, :, :].rearrange("p a d -> p (a d)"), 4, 6 + t, [v])
                e = A([tr, *e0], kTg[:, :, 128 * t:128 * t + 128], bank(6 + t).rearrange("p (k n) -> p k n", k=4), ACT.Copy)
                emptied[6 + t] = [e]
                kg_tok.append(e)
            xT_multiplied[0] = [gt]

            def plain(i, t, P, S, after):
                return V(after, nc.vector.tensor_copy, P, S)

            o_tok = attention("g", ph, 8, 64, [256, 256],
                              lambda h, t: (qTg[64 * (h % 2):64 * (h % 2) + 64, h // 2, 128 * t:128 * t + 128], [qg_tok[h // 8, t]]),
                              lambda h, n: (kTg[64 * (h % 2):64 * (h % 2) + 64, h // 4, 0:n], kg_tok),
                              lambda h, kk: vg[:, kk, 64 * (h // 4):64 * (h // 4) + 64], v_tok, plain, xT, e0)
            p = take(4)
            last = [None, None]
            for t in range(2):
                for q in range(4):
                    last[t] = down(p + q, t, lambda k: (xTh[:, 2 * q + k, t, :], xTl[:, 2 * q + k, t, :]), q == 0,
                                   q == 3, o_tok)
            xT_multiplied[0] = [last[1]]
        flow(last, None, False, "ffn1", None)
        if stop == "odd":
            return write_out()
        last = ffn("f", bounds())
        flow(last, None, False, None, None)
        assert piece[0] == n_pieces, (piece[0], n_pieces)
        write_out()


def kernel(**inputs):
    import concourse.bacc as bacc
    from concourse.bass_utils import run_bass_kernel_spmd as run

    i = {k: np.asarray(v) for k, v in inputs.items()}
    arrays = {
        "in_x": np.ascontiguousarray(i["x"].reshape(256, D)),
        "in_w": np.ascontiguousarray(pack_stream(i)),
        "in_rows": np.ascontiguousarray(pack_rows(i)),
        "in_small": np.ascontiguousarray(pack_small(i)),
        "in_cols": np.ascontiguousarray(pack_cols(i)),
        "in_bias": np.ascontiguousarray(pack_bias(i)),
        "in_rpb": np.ascontiguousarray(i["na_rel_bias_2"][0][:, :, ::-1].reshape(-1)),
        "in_cst": constants(),
    }
    nc = bacc.Bacc("TRN2", target_bir_lowering=False, num_devices=1, dynamic_dma_scratch_size=1024)
    args = [nc.dram_tensor(k, a.shape, mybir.dt.from_np(a.dtype), kind="ExternalInput").ap() for k, a in arrays.items()]
    out = nc.dram_tensor("out_x", (256, D), F32, kind="ExternalOutput").ap()
    build(nc, *args, out)
    r = run(nc, [arrays], core_ids=[0])
    return r.results[0]["out_x"].reshape(1, 256, D)
```

```python
from contextlib import ExitStack

import numpy as np

import concourse.bass as bass
from concourse import mybir

F32 = mybir.dt.float32
F32R = mybir.dt.float32r
ACT = mybir.ActivationFunctionType
ALU = mybir.AluOpType
AX = mybir.AxisListType

D = 1024
FF = 2816
NJ = FF // 256
RAW = 7
RING = 5
TAPS = 31
NGAIN = 3
BIG = 1.0e33
NEG = -1.0e30

GAINS = (["pre00", "post00", "mixpre0", "lng", "lnb", "mixpost0", "pre01", "post01", "pre10", "post10",
          "kv", "mixpre1", "mixpost1", "pre11", "post11", "evenmix", "ssdnorm", "ffn0", "oddmix", "ffn1"])

CST = {}
COLS = {}


def _layout(table, items):
    at = 0
    for name, n in items:
        table[name] = (at, n)
        at += n
    return at


N_CST = _layout(CST, [("ident", 128), ("tf", 128), ("tb", 128), ("ones", 128), ("mf", 128), ("mb", 128),
                      ("dm", 512), ("win", 128), ("cos", 128), ("sin", 128)])
N_KEEP = 128
N_COLS = _layout(COLS, [("dw", 8 * TAPS), ("dwb", 8), ("cw", 64), ("cb", 16), ("wdt", 256)])


def constants():
    c = np.zeros((128, N_CST), np.float32)

    def put(name, v):
        a, n = CST[name]
        c[:, a:a + n] = v.reshape(128, n)

    i = np.arange(128)
    put("ident", np.eye(128))
    put("tf", (i[:, None] <= i[None, :]))
    put("tb", (i[:, None] >= i[None, :]))
    put("ones", np.ones((128, 128)))
    put("mf", np.where(i[:, None] <= i[None, :], 0.0, NEG))
    put("mb", np.where(i[:, None] >= i[None, :], 0.0, NEG))
    q = i[:, None, None] + 128 * np.arange(2)[None, :, None]
    k = np.arange(256)[None, None, :]
    put("dm", np.where(k <= q, q - k, BIG))
    cq = i % 64
    st = np.clip(cq - 8, 0, 48)
    kc = np.arange(64)
    inside = (kc[None] >= st[:, None]) & (kc[None] < st[:, None] + 16)
    put("win", np.stack([inside, np.where(inside, 0.0, NEG)], axis=1))
    t = i[:, None] + 128 * np.arange(2)[None, :]
    freqs = (np.float32(10000.0) ** (-np.arange(0, 32, 2, dtype=np.float32) / np.float32(32))).astype(np.float32)
    ang = np.concatenate([(t // 64).astype(np.float32)[:, :, None] * freqs,
                          (t % 64).astype(np.float32)[:, :, None] * freqs], axis=-1)
    put("cos", np.repeat(np.cos(ang), 2, axis=-1))
    s = np.repeat(np.sin(ang), 2, axis=-1)
    s[:, :, 0::2] *= -1.0
    put("sin", s)
    return c


def pack_stream(i):
    out = []

    def cols(w, spans):
        w = np.concatenate([w[:, a:b] for a, b in spans], axis=1)
        v = w.reshape(2, 4, 128, 512).transpose(0, 2, 1, 3).reshape(2, 128, 2048)
        out.extend([v[0], v[1]])

    def rows(w, r0):
        out.append(w[r0:r0 + 256].reshape(2, 128, 1024).transpose(1, 0, 2).reshape(128, 2048))

    def ffn(wgu, wd):
        for j in range(NJ):
            cols(wgu, [(256 * j, 256 * j + 256), (FF + 256 * j, FF + 256 * j + 256)])
            if j:
                rows(wd, 256 * (j - 1))
        rows(wd, 256 * (NJ - 1))

    gu, dn = i["ffn_w_gate_up"], i["ffn_w_down"]
    ffn(gu[0, 0], dn[0, 0])
    for j in range(4):
        cols(i["conv_w_in"][0], [(256 * j, 256 * j + 256), (1024 + 256 * j, 1280 + 256 * j)])
    for j in range(4):
        rows(i["conv_w_out"][0], 256 * j)
    ffn(gu[0, 1], dn[0, 1])
    ffn(gu[1, 0], dn[1, 0])
    for j in (2, 3, 0, 1):
        cols(i["w_kv"], [(512 * j, 512 * j + 512)])
    for j in range(2):
        cols(i["attn_w_q"][0], [(512 * j, 512 * j + 512)])
    for j in range(4):
        rows(i["attn_w_o"][0], 256 * j)
    ffn(gu[1, 1], dn[1, 1])
    we = i["even_w_in_2"][0]
    for c in (0, 512, 2560, 3072, 3584, 4096, 1024, 1536, 2048):
        cols(we, [(c, c + 512)])
    for j in range(6):
        rows(i["even_w_out_2"][0], 256 * j)
    ffn(i["ffn_w13_2"][0], i["ffn_w2_2"][0])
    for j in range(3):
        cols(i["odd_w_qkv_2"][0], [(512 * j, 512 * j + 512)])
    for j in range(4):
        rows(i["odd_w_out_2"][0], 256 * j)
    ffn(i["ffn_w13_2"][1], i["ffn_w2_2"][1])
    return np.stack(out)


def pack_rows(i):
    a, b = i["ffn_norm_pre"], i["ffn_norm_post"]
    v = {"pre00": a[0, 0], "post00": b[0, 0], "pre01": a[0, 1], "post01": b[0, 1],
         "pre10": a[1, 0], "post10": b[1, 0], "pre11": a[1, 1], "post11": b[1, 1],
         "mixpre0": i["mix_norm_pre"][0], "mixpre1": i["mix_norm_pre"][1],
         "mixpost0": i["mix_norm_post"][0], "mixpost1": i["mix_norm_post"][1],
         "lng": i["conv_ln_g"][0], "lnb": i["conv_ln_b"][0], "kv": i["kv_norm"],
         "evenmix": i["even_mix_norm_2"][0], "ssdnorm": i["ssd_out_norm_2"][0],
         "ffn0": i["ffn_norm_2"][0], "ffn1": i["ffn_norm_2"][1], "oddmix": i["odd_mix_norm_2"][0]}
    return np.stack([v[n] for n in GAINS])


SMALL = {}
N_SMALL = _layout(SMALL, [("naq", 64), ("nak", 64), ("gq", 64), ("gk", 64), ("dtb", 32), ("alog", 32), ("dskip", 16)])


def pack_small(i):
    return np.concatenate([i["na_q_norm_2"][0], i["na_k_norm_2"][0], i["gqa_q_norm_2"][0], i["gqa_k_norm_2"][0],
                           i["ssd_dt_bias_2"][0].ravel(), i["ssd_A_log_2"][0].ravel(), i["ssd_D_2"][0]])[None]


def pack_cols(i):
    def tiles(v, n):
        return v.reshape(-1, n, 128).transpose(2, 1, 0).reshape(128, -1)

    wdt = i["even_w_in_2"][0][:, 4608:4640].reshape(8, 128, 32).transpose(1, 0, 2).reshape(128, 256)
    return np.concatenate([tiles(i["conv_w_dw"][0], 8), tiles(i["conv_b_dw"], 8), tiles(i["ssd_conv_w_2"][0], 16),
                           tiles(i["ssd_conv_b_2"], 16), wdt], axis=1)


def pack_bias(i):
    return np.concatenate([i["conv_b_in"][0].reshape(2, 4, 256).transpose(1, 0, 2).ravel(), i["conv_b_out"][0]])[None]


def build(nc, x_in, w_in, rows_in, small_in, cols_in, bias_in, rpb_in, cst_in, out, stop=None):
    ctx = ExitStack()
    with ctx:
        def sb(name, shape, dt=F32, stack=ctx):
            return stack.enter_context(nc.sbuf_tensor(name, shape, dt))

        sems = {}
        counts = {}

        def sem(key):
            sems[key] = ctx.enter_context(nc.semaphore("s_" + key))
            counts[key] = 0
            return key

        engines = {"pe": nc.tensor, "act": nc.scalar, "dve": nc.vector, "pool": nc.gpsimd, "sp": nc.sync}
        for e in ("pe", "act", "dve", "pool"):
            sem(e)
        passed = {e: {} for e in engines}

        def wait(e, *toks):
            for tok in toks:
                if tok is None:
                    continue
                key, n = tok
                if passed[e].get(key, 0) < n:
                    engines[e].wait_ge(sems[key], n)
                    passed[e][key] = n

        def signal(key, ins, n=1):
            counts[key] += n
            ins.then_inc(sems[key], n)
            return (key, counts[key])

        def A(after, out_, in_, func, **kw):
            wait("act", *after)
            return signal("act", nc.scalar.activation(out_, in_, func, **kw))

        def V(after, op, *a, **kw):
            wait("dve", *after)
            return signal("dve", op(*a, **kw))

        def G(after, op, *a, **kw):
            wait("pool", *after)
            return signal("pool", op(*a, **kw))

        TT, TS, STT = nc.vector.tensor_tensor, nc.vector.tensor_scalar, nc.vector.scalar_tensor_tensor

        def load(e, key, dst, src, after=()):
            wait(e, *after)
            return signal(key, engines[e].dma_start(dst, src), 16)

        def MM(o, l, r, start, stop, skip=False):
            return nc.tensor.matmul(o, l, r, start=start, stop=stop, skip_group_check=skip)

        def mm3(o, lh, ll, rh, rl, start, stop):
            MM(o, lh, rh, start, False)
            MM(o, lh, rl, False, False)
            return MM(o, ll, rh, False, stop)

        def done(ins):
            return signal("pe", ins)

        def spread(ap, at, n):
            dims = [list(d) for d in ap.ap]
            return bass.AP(tensor=ap.tensor, offset=ap.offset, ap=dims[:at] + [[0, n]] + dims[at:])

        ps = ctx.enter_context(nc.psum_tensor("ps", [128, 4096], F32))
        emptied = {b: [] for b in range(8)}

        def bank(b, n=1):
            return ps[:, 512 * b:512 * (b + n)]

        def after_emptied(*bs):
            for b in bs:
                wait("pe", *emptied[b])
                emptied[b] = []

        with ExitStack() as same:
            raw = sb("raw", [128, RAW, 2048], F32, same)
        wl = sb("wl", [128, RAW, 2048], F32R)
        wh = sb("wh", [128, RING, 2048], F32R)
        x = sb("x", [128, 2, D])
        xTh = sb("xTh", [128, 8, 2, 128], F32R)
        xTl = sb("xTl", [128, 8, 2, 128], F32R)
        gains = sb("gains", [128, NGAIN, D])
        xn = sb("xn", [128, 2, D])
        tmp = sb("tmp", [128, D])
        ident = sb("ident", [128, 128])
        cols = sb("cols", [128, N_COLS])
        small = sb("small", [128, N_SMALL])
        st = sb("st", [128, 512])
        mhalf = sb("mhalf", [128, 8])
        ones1 = sb("ones1", [1, 128])

        for n in range(RAW):
            sem(f"raw{n}")
        for n in range(NGAIN):
            sem(f"gain{n}")
        for n in ("x0", "x1", "ident", "cols", "small", "bias", "cst", "out", "nab0", "nab1"):
            sem(n)

        at = [0]

        def stat(n=1):
            a = at[0]
            at[0] += n
            assert at[0] <= 512
            return st[:, a:a + n]

        t_half = G([], nc.gpsimd.memset, mhalf[:, :], -0.5)
        t_one = G([], nc.gpsimd.memset, ones1[:, :], 1.0)
        x_v = x_in.rearrange("(t p) d -> p t d", p=128)
        t_x = [load("act", f"x{t}", x[:, t, :], x_v[:, t, :]) for t in range(2)]
        t_ident = load("act", "ident", ident[:, :], cst_in[:, 0:128])
        t_cols = load("act", "cols", cols[:, :], cols_in)

        n_pieces = w_in.shape[0]
        fetched, landed, split_done, multiplied = [0], {}, {}, {}

        def fetch():
            while fetched[0] < n_pieces and (fetched[0] < RAW or fetched[0] - RAW in multiplied):
                p = fetched[0]
                after = [multiplied[p - RAW]] if p >= RAW else []
                landed[p] = load("sp", f"raw{p % RAW}", raw[:, p % RAW, :], w_in[p], after)
                fetched[0] += 1

        n_split = [0]

        def split():
            p = n_split[0]
            fetch()
            piece_in, hi = raw[:, p % RAW, :], wh[:, p % RING, :]
            after = [multiplied[p - RING]] if p >= RING else []
            h = A([landed[p], *after], hi, piece_in, ACT.Copy)
            split_done[p] = V([h], TT, wl[:, p % RAW, :], piece_in, hi.bitcast(F32), ALU.subtract)
            n_split[0] += 1

        def top_up(n=RING):
            fetch()
            while n and n_split[0] in landed and (n_split[0] < RING or n_split[0] - RING in multiplied):
                split()
                n -= 1

        t_small = load("sp", "small", small[:, :], spread(small_in[0, :], 0, 128))

        g_at, g_tok, gain_applied = [0], {}, {}

        def gain_to(n):
            while g_at[0] < min(n, len(GAINS)):
                i = g_at[0]
                after = gain_applied[i - NGAIN] if i >= NGAIN else []
                g_tok[i] = load("sp", f"gain{i % NGAIN}", gains[:, i % NGAIN, :], spread(rows_in[i, :], 0, 128), after)
                g_at[0] += 1

        def gain(name):
            i = GAINS.index(name)
            return gains[:, i % NGAIN, :], g_tok[i], i

        def gain_next():
            while g_at[0] < len(GAINS) and g_at[0] - NGAIN in gain_applied:
                gain_to(g_at[0] + 1)

        gain_to(1)
        fetch()
        gain_to(NGAIN)
        piece = [0]

        def take(n):
            p = piece[0]
            piece[0] += n
            while n_split[0] < p + n:
                split()
            return p

        def parts(p, k):
            return (wh[:, p % RING, :].rearrange("p (k n) -> p k n", k=k),
                    wl[:, p % RAW, :].rearrange("p (k n) -> p k n", k=k))

        def wcols(p):
            return parts(p, 4)

        def wrows(p):
            return parts(p, 2)

        def project(p, t, b, act, act_tok, bias=None, mid=None):
            wait("pe", *act_tok[t])
            after_emptied(b)
            if bias is not None:
                MM(bank(b), ones1[0:1, :], bias, True, False)
            for half in range(2):
                wait("pe", split_done[p + half])
                H, L = wcols(p + half)
                for k in range(4):
                    kk = 4 * half + k
                    last = mm3(bank(b), act[0][:, kk, t, :], act[1][:, kk, t, :], H[:, k, :], L[:, k, :],
                               kk == 0 and bias is None, kk == 7)
                tok = done(last)
                if t == 1:
                    multiplied[p + half] = tok
                if half == 0 and mid:
                    mid()
                    wait("pe", *act_tok[t])
            return tok

        def project_t(p, act, act_tok, b0):
            wait("pe", *act_tok[0], *act_tok[1], split_done[p], split_done[p + 1])
            toks = []
            for n in range(4):
                b = b0 + n // 2
                if n % 2 == 0:
                    after_emptied(b)
                o = bank(b)[:, 256 * (n % 2):256 * (n % 2) + 256]
                for kk in range(8):
                    H, L = wcols(p + kk // 4)
                    a, c = H[:, kk % 4, 128 * n:128 * n + 128], L[:, kk % 4, 128 * n:128 * n + 128]
                    MM(o, a, act[0][:, kk, :, :], kk == 0, False)
                    MM(o, c, act[0][:, kk, :, :], False, False)
                    last = MM(o, a, act[1][:, kk, :, :], False, kk == 7)
                if n % 2 == 1:
                    toks.append(done(last))
            multiplied[p] = multiplied[p + 1] = toks[1]
            return toks

        def down(p, t, lhs, first, last_, toks=()):
            wait("pe", split_done[p], *toks)
            if first:
                after_emptied(2 * t, 2 * t + 1)
            H, L = wrows(p)
            for k in range(2):
                for half in range(2):
                    r = slice(512 * half, 512 * half + 512)
                    m = mm3(bank(2 * t + half), lhs(k)[0], lhs(k)[1], H[:, k, r], L[:, k, r],
                            first and k == 0, last_ and k == 1)
            tok = done(m)
            if t == 1:
                multiplied[p] = tok
            return tok

        x_tok = list(t_x)
        xn_turned = [[], []]
        tmp_added = [[]]

        def rstd(tok, ss, mul, add, n=1):
            v, r = stat(n), stat(n)
            g = G([tok], nc.gpsimd.tensor_scalar, v, ss, mul, add, ALU.mult, ALU.add)
            return G([g, t_half], nc.gpsimd.tensor_tensor, r, v, mhalf[:, 0:n], ALU.pow), r

        def post(t, tok, name, half):
            a = bank(2 * t, 2)
            if name is None:
                x_tok[t] = V([tok, x_tok[t]], TT, x[:, t, :], x[:, t, :], a, ALU.add)
                emptied[2 * t] = emptied[2 * t + 1] = [x_tok[t]]
                return
            ss = stat()
            s = A([tok, *tmp_added[0]], tmp[:, :], a, ACT.Square, accum_out=ss)
            m = 4.0 if half else 1.0
            g, r = rstd(s, ss, m / D, m * 1e-6)
            ga, gt, gi = gain(name)
            v = V([g, gt] + tmp_added[0], STT, tmp[:, :], a, r, ga, ALU.mult, ALU.mult)
            emptied[2 * t] = emptied[2 * t + 1] = [v]
            gain_applied[gi] = [v]
            x_tok[t] = V([v, x_tok[t]], TT, x[:, t, :], x[:, t, :], tmp[:, :], ALU.add)
            tmp_added[0] = [x_tok[t]]

        def transposed(src, n, b, after):
            wait("pe", t_ident, *after)
            after_emptied(b)
            for k in range(n):
                m = nc.tensor.transpose(bank(b)[:, 128 * k:128 * k + 128], src(k), ident[:, :])
            return done(m)

        def hilo(b, src, dh, dl, tok, after=()):
            h = A([tok, *after], dh, src, ACT.Copy)
            v = V([h], TT, dl, src, dh.bitcast(F32), ALU.subtract)
            emptied[b] = [v]
            return v

        def flip(t, src, tok, act, after=()):
            toks = []
            for b in range(2):
                tr = transposed(lambda k: src[:, 512 * b + 128 * k:512 * b + 128 * k + 128], 4, 6 + b, [tok])
                s = bank(6 + b).rearrange("p (k n) -> p k n", k=4)
                toks.append(hilo(6 + b, s, act[0][:, 4 * b:4 * b + 4, t, :], act[1][:, 4 * b:4 * b + 4, t, :], tr, after))
            return tr, toks

        def norm_stat(t):
            ss = stat()
            s = A([x_tok[t], *xn_turned[t]], xn[:, t, :], x[:, t, :], ACT.Square, accum_out=ss)
            return rstd(s, ss, 1.0 / D, 1e-6)

        xn_ready = [None, None]
        x_stats = [None, None]

        def pre_scale(t, name, stats=None):
            g, rs = stats or norm_stat(t)
            x_stats[t] = (g, rs)
            ga, gt, gi = gain(name)
            xn_ready[t] = V([g, gt, x_tok[t]] + xn_turned[t], STT, xn[:, t, :], x[:, t, :], rs, ga, ALU.mult, ALU.mult)
            gain_applied[gi] = [xn_ready[t]]

        def pre_turn(t, act, after=()):
            tr, toks = flip(t, xn[:, t, :], xn_ready[t], act, after)
            xn_turned[t] = [tr]
            return toks

        xT = (xTh, xTl)
        ready = [None, None]
        xT_multiplied = [[]]

        def ffn(tag, ph_w, post_name, half, pre_name):
            ph = ExitStack()
            with ph:
                hTh = sb(f"hTh{tag}", [128, 2, 2, 2, 128], F32R, ph)
                hTl = sb(f"hTl{tag}", [128, 2, 2, 2, 128], F32R, ph)
                sg = sb(f"sg{tag}", [128, 2, 2, 256], F32, ph)
                hb = sb(f"hb{tag}", [128, 2, 2, 256], F32, ph)
                hT_multiplied, hb_turned, h_tok, hT_tok = {}, {}, {}, {}

                def act_of(j, t, b, tok):
                    a = bank(b)
                    s = A([tok, *hb_turned.get((j - 2, t), ()), *ph_w], sg[:, j % 2, t, :], a[:, 0:256], ACT.Silu)
                    h_tok[j, t] = V([s], TT, hb[:, j % 2, t, :], sg[:, j % 2, t, :], a[:, 256:512], ALU.mult)
                    emptied[b] = [h_tok[j, t]]

                def turn(j, ts):
                    b = 6 + (j + ts[0]) % 2
                    after_emptied(b)
                    wait("pe", t_ident, *[h_tok[j, t] for t in ts])
                    for ft in range(2):
                        for t in ts:
                            m = nc.tensor.transpose(bank(b)[:, 256 * ft + 128 * t:256 * ft + 128 * t + 128],
                                                    hb[:, j % 2, t, 128 * ft:128 * ft + 128], ident[:, :])
                    tr = done(m)
                    for t in ts:
                        hb_turned[j, t] = [tr]
                    u = slice(ts[0], ts[-1] + 1)
                    src = bank(b).rearrange("p (f t n) -> p f t n", f=2, t=2)[:, :, u, :]
                    v = hilo(b, src, hTh[:, j % 2, :, u, :], hTl[:, j % 2, :, u, :], tr, hT_multiplied.get(j - 2, ()))
                    for t in ts:
                        hT_tok[j, t] = v

                def dn(j, p, t):
                    tok = down(p, t, lambda k: (hTh[:, j % 2, k, t, :], hTl[:, j % 2, k, t, :]), j == 0,
                               j == NJ - 1, [hT_tok[j, t]])
                    if t == 1:
                        hT_multiplied[j] = [tok]
                    return tok

                pair(xT, ready, turn1, act_of, lambda: turn(0, [0, 1]))
                q = take(1)
                dn(0, q, 0)
                turn(1, [0, 1])
                dn(0, q, 1)
                for j in range(2, NJ - 1):
                    p = take(2)
                    for t in range(2):
                        act_of(j, t, 4 + t, project(p, t, 4 + t, xT, ready))
                    top_up(2)
                    q = take(1)
                    dn(j - 1, q, 0)
                    turn(j, [0, 1])
                    dn(j - 1, q, 1)
                    top_up(1)
                j = NJ - 1
                p = take(4)

                def close(t):
                    tok = project(p, t, 4 + t, xT, ready)
                    act_of(j, t, 4 + t, tok)
                    if t == 1:
                        xT_multiplied[0] = [tok]
                    dn(j - 1, p + 2, t)
                    turn(j, [t])
                    top_up(1)
                    return dn(j, p + 3, t)

                seam(close, post_name, half, pre_name)

        def seam(close, post_name, half, pre_name):
            for t in range(2):
                tok = close(t)
                if t == 1 and pre_name:
                    ready[0] = pre_turn(0, xT, xT_multiplied[0])
                    top_up(1)
                post(t, tok, post_name, half)
                if t == 1:
                    top_up(1)
                if pre_name:
                    pre_scale(t, pre_name)
            gain_next()

        def turn1():
            ready[1] = pre_turn(1, xT, xT_multiplied[0])

        def pair(act, act_ready, between, taken, later=None, bias=None, fresh=2):
            p = take(2)
            for t in range(2):
                for j in range(2):
                    if t == 0 and j == 1:
                        take(2)
                    b = 4 * (1 - t) + j
                    tok = project(p + 2 * j, t, b, act, act_ready, bias(j) if bias else None,
                                  (between, later)[t] if j else None)
                    taken(j, t, b, tok)
                    top_up(fresh)

        def write_out():
            for t in range(2):
                tk = load("sp", "out", out.rearrange("(t p) d -> p t d", p=128)[:, t, :], x[:, t, :], [x_tok[t]])
            wait("sp", tk)
            for key in counts:
                if counts[key]:
                    wait("sp", (key, counts[key]))

        def bounds():
            return list(ready[0])

        for t in range(2):
            pre_scale(t, "pre00")
            top_up(1)
        ready[0] = pre_turn(0, xT)
        ph0 = ExitStack()
        ctx.enter_context(ph0)
        brow = sb("brow", [1, 3072], F32, ph0)
        t_b = load("act", "bias", brow[:, :], bias_in)
        ffn("a", [], "post00", True, "mixpre0")
        if stop == "ffn0":
            return write_out()

        ph = ExitStack()
        with ph:
            PADL = TAPS - 1
            W = PADL + 256
            uT = sb("uT", [128, 8, W], F32, ph)
            ca = sb("ca", [128, 8, 256], F32, ph)
            sg = sb("csg", [128, 2, 2, 256], F32, ph)
            ub = sb("cub", [128, 2, 2, 256], F32, ph)
            ya = sb("ya", [128, 2, D], F32, ph)
            e0 = bounds()
            t_z = G(e0, nc.gpsimd.memset, uT[:, :, 0:PADL], 0.0)
            wait("pe", t_b, t_one)
            ub_turned = {}
            dw0, dwb = COLS["dw"][0], COLS["dwb"][0]
            ca_tok = {}

            diag = sb("cdg", [128, 8, 128], F32, ph)
            odd = sb("cod", [128, 256], F32, ph)
            prod = sb("cpr", [128, 2, 256], F32, ph)
            odd_added, diag_multiplied = [[]], {}
            taps, u_turned, n_diag = [], {}, [0]

            def tap_column(c, k):
                return cols[:, dw0 + TAPS * c + k:dw0 + TAPS * c + k + 1]

            def vector_tap(c, k, sums):
                if k == TAPS:
                    ca_tok[c] = V([sums[0], sums[1]], TT, ca[:, c, :], ca[:, c, :], odd[:, :], ALU.add)
                    odd_added[0] = [ca_tok[c]]
                    return
                src, dst = uT[:, c, k:k + 256], (ca[:, c, :], odd[:, :])[k % 2]
                first = [t_z, t_cols, *e0, u_turned[c // 2]]
                if k == 0:
                    v = V(first, TS, dst, src, tap_column(c, k), cols[:, dwb + c:dwb + c + 1], ALU.mult, ALU.add)
                elif k == 1:
                    v = V([*first, *odd_added[0]], TS, dst, src, tap_column(c, k), None, ALU.mult)
                else:
                    v = V([sums[k % 2]], STT, dst, src, tap_column(c, k), dst, ALU.mult, ALU.add)
                sums[k % 2] = v

            def tap_some(n):
                for args in taps[:n]:
                    vector_tap(*args)
                del taps[:n]

            def conv_pool(c):
                first, added = [t_z, t_cols, *e0, u_turned[c // 2]], {}
                for k in range(TAPS):
                    src = uT[:, c, k:k + 256]
                    if k == 0:
                        g = G(first, nc.gpsimd.tensor_scalar, ca[:, c, :], src, tap_column(c, k),
                              cols[:, dwb + c:dwb + c + 1], ALU.mult, ALU.add)
                    else:
                        m = G([*first, *added.get(k - 2, ())], nc.gpsimd.tensor_scalar, prod[:, k % 2, :], src,
                              tap_column(c, k), None, ALU.mult)
                        g = G([m, g], nc.gpsimd.tensor_tensor, ca[:, c, :], ca[:, c, :], prod[:, k % 2, :], ALU.add)
                        added[k] = [g]
                ca_tok[c] = g

            def conv_diagonal(c):
                b = 2 + c // 2 % 2
                after_emptied(b)
                wait("pe", t_z, u_turned[c // 2])
                for k in range(TAPS):
                    n = n_diag[0]
                    n_diag[0] += 1
                    d = A([t_ident, t_cols, *e0, *diag_multiplied.get(n - 8, ())], diag[:, n % 8, :], ident[:, :],
                          ACT.Copy, scale=tap_column(c, k))
                    wait("pe", d)
                    tok = done(MM(bank(b)[:, 0:256], diag[:, n % 8, :], uT[:, c, k:k + 256], k == 0, k == TAPS - 1))
                    diag_multiplied[n] = [tok]
                ca_tok[c] = A([tok], ca[:, c, :], bank(b)[:, 0:256], ACT.Identity, bias=cols[:, dwb + c:dwb + c + 1])
                emptied[b] = [ca_tok[c]]

            def conv_part(j, e):
                u_turned[j] = e
                sums = [None, None]
                taps.extend((2 * j, k, sums) for k in range(TAPS + 1))
                if j == 0:
                    conv_pool(1)
                else:
                    conv_diagonal(2 * j + 1)

            u_tok = {}

            def glu(j, t, b, tok):
                a = bank(b)
                s = A([tok, *ub_turned.get((j - 2, t), ()), *e0], sg[:, j % 2, t, :], a[:, 256:512], ACT.Sigmoid)
                u_tok[j, t] = V([s], TT, ub[:, j % 2, t, :], sg[:, j % 2, t, :], a[:, 0:256], ALU.mult)
                emptied[b] = [u_tok[j, t]]

            def conv_in(j):
                b = 6 + j % 2
                after_emptied(b)
                wait("pe", u_tok[j, 0], u_tok[j, 1])
                for c in range(2):
                    for t in range(2):
                        m = nc.tensor.transpose(bank(b)[:, 256 * c + 128 * t:256 * c + 128 * t + 128],
                                                ub[:, j % 2, t, 128 * c:128 * c + 128], ident[:, :])
                tr = done(m)
                ub_turned[j, 0] = ub_turned[j, 1] = [tr]
                e = A([tr, *e0], uT[:, 2 * j:2 * j + 2, PADL:W], bank(b).rearrange("p (c n) -> p c n", c=2), ACT.Copy)
                emptied[b] = [e]
                return e

            pair(xT, ready, turn1, glu, lambda: conv_part(0, conv_in(0)), lambda j: brow[:, 512 * j:512 * j + 512])
            tap_some(8)
            p = take(4)
            for j in (2, 3):
                for t in range(2):
                    tok = project(p + 2 * j - 4, t, 4 + t, xT, ready, brow[:, 512 * j:512 * j + 512],
                                  None if t else lambda: conv_part(j - 1, conv_in(j - 1)))
                    glu(j, t, 4 + t, tok)
                    tap_some(14)
                    top_up(1)
            conv_part(3, conv_in(3))
            tap_some(len(taps))
            xT_multiplied[0] = [tok]
            lg, lgt, lgi = gain("lng")
            lb, lbt, lbi = gain("lnb")
            centred = []
            for t in range(2):
                after_emptied(2 * t, 2 * t + 1)
                for c in range(8):
                    wait("pe", ca_tok[c])
                    m = nc.tensor.transpose(bank(2 * t, 2)[:, 128 * c:128 * c + 128], ca[:, c, 128 * t:128 * t + 128],
                                            ident[:, :])
                tr = done(m)
                bs, mv, nm = stat(12), stat(2), stat()
                for h in range(2):
                    b = V([tr], nc.vector.bn_stats, bs[:, 6 * h:6 * h + 6], bank(2 * t + h))
                b = V([b], nc.vector.bn_aggr, mv, bs)
                g, r = rstd(b, mv[:, 1:2], 1.0, 1e-5)
                centred.append((g, r, mv, nm))
            for t in range(2):
                g, r, mv, nm = centred[t]
                n = V([g], STT, nm, mv[:, 0:1], -1.0, r, ALU.mult, ALU.mult)
                a = A([n, *e0], ya[:, t, :], bank(2 * t, 2), ACT.Identity, bias=nm, scale=r)
                emptied[2 * t] = emptied[2 * t + 1] = [a]
                centred[t] = a
            for t in range(2):
                v = V([centred[t], lgt], TT, ya[:, t, :], ya[:, t, :], lg, ALU.mult)
                v = V([v, lbt], TT, ya[:, t, :], ya[:, t, :], lb, ALU.add)
                gain_applied[lgi] = gain_applied[lbi] = [v]
                a = A([v, *xn_turned[t]], xn[:, t, :], ya[:, t, :], ACT.Silu)
                tr, ready[t] = flip(t, xn[:, t, :], a, xT, xT_multiplied[0])
                xn_turned[t] = [tr]
            gain_next()
            p = take(4)

            def close(t):
                wait("pe", *ready[t])
                after_emptied(2 * t, 2 * t + 1)
                for h in range(2):
                    MM(bank(2 * t + h), ones1[0:1, :], brow[:, 2048 + 512 * h:2560 + 512 * h], True, False)
                for q in range(4):
                    wait("pe", split_done[p + q])
                    H, L = wrows(p + q)
                    for k in range(2):
                        kk = 2 * q + k
                        for h in range(2):
                            m = mm3(bank(2 * t + h), xTh[:, kk, t, :], xTl[:, kk, t, :], H[:, k, 512 * h:512 * h + 512],
                                    L[:, k, 512 * h:512 * h + 512], False, kk == 7)
                    tok = done(m)
                    if t == 1:
                        multiplied[p + q] = tok
                        if q in (1, 2):
                            top_up(1)
                if t == 1:
                    xT_multiplied[0] = [tok]
                return tok

            seam(close, "mixpost0", False, "pre01")
        if stop == "conv":
            return write_out()
        ph0.close()
        ffn("b", bounds(), "post01", True, "pre10")
        ffn("c", bounds(), "post10", True, "kv")
        if stop == "ffn10":
            return write_out()

        def attention(tag, ph, n_pairs, M, W, q_of, k_of, v_of, v_tok, bias, oT, e0):
            sc = sb(f"sc{tag}", [128, 3, 2, 2, 256], F32, ph)
            PT = sb(f"PT{tag}", [128, 2, 2, 2, 256], F32, ph)
            p_turned = {}
            pt_multiplied = {}
            o_tok = None

            def scores(i):
                u, s = i % 3, 2 * (i % 2)
                after_emptied(s, s + 1)
                for t in range(2):
                    for hh in range(2):
                        l, lt = q_of(2 * i + hh, t)
                        r, rt = k_of(2 * i + hh, W[t])
                        wait("pe", *lt, *rt)
                        m = MM(bank(s + hh)[:, 256 * t:256 * t + W[t]], l, r, True, True)
                tok = done(m)
                after = [tok, *p_turned.get(i - 3, ()), *e0]
                bufs_of, biased, peak, tops = {}, {}, {}, []
                for t in range(2):
                    P = sc[:, u, t, :, 0:W[t]]
                    S = bank(s, 2).rearrange("p (h t n) -> p h t n", h=2, t=2)[:, :, t, 0:W[t]]
                    biased[t] = bias(i, t, P, S, after) if bias else tok
                    bufs_of[t] = P, P if bias else S, *stat2(t, u)
                    peak[t] = V([biased[t]], nc.vector.tensor_reduce, bufs_of[t][2], bufs_of[t][1], AX.X, ALU.max, negate=True)
                for t in range(2):
                    P, src, mx, sm, rc = bufs_of[t]
                    for hh in range(2):
                        a = A([peak[t] if bias else peak[1], *after], P[:, hh, :], src[:, hh, :], ACT.Exp, bias=mx[:, hh:hh + 1],
                              accum_out=sm[:, hh:hh + 1])
                    tops.append(a)
                for b in (s, s + 1):
                    emptied[b] = [biased[1] if bias else a]
                return [bufs_of[t] + (tops[t],) for t in range(2)]

            def scaled(parts_of):
                toks = []
                for P, _, _, sm, rc, a in parts_of:
                    r = V([a], nc.vector.reciprocal, rc, sm)
                    for hh in range(2):
                        v = V([r], TS, P[:, hh, :], P[:, hh, :], rc[:, hh:hh + 1], None, ALU.mult)
                    toks.append(v)
                return toks

            def turned(i, toks):
                s, u = i % 2, i % 3
                pt = []
                for kk in range(2):
                    ts = [t for t in range(2) if W[t] > 128 * kk]
                    after_emptied(4 + kk)
                    wait("pe", *toks)
                    for hh in range(2):
                        for t in ts:
                            m = nc.tensor.transpose(bank(4 + kk)[:, 256 * hh + 128 * t:256 * hh + 128 * t + 128],
                                                    sc[:, u, t, hh, 128 * kk:128 * kk + 128], ident[:, :])
                    tr = done(m)
                    lo = 128 * ts[0]
                    src = bank(4 + kk).rearrange("p (h n) -> p h n", h=2)[:, :, lo:256]
                    dst = PT[:, s, kk, :, lo:256]
                    w = [tr, *pt_multiplied.get(i - 2, ()), *e0]
                    e = A(w, dst, src, ACT.Copy)
                    emptied[4 + kk] = [e]
                    pt.append((e, lo))
                p_turned[i] = [tr]
                return pt

            def values(i, pt):
                s, ob = i % 2, 6 + i % 2
                after_emptied(ob)
                wait("pe", *v_tok)
                for hh in range(2):
                    o = bank(ob)[:, 256 * hh:256 * hh + 256] if M == 128 else bank(ob)[64 * hh:64 * hh + 64, 0:256]
                    for kk in range(2):
                        e, lo = pt[kk]
                        wait("pe", e)
                        m = MM(o[:, lo:256], v_of(2 * i + hh, kk), PT[:, s, kk, hh, lo:256], kk == 0, kk == 1)
                tok = done(m)
                pt_multiplied[i] = [tok]
                if M == 128:
                    src = bank(ob).rearrange("p (h t n) -> p h t n", h=2, t=2)
                    d = slice(2 * i, 2 * i + 2)
                    return hilo(ob, src, oT[0][:, d, :, :], oT[1][:, d, :, :], tok, [*e0, *xT_multiplied[0]])
                src = bank(ob)[:, 0:256].rearrange("p (t n) -> p t n", t=2)
                return hilo(ob, src, oT[0][:, i, :, :], oT[1][:, i, :, :], tok, [*e0, *xT_multiplied[0]])

            bufs = sb(f"sm{tag}", [128, 36], F32, ph)

            def stat2(t, s):
                a = 12 * s + 6 * t
                return bufs[:, a:a + 2], bufs[:, a + 2:a + 4], bufs[:, a + 4:a + 6]

            toks, pts, outs = {}, {}, []
            for i in range(n_pairs + 3):
                if 1 <= i <= n_pairs:
                    toks[i - 1] = scaled(toks[i - 1])
                if i < n_pairs:
                    toks[i] = scores(i)
                if 2 <= i < n_pairs + 2:
                    pts[i - 2] = turned(i - 2, toks[i - 2])
                if i >= 3:
                    outs.append(values(i - 3, pts[i - 3]))
                top_up(1)
            return outs

        def close_with(p, o_tok, first_act=None):
            def close(t):
                for q in range(4):
                    tok = down(p + q, t, lambda k: (xTh[:, 2 * q + k, t, :], xTl[:, 2 * q + k, t, :]),
                               q == 0 and first_act is None, q == 3, o_tok[t])
                    if t == 1 and q in (1, 2):
                        top_up(1)
                if t == 1:
                    xT_multiplied[0] = [tok]
                return tok
            return close

        ph = ExitStack()
        with ph:
            qh = sb("qh", [128, 8, 2, 128], F32R, ph)
            ql = sb("ql", [128, 8, 2, 128], F32R, ph)
            kT = sb("kT", [128, 8, 256], F32, ph)
            qT = sb("qT", [128, 8, 256], F32, ph)
            vv = sb("vv", [128, 2, D], F32, ph)
            dm = sb("dm", [128, 2, 256], F32, ph)
            e0 = bounds()
            a0 = CST["dm"][0]
            t_dm = load("sp", "cst", dm[:, :, :], cst_in[:, a0:a0 + 512].rearrange("p (t n) -> p t n", t=2), e0)
            v_tok = []

            def keep_v(j, t, b, tok):
                v_tok.append(A([tok, *e0], vv[:, t, 512 * j:512 * j + 512], bank(b), ACT.Copy))
                emptied[b] = [v_tok[-1]]

            qready = [None, None]

            def q_scale():
                turn1()
                for t in range(2):
                    pre_scale(t, "mixpre1", x_stats[t])

            def q_turned(t):
                qready[t] = pre_turn(t, (qh, ql), e0)

            pair(xT, ready, q_scale, keep_v, lambda: q_turned(0))
            gain_next()

            def heads_t(dst, act, tok, scale):
                toks = []
                for j in range(2):
                    p = take(2)
                    for n, m in enumerate(project_t(p, act, tok, 4 - 4 * j)):
                        h, b = 4 * j + 2 * n, 4 - 4 * j + n
                        toks.append(A([m, *e0], dst[:, h:h + 2, :], bank(b).rearrange("p (h n) -> p h n", h=2),
                                      ACT.Copy, scale=scale))
                        emptied[b] = [toks[-1]]
                    top_up(2)
                return toks

            k_tok = heads_t(kT, xT, ready, 1.0)
            q_turned(1)
            xT_multiplied[0] = [("pe", counts["pe"])]
            q_tok = heads_t(qT, (qh, ql), qready, float(128 ** -0.5))

            def alibi(i, t, P, S, after):
                n = P.shape[2]
                for hh in range(2):
                    v = V([t_dm, *after], STT, P[:, hh, :], dm[:, t, 0:n], -float(2.0 ** -(2 * i + hh + 1)), S[:, hh, :],
                          ALU.mult, ALU.add)
                return v

            o_tok = attention("a", ph, 4, 128, [128, 256],
                              lambda h, t: (qT[:, h, 128 * t:128 * t + 128], q_tok),
                              lambda h, n: (kT[:, h, 0:n], k_tok),
                              lambda h, kk: vv[:, kk, 128 * h:128 * h + 128], v_tok, alibi, xT, e0)
            seam(close_with(take(4), [o_tok, o_tok]), "mixpost1", False, "pre11")
        if stop == "attn":
            return write_out()
        ffn("d", bounds(), "post11", True, "evenmix")
        if stop == "ffn11":
            return write_out()

        def head_norm(src, n, gname, dst, tok, after, mul, add):
            a0 = SMALL[gname][0]
            g64 = small[:, a0:a0 + 64]
            ss, v, r = stat(n), stat(n), stat(n)
            src3 = src.rearrange("p (h d) -> p h d", d=64)
            s = A([tok, *after], dst, src3, ACT.Square)
            s = V([s], nc.vector.tensor_reduce, ss, dst, AX.X, ALU.add)
            g = G([s], nc.gpsimd.tensor_scalar, v, ss, mul, add, ALU.mult, ALU.add)
            g = G([g, t_half], nc.gpsimd.tensor_tensor, r, v, mhalf[:, 0:n], ALU.pow)
            top_up(1)
            v1 = V([g], TT, dst, src3, spread(r, 2, 64), ALU.mult)
            v2 = V([v1, t_small], TT, dst, dst, spread(g64, 1, n), ALU.mult)
            return v1, v2

        ph = ExitStack()
        with ph:
            oTh = sb("oTh", [128, 4, 2, 128], F32R, ph)
            oTl = sb("oTl", [128, 4, 2, 128], F32R, ph)
            zs = sb("zs", [128, 2, D], F32, ph)
            xc = sb("xc", [128, 16, 256], F32, ph)
            dz = sb("dz", [128, 8, 64], F32, ph)
            nac = sb("nac", [128, 64], F32, ph)
            e0 = bounds()
            xw = [*e0]
            ph2 = ExitStack()
            with ph2:
                kTn = sb("kTn", [128, 4, 256], F32, ph2)
                qTn = sb("qTn", [128, 4, 256], F32, ph2)
                vn = sb("vn", [128, 2, 512], F32, ph2)
                ph3 = ExitStack()
                ctx.enter_context(ph3)
                nabr = sb("nabr", [128, 2, 2, 256], F32, ph2)
                win = sb("win", [128, 2, 64], F32, ph2)
                a0 = CST["win"][0]
                t_win = load("sp", "cst", win[:, :, :], cst_in[:, a0:a0 + 128].rearrange("p (a n) -> p a n", a=2), e0)
                xp = sb("xp", [128, 4, 260], F32, ph3)
                qn = sb("qn", [128, 2, 2, 512], F32, ph3)
                t_z = G(e0, nc.gpsimd.memset, xp[:, :, 0:2], 0.0)
                t_z = G(e0, nc.gpsimd.memset, xp[:, :, 258:260], 0.0)
                wd = cols[:, COLS["wdt"][0]:COLS["wdt"][0] + 256].rearrange("p (k n) -> p k n", k=8)
                qk_normed, qk_tok = {}, {}

                def qk_norm(j, t, b, tok):
                    mul, add = (1.0 / 64, 1e-6) if j else (1.0, 64e-6)
                    name = "nak" if j else "naq"
                    v1, v2 = head_norm(bank(b), 8, name, qn[:, j, t, :].rearrange("p (h d) -> p h d", d=64),
                                          tok, e0, mul, add)
                    emptied[b] = [v1]
                    qk_normed[j, t] = v2

                def qk_turn(j, t):
                    dst = kTn if j else qTn
                    b = 6 + (j + t) % 2
                    tr = transposed(lambda k: qn[:, j, t, 128 * k:128 * k + 128], 4, b, [qk_normed[j, t]])
                    e = A([tr, *e0], dst[:, :, 128 * t:128 * t + 128], bank(b).rearrange("p (k n) -> p k n", k=4), ACT.Copy)
                    emptied[b] = [e]
                    qk_tok[j, t] = e

                pair(xT, ready, turn1, qk_norm, fresh=0)
                nab = xn[:, :, :].rearrange("p s (t h k) -> p s t h k", t=2, h=2)
                nab_added, nab_win = {}, {}

                def nab_load(i):
                    s = i % 2
                    for r in range(4):
                        for j in range(4):
                            off = 2 * i * 465 + (j - r + 7) * 31 - 48
                            src = bass.AP(tensor=rpb_in.tensor, offset=off, ap=[[1, 64], [465, 2], [1, 64]])
                            dst = nabr[64 * (r % 2):64 * (r % 2) + 64, r // 2, :, 64 * j:64 * j + 64]
                            tok = load("sp", f"nab{s}", dst, src, [*e0, *nab_read.get(i - 1, ())])
                    for t in range(2):
                        B = nabr[:, t, :, :]
                        rev = bass.AP(tensor=B.tensor, offset=B.offset + 63, ap=[list(B.ap[0]), [64, 8], [-1, 64]])
                        N8 = nab[:, s, t, :, :].rearrange("p h (j c) -> p (h j) c", c=64)
                        g = G([tok, t_win, *xn_turned[s]], nc.gpsimd.tensor_tensor, N8, rev, spread(win[:, 0, :], 1, 8), ALU.mult)
                        nab_win[i, t] = G([g], nc.gpsimd.tensor_tensor, N8, N8, spread(win[:, 1, :], 1, 8), ALU.add)
                    nab_read[i] = [g]

                nab_read = {}
                for i in range(2):
                    nab_load(i)
                after_emptied(6)
                wait("pe", t_cols)
                for t in range(2):
                    for k in range(8):
                        o = bank(6)[:, 32 * t:32 * t + 32]
                        MM(o, xTh[:, k, t, :].bitcast(F32), wd[:, k, :], k == 0, False)
                        m = MM(o, xTl[:, k, t, :].bitcast(F32), wd[:, k, :], False, k == 7)
                dt_tok = done(m)
                db = small[:, SMALL["dtb"][0]:SMALL["dtb"][0] + 32]
                al = small[:, SMALL["alog"][0]:SMALL["alog"][0] + 32]
                d = [dz[:, i, :] for i in range(8)]
                d3 = [dz[:, i, :].rearrange("p (t n) -> p t n", t=2) for i in range(8)]
                t_dz = V([dt_tok, t_small, *e0], TT, d3[0], bank(6)[:, 0:64].rearrange("p (t n) -> p t n", t=2), spread(db, 1, 2), ALU.add)
                emptied[6] = [t_dz]
                xp_convolved = {0: [], 1: []}
                xc_tok = {}
                cw0, cb0 = COLS["cw"][0], COLS["cb"][0]
                for c in range(4):
                    p = take(2)
                    top_up(2)
                    for n, m in enumerate(project_t(p, xT, ready, 4 - 4 * (c % 2))):
                        b = 4 - 4 * (c % 2) + n
                        e = A([m, t_z, *e0, *xp_convolved[n]], xp[:, 2 * n:2 * n + 2, 2:258],
                              bank(b).rearrange("p (h n) -> p h n", h=2), ACT.Copy)
                        emptied[b] = [e]
                        tap = {}
                        for k in range(4):
                            for u in range(2):
                                ch = 4 * c + 2 * n + u
                                wk = cols[:, cw0 + 4 * ch + k:cw0 + 4 * ch + k + 1]
                                s = xp[:, 2 * n + u, k:k + 256]
                                if k == 0:
                                    tap[u] = V([e], TS, xc[:, ch, :], s, wk, cols[:, cb0 + ch:cb0 + ch + 1], ALU.mult, ALU.add)
                                else:
                                    tap[u] = V([tap[u]], STT, xc[:, ch, :], s, wk, xc[:, ch, :], ALU.mult, ALU.add)
                        xp_convolved[n] = [tap[1]]
                        ch = 4 * c + 2 * n
                        xc_tok[ch] = xc_tok[ch + 1] = A([tap[0], tap[1]], xc[:, ch:ch + 2, :], xc[:, ch:ch + 2, :], ACT.Silu)
                    qk_turn(c % 2, c // 2)
                p = take(2)
                top_up(2)
                v_tok = []
                for t in range(2):
                    gt = project(p, t, 4 + t, xT, ready)
                    v_tok.append(A([gt, *e0], vn[:, t, :], bank(4 + t), ACT.Copy))
                    emptied[4 + t] = [v_tok[-1]]
                z_tok = [[], []]
                for j in range(2):
                    p = take(2)
                    top_up(2)
                    for t in range(2):
                        b = 2 * j + t
                        gt = project(p, t, b, xT, ready)
                        z = A([gt, *e0], zs[:, t, 512 * j:512 * j + 512], bank(b), ACT.Silu)
                        emptied[b] = [z]
                        z_tok[t].append(z)
                xT_multiplied[0] = [gt]
                v = V([t_dz], STT, d[1], d[0], -1.0, d[0], ALU.mult, ALU.max)
                a = A([v], d[2], d[1], ACT.Exp, scale=-1.0)
                v = V([a], TS, d[3], d[2], 1.0, None, ALU.add)
                a = A([v], d[4], d[3], ACT.Ln)
                v = V([v], STT, d[5], d[3], -1.0, d[2], ALU.add, ALU.subtract)
                v = V([v], nc.vector.reciprocal, d[6], d[3])
                v = V([v], TT, d[5], d[5], d[6], ALU.mult)
                v = V([v, a], TT, d[4], d[4], d[5], ALU.subtract)
                v_dt = V([v], STT, d[0], d[0], 0.0, d[4], ALU.max, ALU.add)
                a = A([t_small, v], d[7][:, 0:32], al, ACT.Exp)
                v_a = V([a, v_dt], STT, d3[1], d3[0], -1.0, spread(d[7][:, 0:32], 1, 2), ALU.mult, ALU.mult)
                e2 = [*e0, dt_tok, v_a, *qk_tok.values(), *v_tok]
                ph3.close()
                def nabias(i, t, P, S, after):
                    if t == 0 and i >= 2:
                        nab_load(i)
                    v = V([*after, nab_win[i, t]], TT, P, nab[:, i % 2, t, :, :], S, ALU.add)
                    nab_added[i] = [v]
                    xn_turned[i % 2] = [v]
                    return v

                o_tok = attention("n", ph2, 4, 64, [256, 256],
                                  lambda h, t: (qTn[64 * (h % 2):64 * (h % 2) + 64, h // 2, 128 * t:128 * t + 128], [qk_tok[0, t]]),
                                  lambda h, n: (kTn[64 * (h % 2):64 * (h % 2) + 64, h // 2, 0:n], [qk_tok[1, 0], qk_tok[1, 1]]),
                                  lambda h, kk: vn[:, kk, 64 * h:64 * h + 64], v_tok, nabias, (oTh, oTl), e2)
            e1 = [o_tok[-1], ("act", counts["act"]), ("dve", counts["dve"]), ("pe", counts["pe"])]
            xd = sb("xd", [128, 2, 2, D], F32, ph)
            cb = sb("cbm", [128, 2, 4, 256], F32, ph)
            m2 = sb("m2", [128, 8, 128], F32, ph)
            tri = sb("tri", [128, 5, 128], F32, ph)
            a0 = CST["tf"][0]
            t_tri = load("sp", "cst", tri[:, :, :], cst_in[:, a0:a0 + 640].rearrange("p (a n) -> p a n", a=5), e1)
            TF, TB, ON, MF, MB = (tri[:, i, :] for i in range(5))
            xs_tok = []
            for t in range(2):
                for b in range(2):
                    tr = transposed(lambda k: xc[:, 4 * b + k, 128 * t:128 * t + 128], 4, 6 + b, [xc_tok[4 * b + k] for k in range(4)])
                    e = A([tr, *xn_turned[t]], xn[:, t, 512 * b:512 * b + 512], bank(6 + b), ACT.Copy)
                    emptied[6 + b] = [e]
                xs_tok.append(e)
            xd_tok = {}
            for t in range(2):
                for r in range(2):
                    xd_tok[r, t] = V([xs_tok[t], v_dt, *e1], TT, xd[:, r, t, :].rearrange("p (h d) -> p h d", d=64),
                                     xn[:, t, :].rearrange("p (h d) -> p h d", d=64),
                                     spread(d3[0][:, t, 16 * r:16 * r + 16], 2, 64), ALU.mult)
            for s in range(2):
                after_emptied(4 + 0, 5)
                wait("pe", *[xc_tok[c] for c in range(8, 16)])
                for g in range(4):
                    m = MM(bank(4 + g // 2)[:, 256 * (g % 2):256 * (g % 2) + 256], xc[:, 8 + g, 128 * s:128 * s + 128],
                           xc[:, 12 + g, :], True, True)
                tok = done(m)
                cb_tok = A([tok, *e1], cb[:, s, :, :], bank(4, 2).rearrange("p (g n) -> p g n", g=4), ACT.Copy)
                emptied[4] = emptied[5] = [cb_tok]
            after_emptied(6)
            wait("pe", t_tri, v_a)
            av = d3[1]
            for r in range(2):
                T = (TF, TB)[r]
                for s in range(2):
                    o = bank(6)[:, 32 * r + 16 * s:32 * r + 16 * s + 16]
                    near = s != r
                    m = MM(o, T, av[:, s, 16 * r:16 * r + 16], True, not near)
                    if near:
                        m = MM(o, ON, av[:, 1 - s, 16 * r:16 * r + 16], False, True)
            tok = done(m)
            t_nac = V([tok, *e1], TS, nac[:, :], bank(6)[:, 0:64], -1.0, None, ALU.mult)
            emptied[6] = [t_nac]
            Mx = [xc[:, 0:4, :].rearrange("p c (u n) -> p (c u) n", u=2), xc[:, 4:8, :].rearrange("p c (u n) -> p (c u) n", u=2),
                  m2[:, :, :]]
            mx_multiplied = {i: [] for i in range(3)}
            sn, snt, sni = gain("ssdnorm")
            Dk = small[:, SMALL["dskip"][0]:SMALL["dskip"][0] + 16]
            for l in range(2):
                blocks = [(0, 0), (1, 0), (1, 1)] if l == 0 else [(0, 0), (0, 1), (1, 1)]
                for hh in range(2):
                    m_tok = []
                    for i, (r, s) in enumerate(blocks):
                        T, msk = (TF, TB)[r], (MF, MB)[r]
                        cross = l != r
                        for b in range(2):
                            bk = 2 * (i % 2) + b
                            after_emptied(bk)
                            if s == l:
                                MM(bank(bk), ident[:, :], spread(msk, 1, 4), True, False)
                            for h in range(4):
                                hd = 8 * hh + 4 * b + h
                                o = bank(bk)[:, 128 * h:128 * h + 128]
                                ends = s != l or h == 3
                                m = MM(o, spread(av[:, l, 16 * r + hd], 1, 128), T, s != l, not cross and ends)
                                if cross:
                                    m = MM(o, spread(av[:, 1 - l, 16 * r + hd], 1, 128), ON, False, ends)
                            tok = done(m)
                            for h in range(4):
                                hd = 8 * hh + 4 * b + h
                                e = A([tok, t_nac, *mx_multiplied[i], *xs_tok, *e1], Mx[i][:, 4 * b + h, :], bank(bk)[:, 128 * h:128 * h + 128],
                                      ACT.Exp, bias=nac[:, 32 * r + 16 * s + hd:32 * r + 16 * s + hd + 1])
                            emptied[bk] = [e]
                        m4 = Mx[i].rearrange("p (g r) n -> p g r n", g=2)
                        m_tok.append(V([e, cb_tok], TT, m4, m4, spread(cb[:, s, 2 * hh:2 * hh + 2, 128 * l:128 * l + 128], 2, 4), ALU.mult))
                    after_emptied(4 + hh)
                    wait("pe", *m_tok, *[xd_tok[k] for k in xd_tok])
                    for h in range(8):
                        hd = 8 * hh + h
                        for i, (r, s) in enumerate(blocks):
                            m = MM(bank(4 + hh)[:, 64 * h:64 * h + 64], Mx[i][:, h, :], xd[:, r, s, 64 * hd:64 * hd + 64], i == 0, i == 2)
                    y_tok = done(m)
                    mx_multiplied = {i: [y_tok] for i in range(3)}
                ya = tmp[:, :]
                y3 = ya.rearrange("p (h d) -> p h d", d=64)
                v = V([xs_tok[l], *tmp_added[0]], TT, y3, xn[:, l, :].rearrange("p (h d) -> p h d", d=64), spread(Dk, 2, 64), ALU.mult)
                v = V([v, y_tok], TT, ya, ya, bank(4, 2), ALU.add)
                emptied[4] = emptied[5] = [v]
                v = V([v, *z_tok[l]], TT, ya, ya, zs[:, l, :], ALU.mult)
                ss = stat(4)
                for g in range(4):
                    a = A([v], xn[:, l, 256 * g:256 * g + 256], ya[:, 256 * g:256 * g + 256], ACT.Square, accum_out=ss[:, g:g + 1])
                g, rr = rstd(a, ss, 1.0 / 256, 1e-6, 4)
                v = V([g], TT, ya.rearrange("p (g d) -> p g d", g=4), ya.rearrange("p (g d) -> p g d", g=4), spread(rr, 2, 256), ALU.mult)
                v = V([v, snt], TT, xn[:, l, :], ya, sn, ALU.mult)
                tmp_added[0] = [v]
                gain_applied[sni] = [v]
                tr, ready[l] = flip(l, xn[:, l, :], v, xT, xT_multiplied[0])
                xn_turned[l] = [tr]
            p = take(2)
            for q in range(2):
                for t in range(2):
                    down(p + q, t, lambda k: (oTh[:, 2 * q + k, t, :], oTl[:, 2 * q + k, t, :]), q == 0, False, o_tok)
            seam(close_with(take(4), ready, p), None, False, "ffn0")
        if stop == "even":
            return write_out()
        ffn("e", bounds(), None, False, "oddmix")
        if stop == "ffn20":
            return write_out()

        ph = ExitStack()
        with ph:
            e0 = bounds()
            qg = sb("qg", [128, 2, D], F32, ph)
            qTg = sb("qTg", [128, 8, 256], F32, ph)
            kd = sb("kd", [128, 2, 4, 2, 64], F32, ph)
            kTg = sb("kTg", [128, 4, 256], F32, ph)
            vg = sb("vg", [128, 2, 256], F32, ph)
            kg = sb("kg", [128, 2, 256], F32, ph)
            r1 = sb("r1", [128, 512], F32, ph)
            r2 = sb("r2", [128, 512], F32, ph)
            cs = sb("cs", [128, 2, 2, 64], F32, ph)
            a0 = CST["cos"][0]
            t_cs = load("sp", "cst", cs[:, :, :, :], cst_in[:, a0:a0 + 256].rearrange("p (a t n) -> p a t n", a=2, t=2), e0)
            rf = [[]]

            def rope(src, n, t, dst, tok):
                a, b = r1[:, 0:64 * n].rearrange("p (h d) -> p h d", d=64), r2[:, 0:64 * n].rearrange("p (h d) -> p h d", d=64)
                v1 = V([tok, t_cs, *rf[0], *e0], TT, a, src, spread(cs[:, 0, t, :], 1, n), ALU.mult)
                sw = bass.AP(tensor=src.tensor, offset=src.offset + 1, ap=[list(src.ap[0]), [64, n], [2, 32], [-1, 2]])
                sn_ = cs[:, 1, t, :]
                v2 = V([], TT, b.rearrange("p h (m u) -> p h m u", u=2), sw,
                       spread(sn_.rearrange("p (m u) -> p m u", u=2), 1, n), ALU.mult)
                for dd in dst:
                    v = V([v1, v2], TT, dd, a, b, ALU.add)
                rf[0] = [v]
                return v

            qg_tok, qg_rope = {}, {}

            def q_norm(j, t, b, tok):
                dst = qg[:, t, 512 * j:512 * j + 512].rearrange("p (h d) -> p h d", d=64)
                v1, v2 = head_norm(bank(b), 8, "gq", dst, tok, e0, 1.0, 64e-6)
                emptied[b] = [v1]
                qg_rope[j, t] = rope(dst, 8, t, [dst], v2)

            pair(xT, ready, turn1, q_norm, fresh=0)

            def q_turn(j, t):
                b = 6 + t
                tr = transposed(lambda k: qg[:, t, 512 * j + 128 * k:512 * j + 128 * k + 128], 4, b, [qg_rope[j, t]])
                e = A([tr, *e0], qTg[:, 4 * j:4 * j + 4, 128 * t:128 * t + 128], bank(b).rearrange("p (k n) -> p k n", k=4), ACT.Copy)
                emptied[b] = [e]
                qg_tok[j, t] = e

            p = take(2)
            kg_tok, v_tok = [], []
            for t in range(2):
                gt = project(p, t, 4 + t, xT, ready)
                b = bank(4 + t)
                dst = kg[:, t, :].rearrange("p (h d) -> p h d", d=64)
                v1, v2 = head_norm(b[:, 0:256], 4, "gk", dst, gt, e0, 1.0 / 64, 1e-6)
                a = A([v1, *e0], vg[:, t, :], b[:, 256:512], ACT.Copy)
                v_tok.append(a)
                emptied[4 + t] = [a]
                v = rope(dst, 4, t, [kd[:, t, :, 0, :], kd[:, t, :, 1, :]], v2)
                tr = transposed(lambda k: kd[:, t, k, :, :].rearrange("p a d -> p (a d)"), 4, 6 + t, [v])
                e = A([tr, *e0], kTg[:, :, 128 * t:128 * t + 128], bank(6 + t).rearrange("p (k n) -> p k n", k=4), ACT.Copy)
                emptied[6 + t] = [e]
                kg_tok.append(e)
            xT_multiplied[0] = [gt]

            for j in range(2):
                for t in range(2):
                    q_turn(j, t)
            o_tok = attention("g", ph, 8, 64, [256, 256],
                              lambda h, t: (qTg[64 * (h % 2):64 * (h % 2) + 64, h // 2, 128 * t:128 * t + 128], [qg_tok[h // 8, t]]),
                              lambda h, n: (kTg[64 * (h % 2):64 * (h % 2) + 64, h // 4, 0:n], kg_tok),
                              lambda h, kk: vg[:, kk, 64 * (h // 4):64 * (h // 4) + 64], v_tok, None, xT, e0)
            seam(close_with(take(4), [o_tok, o_tok]), None, False, "ffn1")
        if stop == "odd":
            return write_out()
        ffn("f", bounds(), None, False, None)
        assert piece[0] == n_pieces, (piece[0], n_pieces)
        write_out()


def kernel(**inputs):
    import concourse.bacc as bacc
    from concourse.bass_utils import run_bass_kernel_spmd as run

    i = {k: np.asarray(v) for k, v in inputs.items()}
    arrays = {
        "in_x": np.ascontiguousarray(i["x"].reshape(256, D)),
        "in_w": np.ascontiguousarray(pack_stream(i)),
        "in_rows": np.ascontiguousarray(pack_rows(i)),
        "in_small": np.ascontiguousarray(pack_small(i)),
        "in_cols": np.ascontiguousarray(pack_cols(i)),
        "in_bias": np.ascontiguousarray(pack_bias(i)),
        "in_rpb": np.ascontiguousarray(i["na_rel_bias_2"][0][:, :, ::-1].reshape(-1)),
        "in_cst": constants(),
    }
    nc = bacc.Bacc("TRN2", target_bir_lowering=False, num_devices=1, dynamic_dma_scratch_size=1024)
    args = [nc.dram_tensor(k, a.shape, mybir.dt.from_np(a.dtype), kind="ExternalInput").ap() for k, a in arrays.items()]
    out = nc.dram_tensor("out_x", (256, D), F32, kind="ExternalOutput").ap()
    build(nc, *args, out)
    r = run(nc, [arrays], core_ids=[0])
    return r.results[0]["out_x"].reshape(1, 256, D)
```

```python
from contextlib import ExitStack

import numpy as np

import concourse.bass as bass
from concourse import mybir

F32 = mybir.dt.float32
F32R = mybir.dt.float32r
ACT = mybir.ActivationFunctionType
ALU = mybir.AluOpType
AX = mybir.AxisListType

D = 1024
FF = 2816
NJ = FF // 256
RAW = 7
RING = 5
TAPS = 31
NGAIN = 3
BIG = 1.0e33
NEG = -1.0e30

GAINS = (["pre00", "post00", "mixpre0", "mixpost0", "pre01", "post01", "pre10", "post10",
          "kv", "mixpre1", "mixpost1", "pre11", "post11", "evenmix", "ssdnorm", "ffn0", "oddmix", "ffn1"])

CST = {}
COLS = {}


def _layout(table, items):
    at = 0
    for name, n in items:
        table[name] = (at, n)
        at += n
    return at


N_CST = _layout(CST, [("ident", 128), ("tf", 128), ("tb", 128), ("ones", 128), ("mf", 128), ("mb", 128),
                      ("dm", 512), ("sel", 18), ("win", 128), ("cos", 128), ("sin", 128)])
N_KEEP = 128
N_COLS = _layout(COLS, [("dw", 8 * TAPS), ("dwb", 8), ("cw", 64), ("cb", 16), ("wdt", 256), ("lng", 8), ("lnb", 8)])


def constants():
    c = np.zeros((128, N_CST), np.float32)

    def put(name, v):
        a, n = CST[name]
        c[:, a:a + n] = v.reshape(128, n)

    i = np.arange(128)
    put("ident", np.eye(128))
    put("tf", (i[:, None] <= i[None, :]))
    put("tb", (i[:, None] >= i[None, :]))
    put("ones", np.ones((128, 128)))
    put("mf", np.where(i[:, None] <= i[None, :], 0.0, NEG))
    put("mb", np.where(i[:, None] >= i[None, :], 0.0, NEG))
    q = i[:, None, None] + 128 * np.arange(2)[None, :, None]
    k = np.arange(256)[None, None, :]
    head = np.arange(16)
    put("sel", np.concatenate([i[:, None] % 16 == head, i[:, None] // 16 % 2 == 0, i[:, None] // 16 % 2 == 1], axis=1))
    put("dm", np.where(k <= q, q - k, BIG))
    cq = i % 64
    st = np.clip(cq - 8, 0, 48)
    kc = np.arange(64)
    inside = (kc[None] >= st[:, None]) & (kc[None] < st[:, None] + 16)
    put("win", np.stack([inside, np.where(inside, 0.0, NEG)], axis=1))
    t = i[:, None] + 128 * np.arange(2)[None, :]
    freqs = (np.float32(10000.0) ** (-np.arange(0, 32, 2, dtype=np.float32) / np.float32(32))).astype(np.float32)
    ang = np.concatenate([(t // 64).astype(np.float32)[:, :, None] * freqs,
                          (t % 64).astype(np.float32)[:, :, None] * freqs], axis=-1)
    put("cos", np.repeat(np.cos(ang), 2, axis=-1))
    s = np.repeat(np.sin(ang), 2, axis=-1)
    s[:, :, 0::2] *= -1.0
    put("sin", s)
    return c


def pack_stream(i):
    out = []

    def cols(w, spans):
        w = np.concatenate([w[:, a:b] for a, b in spans], axis=1)
        v = w.reshape(2, 4, 128, 512).transpose(0, 2, 1, 3).reshape(2, 128, 2048)
        out.extend([v[0], v[1]])

    def rows(w, r0):
        out.append(w[r0:r0 + 256].reshape(2, 128, 1024).transpose(1, 0, 2).reshape(128, 2048))

    def ffn(wgu, wd):
        for j in range(NJ):
            cols(wgu, [(256 * j, 256 * j + 256), (FF + 256 * j, FF + 256 * j + 256)])
            if j:
                rows(wd, 256 * (j - 1))
        rows(wd, 256 * (NJ - 1))

    gu, dn = i["ffn_w_gate_up"], i["ffn_w_down"]
    ffn(gu[0, 0], dn[0, 0])
    for j in range(4):
        cols(i["conv_w_in"][0], [(256 * j, 256 * j + 256), (1024 + 256 * j, 1280 + 256 * j)])
    for j in range(4):
        rows(i["conv_w_out"][0], 256 * j)
    ffn(gu[0, 1], dn[0, 1])
    ffn(gu[1, 0], dn[1, 0])
    for j in (2, 3, 0, 1):
        cols(i["w_kv"], [(512 * j, 512 * j + 512)])
    for j in range(2):
        cols(i["attn_w_q"][0], [(512 * j, 512 * j + 512)])
    for j in range(4):
        rows(i["attn_w_o"][0], 256 * j)
    ffn(gu[1, 1], dn[1, 1])
    we = i["even_w_in_2"][0]
    for c in (0, 512, 2560, 3072, 3584, 4096, 1024, 1536, 2048):
        cols(we, [(c, c + 512)])
    for j in range(6):
        rows(i["even_w_out_2"][0], 256 * j)
    ffn(i["ffn_w13_2"][0], i["ffn_w2_2"][0])
    for j in (2, 0, 1):
        cols(i["odd_w_qkv_2"][0], [(512 * j, 512 * j + 512)])
    for j in range(4):
        rows(i["odd_w_out_2"][0], 256 * j)
    ffn(i["ffn_w13_2"][1], i["ffn_w2_2"][1])
    return np.stack(out)


def pack_rows(i):
    a, b = i["ffn_norm_pre"], i["ffn_norm_post"]
    v = {"pre00": a[0, 0], "post00": b[0, 0], "pre01": a[0, 1], "post01": b[0, 1],
         "pre10": a[1, 0], "post10": b[1, 0], "pre11": a[1, 1], "post11": b[1, 1],
         "mixpre0": i["mix_norm_pre"][0], "mixpre1": i["mix_norm_pre"][1],
         "mixpost0": i["mix_norm_post"][0], "mixpost1": i["mix_norm_post"][1],
         "kv": i["kv_norm"],
         "evenmix": i["even_mix_norm_2"][0], "ssdnorm": i["ssd_out_norm_2"][0],
         "ffn0": i["ffn_norm_2"][0], "ffn1": i["ffn_norm_2"][1], "oddmix": i["odd_mix_norm_2"][0]}
    return np.stack([v[n] for n in GAINS])


SMALL = {}
N_SMALL = _layout(SMALL, [("naq", 64), ("nak", 64), ("gq", 64), ("gk", 64), ("dtb", 32), ("alog", 32), ("dskip", 16)])


def pack_small(i):
    return np.concatenate([i["na_q_norm_2"][0], i["na_k_norm_2"][0], i["gqa_q_norm_2"][0], i["gqa_k_norm_2"][0],
                           i["ssd_dt_bias_2"][0].ravel(), i["ssd_A_log_2"][0].ravel(), i["ssd_D_2"][0]])[None]


def pack_cols(i):
    def tiles(v, n):
        return v.reshape(-1, n, 128).transpose(2, 1, 0).reshape(128, -1)

    wdt = i["even_w_in_2"][0][:, 4608:4640].reshape(8, 128, 32).transpose(1, 0, 2).reshape(128, 256)
    return np.concatenate([tiles(i["conv_w_dw"][0], 8), tiles(i["conv_b_dw"], 8), tiles(i["ssd_conv_w_2"][0], 16),
                           tiles(i["ssd_conv_b_2"], 16), wdt,
                           tiles(i["conv_ln_g"], 8), tiles(i["conv_ln_b"], 8)], axis=1)


def pack_bias(i):
    return np.concatenate([i["conv_b_in"][0].reshape(2, 4, 256).transpose(1, 0, 2).ravel(), i["conv_b_out"][0]])[None]


def build(nc, x_in, w_in, rows_in, small_in, cols_in, bias_in, rpb_in, cst_in, out, stop=None):
    ctx = ExitStack()
    with ctx:
        def sb(name, shape, dt=F32, stack=ctx):
            return stack.enter_context(nc.sbuf_tensor(name, shape, dt))

        sems = {}
        counts = {}

        def sem(key):
            sems[key] = ctx.enter_context(nc.semaphore("s_" + key))
            counts[key] = 0
            return key

        engines = {"pe": nc.tensor, "act": nc.scalar, "dve": nc.vector, "pool": nc.gpsimd, "sp": nc.sync}
        for e in ("pe", "act", "dve", "pool"):
            sem(e)
        passed = {e: {} for e in engines}

        def wait(e, *toks):
            for tok in toks:
                if tok is None:
                    continue
                key, n = tok
                if passed[e].get(key, 0) < n:
                    engines[e].wait_ge(sems[key], n)
                    passed[e][key] = n

        def signal(key, ins, n=1):
            counts[key] += n
            ins.then_inc(sems[key], n)
            return (key, counts[key])

        def A(after, out_, in_, func, **kw):
            wait("act", *after)
            return signal("act", nc.scalar.activation(out_, in_, func, **kw))

        def V(after, op, *a, **kw):
            wait("dve", *after)
            return signal("dve", op(*a, **kw))

        def G(after, op, *a, **kw):
            wait("pool", *after)
            return signal("pool", op(*a, **kw))

        TT, TS, STT = nc.vector.tensor_tensor, nc.vector.tensor_scalar, nc.vector.scalar_tensor_tensor

        def load(e, key, dst, src, after=()):
            wait(e, *after)
            return signal(key, engines[e].dma_start(dst, src), 16)

        def MM(o, l, r, start, stop, skip=False):
            return nc.tensor.matmul(o, l, r, start=start, stop=stop, skip_group_check=skip)

        def mm3(o, lh, ll, rh, rl, start, stop):
            MM(o, lh, rh, start, False)
            MM(o, lh, rl, False, False)
            return MM(o, ll, rh, False, stop)

        def done(ins):
            return signal("pe", ins)

        def spread(ap, at, n):
            dims = [list(d) for d in ap.ap]
            return bass.AP(tensor=ap.tensor, offset=ap.offset, ap=dims[:at] + [[0, n]] + dims[at:])

        ps = ctx.enter_context(nc.psum_tensor("ps", [128, 4096], F32))
        emptied = {b: [] for b in range(8)}

        def bank(b, n=1):
            return ps[:, 512 * b:512 * (b + n)]

        def after_emptied(*bs):
            for b in bs:
                wait("pe", *emptied[b])
                emptied[b] = []

        with ExitStack() as same:
            raw = sb("raw", [128, RAW, 2048], F32, same)
        wl = sb("wl", [128, RAW, 2048], F32R)
        wh = sb("wh", [128, RING, 2048], F32R)
        x = sb("x", [128, 2, D])
        xTh = sb("xTh", [128, 8, 2, 128], F32R)
        xTl = sb("xTl", [128, 8, 2, 128], F32R)
        gains = sb("gains", [128, NGAIN, D])
        xn = sb("xn", [128, 2, D])
        tmp = sb("tmp", [128, D])
        ident = sb("ident", [128, 128])
        cols = sb("cols", [128, N_COLS])
        small = sb("small", [128, N_SMALL])
        st = sb("st", [128, 512])
        mhalf = sb("mhalf", [128, 8])
        ones2 = sb("ones2", [2, 128], F32R)

        for n in range(RAW):
            sem(f"raw{n}")
        for n in range(NGAIN):
            sem(f"gain{n}")
        for n in ("x0", "x1", "ident", "cols", "small", "bias", "cst", "out", "nab0", "nab1"):
            sem(n)

        at = [0]

        def stat(n=1):
            a = at[0]
            at[0] += n
            assert at[0] <= 512
            return st[:, a:a + n]

        t_half = G([], nc.gpsimd.memset, mhalf[:, :], -0.5)
        x_v = x_in.rearrange("(t p) d -> p t d", p=128)
        t_x = [load("act", "x0", x[:, 0, :], x_v[:, 0, :])]
        t_ident = load("act", "ident", ident[:, :], cst_in[:, 0:128])
        t_x.append(load("act", "x1", x[:, 1, :], x_v[:, 1, :]))
        t_cols = load("act", "cols", cols[:, :], cols_in)

        n_pieces = w_in.shape[0]
        fetched, landed, split_done, multiplied = [0], {}, {}, {}

        def fetch():
            while fetched[0] < n_pieces and (fetched[0] < RAW or fetched[0] - RAW in multiplied):
                p = fetched[0]
                after = [multiplied[p - RAW]] if p >= RAW else []
                landed[p] = load("sp", f"raw{p % RAW}", raw[:, p % RAW, :], w_in[p], after)
                fetched[0] += 1

        n_split = [0]

        hi_done = {}

        def split_hi():
            p = n_split[0]
            fetch()
            after = [multiplied[p - RING]] if p >= RING else []
            hi_done[p] = A([landed[p], *after], wh[:, p % RING, :], raw[:, p % RAW, :], ACT.Copy)

        def split_lo(on=V):
            p = n_split[0]
            split_done[p] = on([hi_done[p]], TT if on is V else nc.gpsimd.tensor_tensor, wl[:, p % RAW, :], raw[:, p % RAW, :],
                               wh[:, p % RING, :].bitcast(F32), ALU.subtract)
            n_split[0] += 1

        def split():
            split_hi()
            split_lo()

        def room():
            fetch()
            return n_split[0] in landed and (n_split[0] < RING or n_split[0] - RING in multiplied)

        def top_up(n=RING):
            while n and room():
                split()
                n -= 1

        t_small = load("sp", "small", small[:, :], spread(small_in[0, :], 0, 128))

        g_at, g_tok, gain_applied = [0], {}, {}

        def gain_to(n):
            while g_at[0] < min(n, len(GAINS)):
                i = g_at[0]
                after = gain_applied[i - NGAIN] if i >= NGAIN else []
                g_tok[i] = load("sp", f"gain{i % NGAIN}", gains[:, i % NGAIN, :], spread(rows_in[i, :], 0, 128), after)
                g_at[0] += 1

        def gain(name):
            i = GAINS.index(name)
            return gains[:, i % NGAIN, :], g_tok[i], i

        def gain_next():
            while g_at[0] < len(GAINS) and g_at[0] - NGAIN in gain_applied:
                gain_to(g_at[0] + 1)

        gain_to(1)
        fetch()
        gain_to(NGAIN)
        piece = [0]

        def take(n):
            p = piece[0]
            piece[0] += n
            while n_split[0] < p + n:
                split()
            return p

        def parts(p, k):
            return (wh[:, p % RING, :].rearrange("p (k n) -> p k n", k=k),
                    wl[:, p % RAW, :].rearrange("p (k n) -> p k n", k=k))

        def wcols(p):
            return parts(p, 4)

        def wrows(p):
            return parts(p, 2)

        def project(p, t, b, act, act_tok, bias=None, mid=None):
            wait("pe", *act_tok[t])
            after_emptied(b)
            if bias is not None:
                MM(bank(b), ones2[:, :], bias, True, False)
            for half in range(2):
                wait("pe", split_done[p + half])
                H, L = wcols(p + half)
                for k in range(4):
                    kk = 4 * half + k
                    last = mm3(bank(b), act[0][:, kk, t, :], act[1][:, kk, t, :], H[:, k, :], L[:, k, :],
                               kk == 0 and bias is None, kk == 7)
                tok = done(last)
                if t == 1:
                    multiplied[p + half] = tok
                if half == 0 and mid:
                    mid()
                    wait("pe", *act_tok[t])
            return tok

        def project_t(p, act, act_tok, b0):
            wait("pe", *act_tok[0], *act_tok[1], split_done[p], split_done[p + 1])
            toks = []
            for n in range(4):
                b = b0 + n // 2
                if n % 2 == 0:
                    after_emptied(b)
                o = bank(b)[:, 256 * (n % 2):256 * (n % 2) + 256]
                for kk in range(8):
                    H, L = wcols(p + kk // 4)
                    a, c = H[:, kk % 4, 128 * n:128 * n + 128], L[:, kk % 4, 128 * n:128 * n + 128]
                    MM(o, a, act[0][:, kk, :, :], kk == 0, False)
                    MM(o, c, act[0][:, kk, :, :], False, False)
                    last = MM(o, a, act[1][:, kk, :, :], False, kk == 7)
                if n % 2 == 1:
                    toks.append(done(last))
            multiplied[p] = multiplied[p + 1] = toks[1]
            return toks

        def down(p, t, lhs, first, last_, toks=(), mid=None):
            wait("pe", split_done[p], *toks)
            if first:
                after_emptied(2 * t, 2 * t + 1)
            H, L = wrows(p)
            for k in range(2):
                if k and mid:
                    mid()
                for half in range(2):
                    r = slice(512 * half, 512 * half + 512)
                    m = mm3(bank(2 * t + half), lhs(k)[0], lhs(k)[1], H[:, k, r], L[:, k, r],
                            first and k == 0, last_ and k == 1)
            tok = done(m)
            if t == 1:
                multiplied[p] = tok
            return tok

        x_tok = list(t_x)
        xn_turned = [[], []]
        tmp_added = [[]]

        def rstd(tok, ss, mul, add, n=1):
            v, r = stat(n), stat(n)
            g = G([tok], nc.gpsimd.tensor_scalar, v, ss, mul, add, ALU.mult, ALU.add)
            return G([g, t_half], nc.gpsimd.tensor_tensor, r, v, mhalf[:, 0:n], ALU.pow), r

        def post(t, tok, name, half):
            a = bank(2 * t, 2)
            if name is None:
                x_tok[t] = V([tok, x_tok[t]], TT, x[:, t, :], x[:, t, :], a, ALU.add)
                emptied[2 * t] = emptied[2 * t + 1] = [x_tok[t]]
                return
            ss = stat()
            s = A([tok, *tmp_added[0]], tmp[:, :], a, ACT.Square, accum_out=ss)
            m = 4.0 if half else 1.0
            g, r = rstd(s, ss, m / D, m * 1e-6)
            ga, gt, gi = gain(name)
            v = V([g, gt] + tmp_added[0], STT, tmp[:, :], a, r, ga, ALU.mult, ALU.mult)
            emptied[2 * t] = emptied[2 * t + 1] = [v]
            gain_applied[gi] = [v]
            x_tok[t] = V([v, x_tok[t]], TT, x[:, t, :], x[:, t, :], tmp[:, :], ALU.add)
            tmp_added[0] = [x_tok[t]]

        def transposed(src, n, b, after):
            wait("pe", t_ident, *after)
            after_emptied(b)
            for k in range(n):
                m = nc.tensor.transpose(bank(b)[:, 128 * k:128 * k + 128], src(k), ident[:, :])
            return done(m)

        def hilo(b, src, dh, dl, tok, after=()):
            h = A([tok, *after], dh, src, ACT.Copy)
            v = V([h], TT, dl, src, dh.bitcast(F32), ALU.subtract)
            emptied[b] = [v]
            return v

        def flip(t, src, tok, act, after=(), b0=6):
            toks = []
            for b in range(2):
                tr = transposed(lambda k: src[:, 512 * b + 128 * k:512 * b + 128 * k + 128], 4, b0 + b, [tok])
                s = bank(b0 + b).rearrange("p (k n) -> p k n", k=4)
                toks.append(hilo(b0 + b, s, act[0][:, 4 * b:4 * b + 4, t, :], act[1][:, 4 * b:4 * b + 4, t, :], tr, after))
            return tr, toks

        def norm_stat(t):
            ss = stat()
            s = A([x_tok[t], *xn_turned[t]], xn[:, t, :], x[:, t, :], ACT.Square, accum_out=ss)
            return rstd(s, ss, 1.0 / D, 1e-6)

        xn_ready = [None, None]
        x_stats = [None, None]

        def pre_scale(t, name, stats=None):
            g, rs = stats or norm_stat(t)
            x_stats[t] = (g, rs)
            ga, gt, gi = gain(name)
            xn_ready[t] = V([g, gt, x_tok[t]] + xn_turned[t], STT, xn[:, t, :], x[:, t, :], rs, ga, ALU.mult, ALU.mult)
            gain_applied[gi] = [xn_ready[t]]

        def pre_turn(t, act, after=()):
            tr, toks = flip(t, xn[:, t, :], xn_ready[t], act, after)
            xn_turned[t] = [tr]
            return toks

        xT = (xTh, xTl)
        ready = [None, None]
        xT_multiplied = [[]]

        def ffn(tag, ph_w, post_name, half, pre_name, beside=None):
            ph = ExitStack()
            with ph:
                hTh = sb(f"hTh{tag}", [128, 2, 2, 2, 128], F32R, ph)
                hTl = sb(f"hTl{tag}", [128, 2, 2, 2, 128], F32R, ph)
                sg = sb(f"sg{tag}", [128, 2, 2, 256], F32, ph)
                hb = sb(f"hb{tag}", [128, 2, 2, 256], F32, ph)
                hT_multiplied, hb_turned, h_tok, hT_tok = {}, {}, {}, {}

                def act_of(j, t, b, tok):
                    a = bank(b)
                    s = A([tok, *hb_turned.get((j - 2, t), ()), *ph_w], sg[:, j % 2, t, :], a[:, 0:256], ACT.Silu)
                    h_tok[j, t] = V([s], TT, hb[:, j % 2, t, :], sg[:, j % 2, t, :], a[:, 256:512], ALU.mult)
                    emptied[b] = [h_tok[j, t]]

                def turn(j, ts):
                    b = 6 + (j + ts[0]) % 2
                    after_emptied(b)
                    wait("pe", t_ident, *[h_tok[j, t] for t in ts])
                    for ft in range(2):
                        for t in ts:
                            m = nc.tensor.transpose(bank(b)[:, 256 * ft + 128 * t:256 * ft + 128 * t + 128],
                                                    hb[:, j % 2, t, 128 * ft:128 * ft + 128], ident[:, :])
                    tr = done(m)
                    for t in ts:
                        hb_turned[j, t] = [tr]
                    u = slice(ts[0], ts[-1] + 1)
                    src = bank(b).rearrange("p (f t n) -> p f t n", f=2, t=2)[:, :, u, :]
                    v = hilo(b, src, hTh[:, j % 2, :, u, :], hTl[:, j % 2, :, u, :], tr, hT_multiplied.get(j - 2, ()))
                    for t in ts:
                        hT_tok[j, t] = v

                def dn(j, p, t, mid=None):
                    tok = down(p, t, lambda k: (hTh[:, j % 2, k, t, :], hTl[:, j % 2, k, t, :]), j == 0,
                               j == NJ - 1, [hT_tok[j, t]], mid)
                    if t == 1:
                        hT_multiplied[j] = [tok]
                    return tok

                pair(xT, ready, turn1, act_of, lambda: turn(0, [0, 1]), fresh=(1, 2, 1, 5))
                q = take(1)
                dn(0, q, 0)
                turn(1, [0, 1])
                dn(0, q, 1)
                for j in range(2, NJ - 1):
                    p = take(2)
                    for t in range(2):
                        act_of(j, t, 4 + t, project(p, t, 4 + t, xT, ready))
                    top_up(2)
                    q = take(1)
                    dn(j - 1, q, 0)
                    turn(j, [0, 1])
                    dn(j - 1, q, 1)
                    top_up(1)
                    if beside:
                        beside(j)
                j = NJ - 1
                p = take(4)

                def close(t, before_last):
                    tok = project(p, t, 4 + t, xT, ready)
                    act_of(j, t, 4 + t, tok)
                    if t == 1:
                        xT_multiplied[0] = [tok]
                    dn(j - 1, p + 2, t, lambda: turn(j, [t]))
                    before_last()
                    top_up(1)
                    return dn(j, p + 3, t)

                seam(close, post_name, half, pre_name)

        def seam(close, post_name, half, pre_name):
            def turn0():
                next_ready.append(pre_turn(0, xT, xT_multiplied[0]))

            next_ready = []
            for t in range(2):
                tok = close(t, turn0 if t == 1 and pre_name else lambda: None)
                if next_ready:
                    ready[0] = next_ready[0]
                post(t, tok, post_name, half)
                if t == 1:
                    top_up(1)
                if pre_name:
                    pre_scale(t, pre_name)
            gain_next()

        def turn1():
            ready[1] = pre_turn(1, xT, xT_multiplied[0])

        def pair(act, act_ready, between, taken, later=None, bias=None, fresh=(2, 2, 2, 2)):
            p = take(2)
            for t in range(2):
                for j in range(2):
                    if t == 0 and j == 1:
                        take(2)
                    b = 4 * (1 - t) + j
                    tok = project(p + 2 * j, t, b, act, act_ready, bias(j) if bias else None,
                                  (between, later)[t] if j else None)
                    taken(j, t, b, tok)
                    top_up(fresh[2 * t + j])

        def write_out():
            for t in range(2):
                tk = load("sp", "out", out.rearrange("(t p) d -> p t d", p=128)[:, t, :], x[:, t, :], [x_tok[t]])
            wait("sp", tk)
            for key in counts:
                if counts[key]:
                    wait("sp", (key, counts[key]))

        def bounds():
            return list(ready[0])

        pre_scale(0, "pre00")
        ready[0] = pre_turn(0, xT)
        top_up(2)
        pre_scale(1, "pre00")
        top_up(2)
        ph0 = ExitStack()
        ctx.enter_context(ph0)
        brow = sb("brow", [2, 3072], F32, ph0)
        bhl = sb("bhl", [2, 3072], F32R, ph0)
        t_b = load("act", "bias", brow[:, :], spread(bias_in[0, :], 0, 2))
        t_one = V([t_ident], TS, ones2[:, :], ident[0:2, :], 0.0, 1.0, ALU.mult, ALU.add)
        bias_split = []

        def bias_rows(j):
            if j < 8:
                u = slice(512 * j - 1024, 512 * j - 512)
                h = A([t_b], bhl[:, u], brow[:, u], ACT.Copy)
                v = V([h], TT, brow[:, u], brow[:, u], bhl[:, u].bitcast(F32), ALU.subtract)
                v = V([v, t_ident], TS, brow[:, u], brow[:, u], ident[0:2, 1:2], None, ALU.mult)
                bias_split.append(V([v], STT, bhl[:, u], bhl[:, u].bitcast(F32), ident[0:2, 0:1], brow[:, u], ALU.mult, ALU.add))

        ffn("a", [], "post00", True, "mixpre0", bias_rows)
        if stop == "ffn0":
            return write_out()

        ph = ExitStack()
        with ph:
            PADL = TAPS - 1
            W = PADL + 256
            uT = sb("uT", [128, 8, W], F32, ph)
            ca = sb("ca", [128, 8, 256], F32, ph)
            sg = sb("csg", [128, 2, 2, 256], F32, ph)
            ub = sb("cub", [128, 2, 2, 256], F32, ph)
            ya = sb("ya", [128, 2, D], F32, ph)
            e0 = bounds()
            t_z = G(e0, nc.gpsimd.memset, uT[:, :, 0:PADL], 0.0)
            wait("pe", t_one, *bias_split)
            ub_turned = {}
            dw0, dwb = COLS["dw"][0], COLS["dwb"][0]
            ca_tok = {}

            diag = sb("cdg", [128, 8, 128], F32, ph)
            odd = sb("cod", [128, 256], F32, ph)
            prod = sb("cpr", [128, 2, 256], F32, ph)
            SHARED = 13
            shared = [None]
            odd_added, diag_multiplied = [[]], {}
            taps, u_turned, n_diag = [], {}, [0]

            def tap_column(c, k):
                return cols[:, dw0 + TAPS * c + k:dw0 + TAPS * c + k + 1]

            def vector_tap(c, k, sums):
                if k == TAPS:
                    ca_tok[c] = V([sums[0], sums[1]], TT, ca[:, c, :], ca[:, c, :], odd[:, :], ALU.add)
                    odd_added[0] = [ca_tok[c]]
                    if c == 6:
                        ca_tok[6] = V([ca_tok[6], shared[0]], TT, ca[:, c, :], ca[:, c, :], bank(6)[:, 0:256], ALU.add)
                        emptied[6] = [ca_tok[6]]
                    return
                src, dst = uT[:, c, k:k + 256], (ca[:, c, :], odd[:, :])[k % 2]
                first = [t_z, t_cols, *e0, u_turned[c // 2]]
                if k == 0:
                    v = V(first, TS, dst, src, tap_column(c, k), cols[:, dwb + c:dwb + c + 1], ALU.mult, ALU.add)
                elif k == 1:
                    v = V([*first, *odd_added[0]], TS, dst, src, tap_column(c, k), None, ALU.mult)
                else:
                    v = V([sums[k % 2]], STT, dst, src, tap_column(c, k), dst, ALU.mult, ALU.add)
                sums[k % 2] = v

            def tap_some(n):
                for args in taps[:n]:
                    vector_tap(*args)
                del taps[:n]

            def conv_pool(c):
                first, added = [t_z, t_cols, *e0, u_turned[c // 2]], {}
                for k in range(TAPS):
                    src = uT[:, c, k:k + 256]
                    if k == 0:
                        g = G(first, nc.gpsimd.tensor_scalar, ca[:, c, :], src, tap_column(c, k),
                              cols[:, dwb + c:dwb + c + 1], ALU.mult, ALU.add)
                    else:
                        m = G([*first, *added.get(k - 2, ())], nc.gpsimd.tensor_scalar, prod[:, k % 2, :], src,
                              tap_column(c, k), None, ALU.mult)
                        g = G([m, g], nc.gpsimd.tensor_tensor, ca[:, c, :], ca[:, c, :], prod[:, k % 2, :], ALU.add)
                        added[k] = [g]
                ca_tok[c] = g

            def diagonals(c, dst, first):
                for k in range(first, TAPS):
                    n = n_diag[0]
                    n_diag[0] += 1
                    d = A([t_ident, t_cols, *e0, *diag_multiplied.get(n - 8, ())], diag[:, n % 8, :], ident[:, :],
                          ACT.Copy, scale=tap_column(c, k))
                    wait("pe", d)
                    tok = done(MM(dst, diag[:, n % 8, :], uT[:, c, k:k + 256], k == first, k == TAPS - 1))
                    diag_multiplied[n] = [tok]
                return tok

            def conv_diagonal(c):
                b = 2 + c // 2 % 2
                after_emptied(b)
                wait("pe", t_z, u_turned[c // 2])
                tok = diagonals(c, bank(b)[:, 0:256], 0)
                ca_tok[c] = A([tok], ca[:, c, :], bank(b)[:, 0:256], ACT.Identity, bias=cols[:, dwb + c:dwb + c + 1])
                emptied[b] = [ca_tok[c]]

            def conv_part(j, e):
                u_turned[j] = e
                sums = [None, None]
                taps.extend((2 * j, k, sums) for k in range(TAPS + 1) if j < 3 or k < SHARED or k == TAPS)
                if j == 0:
                    conv_pool(1)
                else:
                    conv_diagonal(2 * j + 1)

            u_tok = {}

            def glu(j, t, b, tok):
                a = bank(b)
                s = A([tok, *ub_turned.get((j - 2, t), ()), *e0], sg[:, j % 2, t, :], a[:, 256:512], ACT.Sigmoid)
                u_tok[j, t] = V([s], TT, ub[:, j % 2, t, :], sg[:, j % 2, t, :], a[:, 0:256], ALU.mult)
                emptied[b] = [u_tok[j, t]]

            def conv_in(j):
                b = 6 + j % 2
                after_emptied(b)
                wait("pe", u_tok[j, 0], u_tok[j, 1])
                for c in range(2):
                    for t in range(2):
                        m = nc.tensor.transpose(bank(b)[:, 256 * c + 128 * t:256 * c + 128 * t + 128],
                                                ub[:, j % 2, t, 128 * c:128 * c + 128], ident[:, :])
                tr = done(m)
                ub_turned[j, 0] = ub_turned[j, 1] = [tr]
                e = A([tr, *e0], uT[:, 2 * j:2 * j + 2, PADL:W], bank(b).rearrange("p (c n) -> p c n", c=2), ACT.Copy)
                emptied[b] = [e]
                return e

            pair(xT, ready, turn1, glu, lambda: conv_part(0, conv_in(0)), lambda j: bhl[:, 512 * j:512 * j + 512])
            tap_some(8)
            p = take(4)
            for j in (2, 3):
                for t in range(2):
                    tok = project(p + 2 * j - 4, t, 4 + t, xT, ready, bhl[:, 512 * j:512 * j + 512],
                                  None if t else lambda: conv_part(j - 1, conv_in(j - 1)))
                    glu(j, t, 4 + t, tok)
                    tap_some(14)
                    if j == 2 or t:
                        top_up(1)
            conv_part(3, conv_in(3))
            after_emptied(6)
            shared[0] = diagonals(6, bank(6)[:, 0:256], SHARED)
            A([t_half], stat(), mhalf[:, 0:1], ACT.Silu)
            tap_some(len(taps))
            xT_multiplied[0] = [tok]
            normed = [None, None]
            for t in range(2):
                after_emptied(2 * t, 2 * t + 1)
            turned = [None, None]
            for cs in ((0, 1, 2, 3, 4, 5, 7), (6,)):
                for t in range(2):
                    for c in cs:
                        wait("pe", ca_tok[c])
                        m = nc.tensor.transpose(bank(2 * t, 2)[:, 128 * c:128 * c + 128],
                                                ca[:, c, 128 * t:128 * t + 128], ident[:, :])
                    turned[t] = done(m)
            lg0, lb0 = COLS["lng"][0], COLS["lnb"][0]
            for t in range(2):
                bs, mv, nm = stat(12), stat(2), stat()
                for h in range(2):
                    b = V([turned[t]], nc.vector.bn_stats, bs[:, 6 * h:6 * h + 6], bank(2 * t + h))
                b = V([b], nc.vector.bn_aggr, mv, bs)
                g, r = rstd(b, mv[:, 1:2], 1.0, 1e-5)
                n = V([g], STT, nm, mv[:, 0:1], -1.0, r, ALU.mult, ALU.mult)
                a = A([n, *e0], ya[:, t, :], bank(2 * t, 2), ACT.Identity, bias=nm, scale=r)
                emptied[2 * t] = emptied[2 * t + 1] = [a]
                normed[t] = a

            def conv_turn(t):
                toks = []
                for b in range(2):
                    tr = transposed(lambda k: ya[:, t, 512 * b + 128 * k:512 * b + 128 * k + 128], 4, 6 + b, [normed[t]])
                    u = xn[:, t, 512 * b:512 * b + 512].rearrange("p (k n) -> p k n", k=4)
                    for k in range(4):
                        c = 4 * b + k
                        a = A([tr, t_cols, *xn_turned[t]], u[:, k, :], bank(6 + b)[:, 128 * k:128 * k + 128], ACT.Silu,
                              bias=cols[:, lb0 + c:lb0 + c + 1], scale=cols[:, lg0 + c:lg0 + c + 1])
                    emptied[6 + b] = [a]
                    h = A([a, *xT_multiplied[0]], xTh[:, 4 * b:4 * b + 4, t, :], u, ACT.Copy)
                    toks.append(V([h], TT, xTl[:, 4 * b:4 * b + 4, t, :], u, xTh[:, 4 * b:4 * b + 4, t, :].bitcast(F32), ALU.subtract))
                xn_turned[t] = toks
                return toks

            def begin(t):
                ready[t] = conv_turn(t)
                after_emptied(2 * t, 2 * t + 1)
                for h in range(2):
                    MM(bank(2 * t + h), ones2[:, :], bhl[:, 2048 + 512 * h:2560 + 512 * h], True, False)

            begin(0)
            p = take(4)

            def close(t, before_last):
                for q in range(4):
                    if q % 2 == 0:
                        wait("pe", ready[t][q // 2])
                    if q == 3:
                        before_last()
                    if t == 0 and q == 1:
                        begin(1)
                    wait("pe", split_done[p + q])
                    H, L = wrows(p + q)
                    for k in range(2):
                        kk = 2 * q + k
                        for h in range(2):
                            m = mm3(bank(2 * t + h), xTh[:, kk, t, :], xTl[:, kk, t, :], H[:, k, 512 * h:512 * h + 512],
                                    L[:, k, 512 * h:512 * h + 512], False, kk == 7)
                    tok = done(m)
                    if t == 1:
                        multiplied[p + q] = tok
                        if q in (2, 3):
                            top_up(1)
                if t == 1:
                    xT_multiplied[0] = [tok]
                return tok

            seam(close, "mixpost0", False, "pre01")
        if stop == "conv":
            return write_out()
        ph0.close()
        ffn("b", bounds(), "post01", True, "pre10")
        ffn("c", bounds(), "post10", True, "kv")
        if stop == "ffn10":
            return write_out()

        def attention(tag, ph, n_pairs, M, W, q_of, k_of, v_of, v_tok, bias, oT, e0, beside, pool_from=99):
            sc = sb(f"sc{tag}", [128, 3, 2, 2, 256], F32, ph)
            PT = sb(f"PT{tag}", [128, 2, 2, 2, 256], F32, ph)
            p_turned = {}
            pt_multiplied = {}
            o_tok = None

            def scores(i):
                u, s = i % 3, 2 * (i % 2)
                after_emptied(s, s + 1)
                for t in range(2):
                    for hh in range(2):
                        l, lt = q_of(2 * i + hh, t)
                        r, rt = k_of(2 * i + hh, W[t])
                        wait("pe", *lt, *rt)
                        m = MM(bank(s + hh)[:, 256 * t:256 * t + W[t]], l, r, True, True)
                tok = done(m)
                after = [tok, *p_turned.get(i - 3, ()), *e0]
                bufs_of, biased, peak, tops = {}, {}, {}, []
                for t in range(2):
                    P = sc[:, u, t, :, 0:W[t]]
                    S = bank(s, 2).rearrange("p (h t n) -> p h t n", h=2, t=2)[:, :, t, 0:W[t]]
                    biased[t] = bias(i, t, P, S, after) if bias else tok
                    bufs_of[t] = P, P if bias else S, *stat2(t, u)
                    peak[t] = V([biased[t]], nc.vector.tensor_reduce, bufs_of[t][2], bufs_of[t][1], AX.X, ALU.max, negate=True)
                for t in range(2):
                    P, src, mx, sm, rc = bufs_of[t]
                    for hh in range(2):
                        a = A([peak[t] if bias else peak[1], *after], P[:, hh, :], src[:, hh, :], ACT.Exp, bias=mx[:, hh:hh + 1],
                              accum_out=sm[:, hh:hh + 1])
                    tops.append(a)
                for b in (s, s + 1):
                    emptied[b] = [biased[1] if bias else a]
                return [bufs_of[t] + (tops[t],) for t in range(2)]

            def scaled(parts_of):
                toks = []
                for P, _, _, sm, rc, a in parts_of:
                    r = V([a], nc.vector.reciprocal, rc, sm)
                    for hh in range(2):
                        v = V([r], TS, P[:, hh, :], P[:, hh, :], rc[:, hh:hh + 1], None, ALU.mult)
                    toks.append(v)
                return toks

            def turned(i, toks):
                s, u = i % 2, i % 3
                pt = []
                for kk in range(2):
                    ts = [t for t in range(2) if W[t] > 128 * kk]
                    after_emptied(4 + kk)
                    wait("pe", *toks)
                    for hh in range(2):
                        for t in ts:
                            m = nc.tensor.transpose(bank(4 + kk)[:, 256 * hh + 128 * t:256 * hh + 128 * t + 128],
                                                    sc[:, u, t, hh, 128 * kk:128 * kk + 128], ident[:, :])
                    tr = done(m)
                    lo = 128 * ts[0]
                    src = bank(4 + kk).rearrange("p (h n) -> p h n", h=2)[:, :, lo:256]
                    dst = PT[:, s, kk, :, lo:256]
                    w = [tr, *pt_multiplied.get(i - 2, ()), *e0]
                    e = A(w, dst, src, ACT.Copy)
                    emptied[4 + kk] = [e]
                    pt.append((e, lo))
                p_turned[i] = [tr]
                return pt

            def values(i, pt):
                s, ob = i % 2, 6 + i % 2
                after_emptied(ob)
                wait("pe", *v_tok)
                for hh in range(2):
                    o = bank(ob)[:, 256 * hh:256 * hh + 256] if M == 128 else bank(ob)[64 * hh:64 * hh + 64, 0:256]
                    for kk in range(2):
                        e, lo = pt[kk]
                        wait("pe", e)
                        m = MM(o[:, lo:256], v_of(2 * i + hh, kk), PT[:, s, kk, hh, lo:256], kk == 0, kk == 1)
                tok = done(m)
                pt_multiplied[i] = [tok]
                if M == 128:
                    src = bank(ob).rearrange("p (h t n) -> p h t n", h=2, t=2)
                    d = slice(2 * i, 2 * i + 2)
                    return hilo(ob, src, oT[0][:, d, :, :], oT[1][:, d, :, :], tok, [*e0, *xT_multiplied[0]])
                src = bank(ob)[:, 0:256].rearrange("p (t n) -> p t n", t=2)
                return hilo(ob, src, oT[0][:, i, :, :], oT[1][:, i, :, :], tok, [*e0, *xT_multiplied[0]])

            bufs = sb(f"sm{tag}", [128, 36], F32, ph)

            def stat2(t, s):
                a = 12 * s + 6 * t
                return bufs[:, a:a + 2], bufs[:, a + 2:a + 4], bufs[:, a + 4:a + 6]

            toks, pts, outs = {}, {}, []
            for i in range(n_pairs + 3):
                if 1 <= i <= n_pairs:
                    toks[i - 1] = scaled(toks[i - 1])
                ahead = room()
                if ahead:
                    split_hi()
                if i < n_pairs:
                    toks[i] = scores(i)
                if ahead:
                    split_lo(V if i < pool_from else G)
                if 2 <= i < n_pairs + 2:
                    pts[i - 2] = turned(i - 2, toks[i - 2])
                if i >= 3:
                    outs.append(values(i - 3, pts[i - 3]))
                if i in beside:
                    beside[i]()
            return outs

        def close_with(p, o_tok, first_act=None):
            def close(t, before_last):
                for q in range(4):
                    if q == 3:
                        before_last()
                    tok = down(p + q, t, lambda k: (xTh[:, 2 * q + k, t, :], xTl[:, 2 * q + k, t, :]),
                               q == 0 and first_act is None, q == 3, o_tok[t])
                    if t == 1 and q in (2, 3):
                        top_up(1)
                if t == 1:
                    xT_multiplied[0] = [tok]
                return tok
            return close

        ph = ExitStack()
        with ph:
            qh = sb("qh", [128, 8, 2, 128], F32R, ph)
            ql = sb("ql", [128, 8, 2, 128], F32R, ph)
            kT = sb("kT", [128, 8, 256], F32, ph)
            qT = sb("qT", [128, 8, 256], F32, ph)
            vv = sb("vv", [128, 2, D], F32, ph)
            dm = sb("dm", [128, 2, 256], F32, ph)
            e0 = bounds()
            a0 = CST["dm"][0]
            t_dm = load("sp", "cst", dm[:, :, :], cst_in[:, a0:a0 + 512].rearrange("p (t n) -> p t n", t=2), e0)
            v_tok = []

            def keep_v(j, t, b, tok):
                v_tok.append(A([tok, *e0], vv[:, t, 512 * j:512 * j + 512], bank(b), ACT.Copy))
                emptied[b] = [v_tok[-1]]

            qready = [None, None]

            def q_scale():
                turn1()
                for t in range(2):
                    pre_scale(t, "mixpre1", x_stats[t])

            def q_turned(t):
                qready[t] = pre_turn(t, (qh, ql), e0)

            pair(xT, ready, q_scale, keep_v, lambda: q_turned(0))
            gain_next()

            def heads_t(toks, j, dst, act, tok, scale, b0):
                p = take(2)
                for n, m in enumerate(project_t(p, act, tok, b0)):
                    h = 4 * j + 2 * n
                    e = A([m, *e0], dst[:, h:h + 2, :], bank(b0 + n).rearrange("p (h n) -> p h n", h=2), ACT.Copy, scale=scale)
                    emptied[b0 + n] = [e]
                    toks[h] = toks[h + 1] = e

            q_turned(1)
            k_tok, q_tok = {}, {}
            for j in range(2):
                heads_t(k_tok, j, kT, xT, ready, 1.0, 4 - 4 * j)
                top_up(2)
            xT_multiplied[0] = [("pe", counts["pe"])]

            def heads_q(j, b0):
                heads_t(q_tok, j, qT, (qh, ql), qready, float(128 ** -0.5), b0)

            heads_q(0, 4)

            def alibi(i, t, P, S, after):
                n = P.shape[2]
                for hh in range(2):
                    v = V([t_dm, *after], STT, P[:, hh, :], dm[:, t, 0:n], -float(2.0 ** -(2 * i + hh + 1)), S[:, hh, :],
                          ALU.mult, ALU.add)
                return v

            o_tok = attention("a", ph, 4, 128, [128, 256],
                              lambda h, t: (qT[:, h, 128 * t:128 * t + 128], [q_tok[h]]),
                              lambda h, n: (kT[:, h, 0:n], [k_tok[h]]),
                              lambda h, kk: vv[:, kk, 128 * h:128 * h + 128], v_tok, alibi, xT, e0, {1: lambda: heads_q(1, 6)}, 0)
            seam(close_with(take(4), [o_tok, o_tok]), "mixpost1", False, "pre11")
        if stop == "attn":
            return write_out()
        ffn("d", bounds(), "post11", True, "evenmix")
        if stop == "ffn11":
            return write_out()

        def head_stat(src, n, dst, tok, after, mul, add):
            ss, v, r = stat(n), stat(n), stat(n)
            s = A([tok, *after], dst, src.rearrange("p (h d) -> p h d", d=64), ACT.Square)
            s = V([s], nc.vector.tensor_reduce, ss, dst, AX.X, ALU.add)
            g = G([s], nc.gpsimd.tensor_scalar, v, ss, mul, add, ALU.mult, ALU.add)
            return G([g, t_half], nc.gpsimd.tensor_tensor, r, v, mhalf[:, 0:n], ALU.pow), r

        def head_scale(src, dst, factors):
            g, r = factors
            return V([g], TT, dst, src.rearrange("p (h d) -> p h d", d=64), spread(r, 2, 64), ALU.mult)

        def head_norm(src, n, gname, dst, tok, after, mul, add):
            factors = head_stat(src, n, dst, tok, after, mul, add)
            top_up(1)
            v1 = head_scale(src, dst, factors)
            if gname is None:
                return v1, v1
            a0 = SMALL[gname][0]
            return v1, V([v1, t_small], TT, dst, dst, spread(small[:, a0:a0 + 64], 1, n), ALU.mult)

        ph = ExitStack()
        with ph:
            oTh = sb("oTh", [128, 4, 2, 128], F32R, ph)
            oTl = sb("oTl", [128, 4, 2, 128], F32R, ph)
            zs = sb("zs", [128, 2, D], F32, ph)
            xc = sb("xc", [128, 16, 256], F32, ph)
            dz = sb("dz", [128, 8, 64], F32, ph)
            nac = sb("nac", [128, 64], F32, ph)
            e0 = bounds()
            xw = [*e0]
            ph2 = ExitStack()
            with ph2:
                kTn = sb("kTn", [128, 4, 256], F32, ph2)
                qTn = sb("qTn", [128, 4, 256], F32, ph2)
                vn = sb("vn", [128, 2, 512], F32, ph2)
                ph3 = ExitStack()
                ctx.enter_context(ph3)
                nabr = sb("nabr", [128, 2, 2, 256], F32, ph2)
                win = sb("win", [128, 2, 64], F32, ph2)
                a0 = CST["win"][0]
                t_win = load("sp", "cst", win[:, :, :], cst_in[:, a0:a0 + 128].rearrange("p (a n) -> p a n", a=2), e0)
                xp = sb("xp", [128, 4, 260], F32, ph3)
                qn = sb("qn", [128, 2, 2, 512], F32, ph3)
                t_z = G(e0, nc.gpsimd.memset, xp[:, :, 0:2], 0.0)
                t_z = G(e0, nc.gpsimd.memset, xp[:, :, 258:260], 0.0)
                wd = cols[:, COLS["wdt"][0]:COLS["wdt"][0] + 256].rearrange("p (k n) -> p k n", k=8)
                wdh = sb("wdh", [128, 8, 32], F32R, ph3)
                wdl = sb("wdl", [128, 8, 32], F32R, ph3)
                dtT = sb("dtT", [32, 256], F32, ph3)
                h = A([t_cols, *e0], wdh[:, :, :], wd, ACT.Copy)
                t_wd = V([h], TT, wdl[:, :, :], wd, wdh[:, :, :].bitcast(F32), ALU.subtract)
                qk_normed, qk_tok = {}, {}

                def qk_norm(j, t, b, tok):
                    mul, add = (1.0 / 64, 1e-6) if j else (1.0, 64e-6)
                    name = "nak" if j else "naq"
                    v1, v2 = head_norm(bank(b), 8, name, qn[:, j, t, :].rearrange("p (h d) -> p h d", d=64),
                                          tok, e0, mul, add)
                    emptied[b] = [v1]
                    qk_normed[j, t] = v2

                def qk_turn(j, t):
                    dst = kTn if j else qTn
                    b = 6 + (j + t) % 2
                    tr = transposed(lambda k: qn[:, j, t, 128 * k:128 * k + 128], 4, b, [qk_normed[j, t]])
                    e = A([tr, *e0], dst[:, :, 128 * t:128 * t + 128], bank(b).rearrange("p (k n) -> p k n", k=4), ACT.Copy)
                    emptied[b] = [e]
                    qk_tok[j, t] = e

                pair(xT, ready, turn1, qk_norm, fresh=(0, 0, 0, 0))
                nab = xn[:, :, :].rearrange("p s (t h k) -> p s t h k", t=2, h=2)
                nab_added, nab_win = {}, {}

                def nab_load(i):
                    for r in range(4):
                        for j in range(4):
                            off = 2 * i * 465 + (j - r + 7) * 31 - 48
                            src = bass.AP(tensor=rpb_in.tensor, offset=off, ap=[[1, 64], [465, 2], [1, 64]])
                            dst = nabr[64 * (r % 2):64 * (r % 2) + 64, r // 2, :, 64 * j:64 * j + 64]
                            nab_in[i] = load("sp", f"nab{i % 2}", dst, src, [*e0, *nab_read.get(i - 1, ())])

                def nab_mask(i):
                    s, tok = i % 2, nab_in[i]
                    for t in range(2):
                        B = nabr[:, t, :, :]
                        rev = bass.AP(tensor=B.tensor, offset=B.offset + 63, ap=[list(B.ap[0]), [64, 8], [-1, 64]])
                        N8 = nab[:, s, t, :, :].rearrange("p h (j c) -> p (h j) c", c=64)
                        g = G([tok, t_win, *xn_turned[s]], nc.gpsimd.tensor_tensor, N8, rev, spread(win[:, 0, :], 1, 8), ALU.mult)
                        nab_win[i, t] = G([g], nc.gpsimd.tensor_tensor, N8, N8, spread(win[:, 1, :], 1, 8), ALU.add)
                    nab_read[i] = [g]

                nab_read = {}
                nab_in = {}
                nab_load(0)
                nab_mask(0)
                after_emptied(2)
                wait("pe", t_wd, *ready[0], *ready[1])
                for k in range(8):
                    m = mm3(bank(2)[0:32, 0:256], wdh[:, k, :], wdl[:, k, :], xTh[:, k, :, :], xTl[:, k, :, :], k == 0, k == 7)
                t_dtT = A([done(m), *e0], dtT[:, :], bank(2)[0:32, 0:256], ACT.Copy)
                emptied[2] = [t_dtT]
                db = small[:, SMALL["dtb"][0]:SMALL["dtb"][0] + 32]
                al = small[:, SMALL["alog"][0]:SMALL["alog"][0] + 32]
                d = [dz[:, i, :] for i in range(8)]
                d3 = [dz[:, i, :].rearrange("p (t n) -> p t n", t=2) for i in range(8)]

                def dt_turn():
                    after_emptied(3)
                    wait("pe", t_dtT)
                    for t in range(2):
                        m = nc.tensor.transpose(bank(3)[:, 32 * t:32 * t + 32], dtT[:, 128 * t:128 * t + 128], ident[0:32, 0:32])
                    v = V([done(m), t_small, *e0], TT, d3[0], bank(3)[:, 0:64].rearrange("p (t n) -> p t n", t=2), spread(db, 1, 2), ALU.add)
                    emptied[3] = [v]
                    return v

                xp_convolved = {0: [], 1: []}
                xc_tok = {}
                cw0, cb0 = COLS["cw"][0], COLS["cb"][0]
                for c in range(4):
                    p = take(2)
                    top_up(2)
                    for n, m in enumerate(project_t(p, xT, ready, 4 - 4 * (c % 2))):
                        b = 4 - 4 * (c % 2) + n
                        e = A([m, t_z, *e0, *xp_convolved[n]], xp[:, 2 * n:2 * n + 2, 2:258],
                              bank(b).rearrange("p (h n) -> p h n", h=2), ACT.Copy)
                        emptied[b] = [e]
                        tap = {}
                        for k in range(4):
                            for u in range(2):
                                ch = 4 * c + 2 * n + u
                                wk = cols[:, cw0 + 4 * ch + k:cw0 + 4 * ch + k + 1]
                                s = xp[:, 2 * n + u, k:k + 256]
                                if k == 0:
                                    tap[u] = V([e], TS, xc[:, ch, :], s, wk, cols[:, cb0 + ch:cb0 + ch + 1], ALU.mult, ALU.add)
                                else:
                                    tap[u] = V([tap[u]], STT, xc[:, ch, :], s, wk, xc[:, ch, :], ALU.mult, ALU.add)
                        xp_convolved[n] = [tap[1]]
                        ch = 4 * c + 2 * n
                        xc_tok[ch] = xc_tok[ch + 1] = A([tap[0], tap[1]], xc[:, ch:ch + 2, :], xc[:, ch:ch + 2, :], ACT.Silu)
                    qk_turn(c % 2, c // 2)
                    if c == 0:
                        t_dz = dt_turn()
                    if c == 1:
                        nab_load(1)
                        nab_mask(1)
                p = take(2)
                top_up(2)
                v_tok = []
                nab_load(2)
                for t in range(2):
                    gt = project(p, t, 4 + t, xT, ready)
                    v_tok.append(A([gt, *e0], vn[:, t, :], bank(4 + t), ACT.Copy))
                    emptied[4 + t] = [v_tok[-1]]
                e2 = [*e0, t_dz, *qk_tok.values(), *v_tok, *xp_convolved[0], *xp_convolved[1]]
                ph3.close()
                z_tok, z_in, zp = [[], []], [[], []], [0]

                def gate(n):
                    j, t, b = n // 2, n % 2, 6 + n % 2
                    if t == 0:
                        zp[0] = take(2)
                    gt = project(zp[0], t, b, xT, ready)
                    z = A([gt, *e0], zs[:, t, 512 * j:512 * j + 512], bank(b), ACT.Copy)
                    emptied[b] = [z]
                    z_in[t].append(z)
                    xT_multiplied[0] = [gt]

                steps = {}

                def step_sizes():
                    v = V([t_dz], STT, d[1], d[0], -1.0, d[0], ALU.mult, ALU.max)
                    a = A([v], d[2], d[1], ACT.Exp, scale=-1.0)
                    v = V([a], TS, d[3], d[2], 1.0, None, ALU.add)
                    a = A([v], d[4], d[3], ACT.Ln)
                    v = V([v], STT, d[5], d[3], -1.0, d[2], ALU.add, ALU.subtract)
                    v = V([v], nc.vector.reciprocal, d[6], d[3])
                    v = V([v], TT, d[5], d[5], d[6], ALU.mult)
                    v = V([v, a], TT, d[4], d[4], d[5], ALU.subtract)
                    v_dt = V([v], STT, d[0], d[0], 0.0, d[4], ALU.max, ALU.add)
                    a = A([t_small, v], d[7][:, 0:32], al, ACT.Exp)
                    v_a = V([a, v_dt], STT, d3[1], d3[0], -1.0, spread(d[7][:, 0:32], 1, 2), ALU.mult, ALU.mult)
                    steps["dt"], steps["a"] = v_dt, v_a

                def gate_silu():
                    for t in range(2):
                        z_tok[t].append(A(z_in[t], zs[:, t, :], zs[:, t, :], ACT.Silu))

                def nabias(i, t, P, S, after):
                    v = V([*after, nab_win[i, t]], TT, P, nab[:, i % 2, t, :, :], S, ALU.add)
                    nab_added[i] = [v]
                    xn_turned[i % 2] = [v]
                    if t == 1 and i < 2:
                        nab_mask(i + 2)
                        if i == 0:
                            nab_load(3)
                    return v

                o_tok = attention("n", ph2, 4, 64, [256, 256],
                                  lambda h, t: (qTn[64 * (h % 2):64 * (h % 2) + 64, h // 2, 128 * t:128 * t + 128], [qk_tok[0, t]]),
                                  lambda h, n: (kTn[64 * (h % 2):64 * (h % 2) + 64, h // 2, 0:n], [qk_tok[1, 0], qk_tok[1, 1]]),
                                  lambda h, kk: vn[:, kk, 64 * h:64 * h + 64], v_tok, nabias, (oTh, oTl), e2,
                                  {0: lambda: gate(0), 1: lambda: gate(1), 2: lambda: [gate(2), step_sizes()], 3: lambda: gate(3), 6: gate_silu})
                v_dt, v_a = steps["dt"], steps["a"]
            e1 = [o_tok[-1], ("act", counts["act"]), ("dve", counts["dve"]), ("pe", counts["pe"])]
            xd = sb("xd", [128, 2, 2, D], F32, ph)
            cb = sb("cbm", [128, 2, 4, 256], F32, ph)
            m2 = sb("m2", [128, 2, 4, 128], F32, ph)
            tri = sb("tri", [128, 5, 128], F32, ph)
            trir = sb("trir", [128, 4, 128], F32R, ph)
            sel = sb("sel", [128, 18], F32, ph)
            act_ = sb("act", [128, 3, 128], F32, ph)
            a0, a1 = CST["tf"][0], CST["sel"][0]
            load("sp", "cst", tri[:, :, :], cst_in[:, a0:a0 + 640].rearrange("p (a n) -> p a n", a=5), e1)
            t_tri = load("sp", "cst", sel[:, :], cst_in[:, a1:a1 + 18], e1)
            TF, TB, ON, MF, MB = (tri[:, i, :] for i in range(5))
            xs_tok = []
            for t in range(2):
                for b in range(2):
                    tr = transposed(lambda k: xc[:, 4 * b + k, 128 * t:128 * t + 128], 4, 6 + b, [xc_tok[4 * b + k] for k in range(4)])
                    e = A([tr, *xn_turned[t]], xn[:, t, 512 * b:512 * b + 512], bank(6 + b), ACT.Copy)
                    emptied[6 + b] = [e]
                xs_tok.append(e)
            after_emptied(4, 5)
            av, a2 = d3[1], act_[:, 1, :]
            t_a2 = V([v_a, *e1], nc.vector.tensor_copy, a2.rearrange("p (m u h) -> p m u h", u=2, h=16),
                     spread(d[1].rearrange("p (m h) -> p m h", h=16), 2, 2))
            wait("pe", t_tri, t_a2)
            for r in range(2):
                T = (TF, TB)[r]
                for s in range(2):
                    near = s != r
                    o, o2 = bank(4)[:, 32 * r + 16 * s:32 * r + 16 * s + 16], bank(5)[64 * r + 32 * s:64 * r + 32 * s + 32, 0:128]
                    MM(o, T, av[:, s, 16 * r:16 * r + 16], True, not near)
                    tok = done(MM(o2, a2[:, 64 * s + 32 * r:64 * s + 32 * r + 32], T, True, not near))
                    if near:
                        MM(o, ON, av[:, 1 - s, 16 * r:16 * r + 16], False, True)
                        n = 64 * (1 - s) + 32 * r
                        tok = done(MM(o2, a2[:, n:n + 32], ON, False, True))
            t_nac = V([tok, *e1], TS, nac[:, :], bank(4)[:, 0:64], -1.0, None, ALU.mult)
            h = A([tok, *e1], trir[:, 3, :], bank(5)[:, 0:128], ACT.Copy)
            v = V([h], TT, act_[:, 0, :], bank(5)[:, 0:128], trir[:, 3, :].bitcast(F32), ALU.subtract)
            emptied[4], emptied[5] = [t_nac], [v]
            v = V([v, t_tri], TS, act_[:, 1, :], act_[:, 0, :], sel[:, 17:18], None, ALU.mult)
            v = V([v], STT, act_[:, 2, :], trir[:, 3, :].bitcast(F32), sel[:, 16:17], act_[:, 1, :], ALU.mult, ALU.add)
            rows = xTh[:, :, :, :].rearrange("p k t n -> p (k t) n")
            t_rows = V([v, *xT_multiplied[0]], TT, rows, spread(act_[:, 2, :], 1, 16), spread(sel[:, 0:16], 2, 128), ALU.mult)
            h = A([t_rows], trir[:, 3, :], ON, ACT.Copy)
            h = A([h], trir[:, 0, :], ident[:, :], ACT.Copy)
            t_trir = A([h], trir[:, 1:3, :], tri[:, 3:5, :], ACT.Copy)
            for s in range(2):
                after_emptied(4, 5)
                wait("pe", *[xc_tok[c] for c in range(8, 16)])
                for g in range(4):
                    m = MM(bank(4 + g // 2)[:, 256 * (g % 2):256 * (g % 2) + 256], xc[:, 8 + g, 128 * s:128 * s + 128],
                           xc[:, 12 + g, :], True, True)
                tok = done(m)
                cb_tok = A([tok, *e1], cb[:, s, :, :], bank(4, 2).rearrange("p (g n) -> p g n", g=4), ACT.Copy)
                emptied[4] = emptied[5] = [cb_tok]
            xd_tok, xk_tok = {}, {}
            Dk = small[:, SMALL["dskip"][0]:SMALL["dskip"][0] + 16]
            for t in range(2):
                for r in range(2):
                    xd_tok[r, t] = V([xs_tok[t], v_dt, *e1], TT, xd[:, r, t, :].rearrange("p (h d) -> p h d", d=64),
                                     xn[:, t, :].rearrange("p (h d) -> p h d", d=64),
                                     spread(d3[0][:, t, 16 * r:16 * r + 16], 2, 64), ALU.mult)
                x3 = xn[:, t, :].rearrange("p (h d) -> p h d", d=64)
                xk_tok[t] = G([xd_tok[1, t]], nc.gpsimd.tensor_tensor, x3, x3, spread(Dk, 2, 64), ALU.mult)
            sn, snt, sni = gain("ssdnorm")
            Mx = [xc[:, 2 * i:2 * i + 2, :].rearrange("p c (u n) -> p (c u) n", u=2) for i in range(4)] + [m2[:, i, :, :] for i in range(2)]
            m_multiplied, m_tok = {}, {}

            def blocks(l):
                return [(0, 0), (1, 0), (1, 1)] if l == 0 else [(0, 0), (0, 1), (1, 1)]

            def decays(u):
                l, q = u // 4, u % 4
                for i, (r, s) in enumerate(blocks(l)):
                    bk, M, g = (3 * u + i) % 4, Mx[3 * (u % 2) + i], 64 * r + 32 * l
                    after_emptied(bk)
                    wait("pe", t_trir, t_rows)
                    if s == l:
                        MM(bank(bk), trir[:, 0, :], spread(trir[:, 1 + r, :], 1, 4), True, False)
                    tok = done(MM(bank(bk), trir[g:g + 32, 3, :], rows[g:g + 32, 4 * q:4 * q + 4, :], s != l, True))
                    for h in range(4):
                        c = 32 * r + 16 * s + 4 * q + h
                        e = A([tok, t_nac, *m_multiplied.get(u - 2, ()), *xs_tok], M[:, h, :], bank(bk)[:, 128 * h:128 * h + 128],
                              ACT.Exp, bias=nac[:, c:c + 1])
                    emptied[bk] = [e]
                    m_tok[u, i] = V([e, cb_tok], TT, M, M, spread(cb[:, s, q, 128 * l:128 * l + 128], 1, 4), ALU.mult)
                return tok

            def outputs(u):
                l, q = u // 4, u % 4
                b = 4 + 2 * l + q // 2
                if q % 2 == 0:
                    after_emptied(b)
                wait("pe", *[m_tok[u, i] for i in range(3)], *xd_tok.values())
                for h in range(4):
                    for i, (r, s) in enumerate(blocks(l)):
                        hd = 4 * q + h
                        m = MM(bank(b)[:, 64 * (hd % 8):64 * (hd % 8) + 64], Mx[3 * (u % 2) + i][:, h, :],
                               xd[:, r, s, 64 * hd:64 * hd + 64], i == 0, i == 2)
                tok = done(m)
                m_multiplied[u] = [tok]
                return tok

            def gated(l, y_tok):
                ya = xn[:, l, :]
                v = V([y_tok, xk_tok[l]], TT, ya, ya, bank(4 + 2 * l, 2), ALU.add)
                emptied[4 + 2 * l] = emptied[5 + 2 * l] = [v]
                v = V([v, *z_tok[l]], TT, ya, ya, zs[:, l, :], ALU.mult)
                ss = stat(4)
                for g in range(4):
                    a = A([v, *tmp_added[0]], tmp[:, 256 * g:256 * g + 256], ya[:, 256 * g:256 * g + 256], ACT.Square,
                          accum_out=ss[:, g:g + 1])
                tmp_added[0] = [a]
                g, rr = rstd(a, ss, 1.0 / 256, 1e-6, 4)
                for c in range(4):
                    u = slice(256 * c, 256 * c + 256)
                    v = V([g, snt], STT, ya[:, u], ya[:, u], rr[:, c:c + 1], sn[:, u], ALU.mult, ALU.mult)
                gain_applied[sni] = [v]
                return v

            gate_tok = {}
            for u in range(9):
                if u < 8:
                    rows_read = decays(u)
                else:
                    tr, ready[0] = flip(0, xn[:, 0, :], gate_tok[0], xT, [rows_read], 4)
                    xn_turned[0] = [tr]
                if u:
                    y_tok = outputs(u - 1)
                if u in (4, 8):
                    gate_tok[u // 4 - 1] = gated(u // 4 - 1, y_tok)
                top_up(1)
            p = take(2)
            for t in range(2):
                for q in range(2):
                    down(p + q, t, lambda k: (oTh[:, 2 * q + k, t, :], oTl[:, 2 * q + k, t, :]), q == 0, False, o_tok)
                    if t == 1:
                        top_up(1)
            tr, ready[1] = flip(1, xn[:, 1, :], gate_tok[1], xT, [rows_read])
            xn_turned[1] = [tr]
            seam(close_with(take(4), ready, p), None, False, "ffn0")
        if stop == "even":
            return write_out()
        ffn("e", bounds(), None, False, "oddmix")
        if stop == "ffn20":
            return write_out()

        ph = ExitStack()
        with ph:
            e0 = bounds()
            qg = sb("qg", [128, 2, D], F32, ph)
            qTg = sb("qTg", [128, 8, 256], F32, ph)
            kd = sb("kd", [128, 2, 4, 2, 64], F32, ph)
            kTg = sb("kTg", [128, 4, 256], F32, ph)
            vg = sb("vg", [128, 2, 256], F32, ph)
            kg = sb("kg", [128, 2, 256], F32, ph)
            r1 = sb("r1", [128, 512], F32, ph)
            r2 = sb("r2", [128, 512], F32, ph)
            cs = sb("cs", [128, 2, 2, 64], F32, ph)
            a0 = CST["cos"][0]
            t_cs = load("sp", "cst", cs[:, :, :, :], cst_in[:, a0:a0 + 256].rearrange("p (a t n) -> p a t n", a=2, t=2), e0)
            rf = [[]]

            gcs = sb("gcs", [128, 2, 2, 2, 64], F32, ph)
            for m, name in enumerate(("gq", "gk")):
                g0 = SMALL[name][0]
                g64 = small[:, g0:g0 + 64]
                turned64 = bass.AP(tensor=g64.tensor, offset=g64.offset + 1, ap=[list(g64.ap[0]), [0, 2], [2, 32], [-1, 2]])
                V([t_cs, t_small, *e0], TT, gcs[:, m, 0, :, :], cs[:, 0, :, :], spread(g64, 1, 2), ALU.mult)
                t_gcs = V([], TT, gcs[:, m, 1, :, :].rearrange("p t (m u) -> p t m u", u=2),
                          cs[:, 1, :, :].rearrange("p t (m u) -> p t m u", u=2), turned64, ALU.mult)

            def rope(m, src, n, t, dst, tok):
                a, b = r1[:, 0:64 * n].rearrange("p (h d) -> p h d", d=64), r2[:, 0:64 * n].rearrange("p (h d) -> p h d", d=64)
                sw = bass.AP(tensor=src.tensor, offset=src.offset + 1, ap=[list(src.ap[0]), [64, n], [2, 32], [-1, 2]])
                v2 = V([tok, t_gcs, *rf[0], *e0], TT, b.rearrange("p h (m u) -> p h m u", u=2), sw,
                       spread(gcs[:, m, 1, t, :].rearrange("p (m u) -> p m u", u=2), 1, n), ALU.mult)
                v1 = V([tok, t_gcs, *rf[0], *e0], TT, a, src, spread(gcs[:, m, 0, t, :], 1, n), ALU.mult)
                for dd in dst:
                    v = V([v1, v2], TT, dd, a, b, ALU.add)
                rf[0] = [v]
                return v

            qg_tok, qg_rope = {}, {}

            q_factors = {}

            def q_part(j, t):
                return qg[:, t, 512 * j:512 * j + 512].rearrange("p (h d) -> p h d", d=64)

            def q_stat(j, t, b, tok):
                q_factors[j, t] = head_stat(bank(b), 8, q_part(j, t), tok, e0, 1.0, 64e-6)

            def q_scale_rope(j, t, b):
                v1 = head_scale(bank(b), q_part(j, t), q_factors[j, t])
                emptied[b] = [v1]
                qg_rope[j, t] = rope(0, q_part(j, t), 8, t, [q_part(j, t)], v1)

            def q_norm(j, t, b, tok):
                q_stat(j, t, b, tok)
                top_up(1)
                q_scale_rope(j, t, b)

            def q_turn(j, t):
                b = 6 + t
                tr = transposed(lambda k: qg[:, t, 512 * j + 128 * k:512 * j + 128 * k + 128], 4, b, [qg_rope[j, t]])
                e = A([tr, *e0], qTg[:, 4 * j:4 * j + 4, 128 * t:128 * t + 128], bank(b).rearrange("p (k n) -> p k n", k=4), ACT.Copy)
                emptied[b] = [e]
                qg_tok[j, t] = e

            kg_tok, v_tok, kg_rope = [], [], {}

            def kv_norm(t, b, tok):
                dst = kg[:, t, :].rearrange("p (h d) -> p h d", d=64)
                v1, _ = head_norm(bank(b)[:, 0:256], 4, None, dst, tok, e0, 1.0 / 64, 1e-6)
                a = A([v1, *e0], vg[:, t, :], bank(b)[:, 256:512], ACT.Copy)
                v_tok.append(a)
                emptied[b] = [a]
                kg_rope[t] = rope(1, dst, 4, t, [kd[:, t, :, 0, :], kd[:, t, :, 1, :]], v1)

            def kv_turn(t):
                tr = transposed(lambda k: kd[:, t, k, :, :].rearrange("p a d -> p (a d)"), 4, 6 + t, [kg_rope[t]])
                e = A([tr, *e0], kTg[:, :, 128 * t:128 * t + 128], bank(6 + t).rearrange("p (k n) -> p k n", k=4), ACT.Copy)
                emptied[6 + t] = [e]
                kg_tok.append(e)

            pair(xT, ready, turn1, lambda j, t, b, tok: q_norm(0, t, b, tok) if j else kv_norm(t, b, tok), fresh=(0, 0, 0, 0))
            p1 = take(2)

            second = {}

            def q_second(t, b, mid=None):
                second[t] = project(p1, t, b, xT, ready, None, mid)
                xT_multiplied[0] = [second[t]]

            q_second(0, 4, lambda: [kv_turn(t) for t in range(2)])
            q_stat(1, 0, 4, second[0])
            for t in range(2):
                q_turn(0, t)
            o_tok = attention("g", ph, 8, 64, [256, 256],
                              lambda h, t: (qTg[64 * (h % 2):64 * (h % 2) + 64, h // 2, 128 * t:128 * t + 128], [qg_tok[h // 8, t]]),
                              lambda h, n: (kTg[64 * (h % 2):64 * (h % 2) + 64, h // 4, 0:n], kg_tok),
                              lambda h, kk: vg[:, kk, 64 * (h // 4):64 * (h // 4) + 64], v_tok, None, xT, e0,
                              {0: lambda: [q_scale_rope(1, 0, 4), q_second(1, 7)], 1: lambda: q_stat(1, 1, 7, second[1]),
                               2: lambda: q_scale_rope(1, 1, 7), 3: lambda: [q_turn(1, t) for t in range(2)]}, 0)
            seam(close_with(take(4), [o_tok, o_tok]), None, False, "ffn1")
        if stop == "odd":
            return write_out()
        ffn("f", bounds(), None, False, None)
        assert piece[0] == n_pieces, (piece[0], n_pieces)
        write_out()


def kernel(**inputs):
    import concourse.bacc as bacc
    from concourse.bass_utils import run_bass_kernel_spmd as run

    i = {k: np.asarray(v) for k, v in inputs.items()}
    arrays = {
        "in_x": np.ascontiguousarray(i["x"].reshape(256, D)),
        "in_w": np.ascontiguousarray(pack_stream(i)),
        "in_rows": np.ascontiguousarray(pack_rows(i)),
        "in_small": np.ascontiguousarray(pack_small(i)),
        "in_cols": np.ascontiguousarray(pack_cols(i)),
        "in_bias": np.ascontiguousarray(pack_bias(i)),
        "in_rpb": np.ascontiguousarray(i["na_rel_bias_2"][0][:, :, ::-1].reshape(-1)),
        "in_cst": constants(),
    }
    nc = bacc.Bacc("TRN2", target_bir_lowering=False, num_devices=1, dynamic_dma_scratch_size=1024)
    args = [nc.dram_tensor(k, a.shape, mybir.dt.from_np(a.dtype), kind="ExternalInput").ap() for k, a in arrays.items()]
    out = nc.dram_tensor("out_x", (256, D), F32, kind="ExternalOutput").ap()
    build(nc, *args, out)
    r = run(nc, [arrays], core_ids=[0])
    return r.results[0]["out_x"].reshape(1, 256, D)
```
